# Optimizing a Trainium2 kernel written in Bass

```python
import jax, jax.numpy as jnp
from jax import lax
import numpy as np

D_MODEL = 1024
BATCH = 1
SEQ = 512
DEPTH = 2

N_META = 16
EPS = 1e-6
ROPE_THETA = 10000.0
Q_BLOCK = 128
N_BRANCHES = 3

POOL_WINDOWS = (2, 4, 8, 16)
N_POOL_GROUPS = 4
C_A = D_MODEL
POOL_GROUP_DIM = C_A // N_POOL_GROUPS

RWKV_HEAD_DIM = 64
C_B = D_MODEL
RWKV_HEADS = C_B // RWKV_HEAD_DIM
RWKV_DECAY_RANK = 64
RWKV_A_RANK = 64
RWKV_GATE_RANK = 128
RWKV_VRES_RANK = 32
RWKV_GN_EPS = 64e-5

DSA_HEADS = 16
DSA_NOPE_DIM = 64
DSA_ROPE_DIM = 32
DSA_V_DIM = 64
C_C = DSA_HEADS * DSA_V_DIM
DSA_Q_RANK = 256
DSA_KV_RANK = 128
IDX_HEADS = 8
IDX_DIM = 64
IDX_ROPE_DIM = 32
MAX_TOPK = 256

N_GROUPS = 4
EXPERTS_PER_GROUP = 4
N_EXPERTS = N_GROUPS * EXPERTS_PER_GROUP
EXPERT_TOPK = 2
EXPERT_HIDDEN = 256

C_SHIFT = 3 * C_B + RWKV_DECAY_RANK + RWKV_A_RANK + RWKV_GATE_RANK
C_DSA_IN = DSA_Q_RANK + DSA_KV_RANK + DSA_ROPE_DIM + IDX_DIM + IDX_HEADS
C_IN = N_BRANCHES * D_MODEL + C_A + C_SHIFT + C_DSA_IN

kernel_name = 'hybrid_pool_rwkv7_dsa_hiermoe'

def rms_norm(x, g, eps=EPS):
    xf = x.astype(jnp.float32)
    y = xf * lax.rsqrt(jnp.mean(xf * xf, axis=-1, keepdims=True) + eps)
    return (y * g.astype(jnp.float32)).astype(x.dtype)

def layer_norm(x, w, b, eps=EPS):
    xf = x.astype(jnp.float32)
    mu = jnp.mean(xf, axis=-1, keepdims=True)
    var = jnp.mean(jnp.square(xf - mu), axis=-1, keepdims=True)
    y = (xf - mu) * lax.rsqrt(var + eps)
    return (y * w.astype(jnp.float32) + b.astype(jnp.float32)).astype(x.dtype)

def rope(x, pos):
    d = x.shape[-1]
    inv = ROPE_THETA ** (-jnp.arange(0, d, 2, dtype=jnp.float32) / d)
    ang = pos.astype(jnp.float32)[:, None] * inv[None, :]
    ang = ang.reshape(ang.shape[:1] + (1,) * (x.ndim - 3) + ang.shape[1:])
    cos, sin = jnp.cos(ang), jnp.sin(ang)
    xf = x.astype(jnp.float32)
    x1, x2 = xf[..., : d // 2], xf[..., d // 2:]
    return jnp.concatenate([x1 * cos - x2 * sin, x2 * cos + x1 * sin], axis=-1).astype(x.dtype)

def token_shift(p, mu):
    prev = jnp.pad(p[:, :-1], ((0, 0), (1, 0), (0, 0)))
    return p + (prev - p) * mu.astype(p.dtype)

def pool_mixer(u, w_grp, scale):
    B, T, _ = u.shape
    uf = u.astype(jnp.float32).reshape(B, T, N_POOL_GROUPS, POOL_GROUP_DIM)
    cs = jnp.cumsum(uf, axis=1)
    t = jnp.arange(T, dtype=jnp.float32)
    means = []
    for g, w in enumerate(POOL_WINDOWS):
        c = cs[:, :, g]
        lo = jnp.pad(c, ((0, 0), (w, 0), (0, 0)))[:, :T]
        cnt = jnp.minimum(t + 1.0, float(w))[None, :, None]
        means.append((c - lo) / cnt)
    pooled = jnp.stack(means, axis=2) - uf
    y = jnp.einsum('btgc,gcd->btgd', pooled.astype(u.dtype), w_grp).reshape(B, T, C_A)
    return y * scale

def rwkv7_scan(r, w, k, v, a, b):
    def step(S, inp):
        r_t, w_t, k_t, v_t, a_t, b_t = inp
        sa = jnp.einsum('bhij,bhj->bhi', S, a_t)
        S = S * w_t[:, :, None, :] + sa[..., :, None] * b_t[..., None, :] + v_t[..., :, None] * k_t[..., None, :]
        return S, jnp.einsum('bhij,bhj->bhi', S, r_t)
    B, T, H, N = r.shape
    S0 = jnp.zeros((B, H, N, N), jnp.float32)
    xs = tuple(jnp.moveaxis(z, 1, 0) for z in (r, w, k, v, a, b))
    _, out = lax.scan(step, S0, xs)
    return jnp.moveaxis(out, 0, 1)

def rwkv7_mixer(pb, vres, v_first, w0, w2, a0, a2, g2, k_k, k_a, r_k, ln_w, ln_b):
    B, T, _ = pb.shape
    H, N = RWKV_HEADS, RWKV_HEAD_DIM
    f32 = jnp.float32
    cuts = [C_B, 2 * C_B, 3 * C_B, 3 * C_B + RWKV_DECAY_RANK, 3 * C_B + RWKV_DECAY_RANK + RWKV_A_RANK]
    r, k, v, wd, ad, gd = jnp.split(pb, cuts, axis=-1)
    w_log = -jax.nn.softplus(-(w0 + jnp.tanh(wd) @ w2).astype(f32)) - 0.5
    decay = jnp.exp(-jnp.exp(w_log))
    a = jax.nn.sigmoid((a0 + ad @ a2).astype(f32))
    g = jax.nn.sigmoid(gd) @ g2
    if vres is None:
        v_first = v
    else:
        vd, v0, v2 = vres
        v = v + (v_first - v) * jax.nn.sigmoid(v0 + vd @ v2)
    heads = lambda z: z.astype(f32).reshape(B, T, H, N)
    rh, vh, ah, dh = heads(r), heads(v), heads(a), heads(decay)
    kk = heads(k * k_k)
    kk = kk / jnp.maximum(jnp.linalg.norm(kk, axis=-1, keepdims=True), 1e-12)
    kh = heads(k) * (1.0 + (ah - 1.0) * k_a.astype(f32).reshape(H, N))
    o = rwkv7_scan(rh, dh, kh, vh, -kk, kk * ah)
    mu = jnp.mean(o, axis=-1, keepdims=True)
    var = jnp.mean(jnp.square(o - mu), axis=-1, keepdims=True)
    o = ((o - mu) * lax.rsqrt(var + RWKV_GN_EPS)).reshape(B, T, C_B)
    o = o * ln_w.astype(f32) + ln_b.astype(f32)
    bonus = jnp.sum(rh * kh * r_k.astype(f32), axis=-1, keepdims=True) * vh
    o = (o + bonus.reshape(B, T, C_B)) * g.astype(f32)
    return o.astype(pb.dtype), v_first

def dsa_mixer(pc, pos, topk, q_norm_g, kv_norm_g, w_uq, w_uk, w_uv, w_q_idx, k_idx_w, k_idx_b):
    B, T, _ = pc.shape
    f32 = jnp.float32
    cuts = [DSA_Q_RANK, DSA_Q_RANK + DSA_KV_RANK, DSA_Q_RANK + DSA_KV_RANK + DSA_ROPE_DIM,
            DSA_Q_RANK + DSA_KV_RANK + DSA_ROPE_DIM + IDX_DIM]
    cq, ckv, krope, kidx, widx = jnp.split(pc, cuts, axis=-1)
    cq = rms_norm(cq, q_norm_g)
    ckv = rms_norm(ckv, kv_norm_g)
    q = (cq @ w_uq).reshape(B, T, DSA_HEADS, DSA_NOPE_DIM + DSA_ROPE_DIM)
    q_nope, q_rope = q[..., :DSA_NOPE_DIM], rope(q[..., DSA_NOPE_DIM:], pos)
    k_rope = rope(krope, pos)
    q_lat = jnp.einsum('bthd,hcd->bthc', q_nope, w_uk)
    q_idx = (cq @ w_q_idx).reshape(B, T, IDX_HEADS, IDX_DIM)
    q_idx = jnp.concatenate([rope(q_idx[..., :IDX_ROPE_DIM], pos), q_idx[..., IDX_ROPE_DIM:]], axis=-1)
    k_idx = layer_norm(kidx, k_idx_w, k_idx_b)
    k_idx = jnp.concatenate([rope(k_idx[..., :IDX_ROPE_DIM], pos), k_idx[..., IDX_ROPE_DIM:]], axis=-1)
    w_head = widx * (IDX_HEADS ** -0.5 * IDX_DIM ** -0.5)
    scale = (DSA_NOPE_DIM + DSA_ROPE_DIM) ** -0.5
    n_blk = -(-T // Q_BLOCK)
    t_pad = n_blk * Q_BLOCK

    def blocks(z):
        z = jnp.pad(z, ((0, 0), (0, t_pad - T)) + ((0, 0),) * (z.ndim - 2))
        return jnp.moveaxis(z.reshape((B, n_blk, Q_BLOCK) + z.shape[2:]), 1, 0)

    qpos = jnp.arange(t_pad, dtype=jnp.int32).reshape(n_blk, Q_BLOCK)
    key_pos = jnp.arange(T, dtype=jnp.int32)
    gather = jax.vmap(lambda tbl, ix: tbl[ix])

    def attend(args):
        ql, qr, qi, wh, tq = args
        score_idx = jnp.einsum('bqhs,bqh->bqs', jax.nn.relu(jnp.einsum('bqhd,bsd->bqhs', qi, k_idx)), wh)
        admissible = key_pos[None, None, :] <= tq[None, :, None]
        score_idx = jnp.where(admissible, score_idx.astype(f32), -jnp.inf)
        _, sel = lax.top_k(score_idx, topk)
        ckv_sel = gather(ckv, sel)
        kr_sel = gather(k_rope, sel)
        s = jnp.einsum('bqhc,bqkc->bqhk', ql, ckv_sel) + jnp.einsum('bqhr,bqkr->bqhk', qr, kr_sel)
        s = s.astype(f32) * scale
        valid = (sel <= tq[None, :, None])[:, :, None, :]
        p = jax.nn.softmax(jnp.where(valid, s, -jnp.inf), axis=-1).astype(ckv_sel.dtype)
        return jnp.einsum('bqhk,bqkc->bqhc', p, ckv_sel)

    o_lat = lax.map(attend, (blocks(q_lat), blocks(q_rope), blocks(q_idx), blocks(w_head), qpos))
    o_lat = jnp.moveaxis(o_lat, 0, 1).reshape(B, t_pad, DSA_HEADS, DSA_KV_RANK)[:, :T]
    return jnp.einsum('bthc,hcv->bthv', o_lat, w_uv).reshape(B, T, C_C)

def hier_moe(h, w_grp, b_grp, w_exp, b_exp, w1, w3, w2):
    B, T, D = h.shape
    n = B * T
    f32 = jnp.float32
    hf = h.reshape(n, D)
    grp_logits = (hf @ w_grp).astype(f32) + b_grp.astype(f32)
    g_sel = jnp.argmax(grp_logits, axis=-1)
    p_grp = jnp.take_along_axis(jax.nn.softmax(grp_logits, axis=-1), g_sel[:, None], axis=1)
    exp_logits = ((hf @ w_exp).astype(f32) + b_exp.astype(f32)).reshape(n, N_GROUPS, EXPERTS_PER_GROUP)
    in_grp = jnp.take_along_axis(exp_logits, g_sel[:, None, None], axis=1)[:, 0]
    top_val, top_idx = lax.top_k(in_grp, EXPERT_TOPK)
    p_exp = jax.nn.softmax(top_val, axis=-1) * p_grp
    eid = g_sel[:, None] * EXPERTS_PER_GROUP + top_idx
    combine = jnp.sum(jax.nn.one_hot(eid, N_EXPERTS, dtype=f32) * p_exp[..., None], axis=1)
    y = jnp.zeros((n, D), f32)
    for gi in range(N_GROUPS):
        sl = slice(gi * EXPERTS_PER_GROUP, (gi + 1) * EXPERTS_PER_GROUP)
        hid = jax.nn.silu(jnp.einsum('nd,edf->nef', hf, w1[sl])) * jnp.einsum('nd,edf->nef', hf, w3[sl])
        hid = hid * combine[:, sl, None].astype(hid.dtype)
        y = y + jnp.einsum('nef,efd->nd', hid, w2[sl]).astype(f32)
    return y.reshape(B, T, D).astype(h.dtype)

def setup_inputs(seed: int = 0) -> dict:
    key = jax.random.key(seed)
    ks = iter(jax.random.split(key, 64))
    nrm = lambda shape, s: s * jax.random.normal(next(ks), shape, jnp.float32)
    gain = lambda shape: 1.0 + nrm(shape, 0.02)
    unif = lambda shape: jax.random.uniform(next(ks), shape, jnp.float32)
    L, V = DEPTH, DEPTH - 1
    decay_base = jnp.linspace(-6.5, -1.5, C_B, dtype=jnp.float32)
    return {
        'x': nrm((BATCH, SEQ, D_MODEL), 1.0),
        'meta_tokens': nrm((N_META, D_MODEL), 1.0),
        'norm_mix': gain((L, D_MODEL)),
        'w_in': nrm((L, D_MODEL, C_IN), D_MODEL ** -0.5),
        'mu_shift': unif((L, C_SHIFT)),
        'pool_w': nrm((L, N_POOL_GROUPS, POOL_GROUP_DIM, POOL_GROUP_DIM), POOL_GROUP_DIM ** -0.5),
        'pool_scale': gain((L, C_A)),
        'rwkv_w0': decay_base + nrm((L, C_B), 0.1),
        'rwkv_w2': nrm((L, RWKV_DECAY_RANK, C_B), 0.5 * RWKV_DECAY_RANK ** -0.5),
        'rwkv_a0': nrm((L, C_B), 0.1),
        'rwkv_a2': nrm((L, RWKV_A_RANK, C_B), 0.5 * RWKV_A_RANK ** -0.5),
        'rwkv_g2': nrm((L, RWKV_GATE_RANK, C_B), RWKV_GATE_RANK ** -0.5),
        'rwkv_k_k': 0.85 + nrm((L, C_B), 0.02),
        'rwkv_k_a': gain((L, C_B)),
        'rwkv_r_k': nrm((L, RWKV_HEADS, RWKV_HEAD_DIM), 0.1),
        'rwkv_ln_w': gain((L, C_B)),
        'rwkv_ln_b': nrm((L, C_B), 0.01),
        'vres_w_down': nrm((V, D_MODEL, RWKV_VRES_RANK), D_MODEL ** -0.5),
        'vres_mu': unif((V, RWKV_VRES_RANK)),
        'vres_v0': 1.0 + nrm((V, C_B), 0.1),
        'vres_v2': nrm((V, RWKV_VRES_RANK, C_B), 0.5 * RWKV_VRES_RANK ** -0.5),
        'mla_q_norm': gain((L, DSA_Q_RANK)),
        'mla_kv_norm': gain((L, DSA_KV_RANK)),
        'mla_w_uq': nrm((L, DSA_Q_RANK, DSA_HEADS * (DSA_NOPE_DIM + DSA_ROPE_DIM)), DSA_Q_RANK ** -0.5),
        'mla_w_uk': nrm((L, DSA_HEADS, DSA_KV_RANK, DSA_NOPE_DIM), DSA_NOPE_DIM ** -0.5),
        'mla_w_uv': nrm((L, DSA_HEADS, DSA_KV_RANK, DSA_V_DIM), DSA_KV_RANK ** -0.5),
        'idx_w_q': nrm((L, DSA_Q_RANK, IDX_HEADS * IDX_DIM), DSA_Q_RANK ** -0.5),
        'idx_k_norm_w': gain((L, IDX_DIM)),
        'idx_k_norm_b': nrm((L, IDX_DIM), 0.01),
        'w_proj_a': nrm((L, C_A, D_MODEL), C_A ** -0.5),
        'w_proj_b': nrm((L, C_B, D_MODEL), C_B ** -0.5),
        'w_proj_c': nrm((L, C_C, D_MODEL), C_C ** -0.5),
        'w_out': nrm((L, D_MODEL, D_MODEL), D_MODEL ** -0.5),
        'norm_ffn': gain((L, D_MODEL)),
        'router_w_group': nrm((L, D_MODEL, N_GROUPS), D_MODEL ** -0.5),
        'router_b_group': nrm((L, N_GROUPS), 0.01),
        'router_w_expert': nrm((L, D_MODEL, N_EXPERTS), D_MODEL ** -0.5),
        'router_b_expert': nrm((L, N_EXPERTS), 0.01),
        'expert_w1': nrm((L, N_EXPERTS, D_MODEL, EXPERT_HIDDEN), D_MODEL ** -0.5),
        'expert_w3': nrm((L, N_EXPERTS, D_MODEL, EXPERT_HIDDEN), D_MODEL ** -0.5),
        'expert_w2': nrm((L, N_EXPERTS, EXPERT_HIDDEN, D_MODEL), EXPERT_HIDDEN ** -0.5),
        'norm_final': gain((D_MODEL,)),
    }

def reference(x, meta_tokens, norm_mix, w_in, mu_shift, pool_w, pool_scale,
              rwkv_w0, rwkv_w2, rwkv_a0, rwkv_a2, rwkv_g2, rwkv_k_k, rwkv_k_a, rwkv_r_k,
              rwkv_ln_w, rwkv_ln_b, vres_w_down, vres_mu, vres_v0, vres_v2,
              mla_q_norm, mla_kv_norm, mla_w_uq, mla_w_uk, mla_w_uv,
              idx_w_q, idx_k_norm_w, idx_k_norm_b,
              w_proj_a, w_proj_b, w_proj_c, w_out, norm_ffn,
              router_w_group, router_b_group, router_w_expert, router_b_expert,
              expert_w1, expert_w3, expert_w2, norm_final):
    B, S, D = x.shape
    T = S + N_META
    topk = min(MAX_TOPK, S // 4)
    pos = jnp.arange(T, dtype=jnp.int32)
    h = jnp.concatenate([jnp.broadcast_to(meta_tokens[None].astype(x.dtype), (B, N_META, D)), x], axis=1)
    o0 = N_BRANCHES * D_MODEL
    o1 = o0 + C_A
    o2 = o1 + C_SHIFT
    o3 = o2 + C_DSA_IN
    v_first = None
    for l in range(DEPTH):
        u = rms_norm(h, norm_mix[l])
        w_cat = w_in[l] if l == 0 else jnp.concatenate([w_in[l], vres_w_down[l - 1]], axis=1)
        p = u @ w_cat
        gates = jax.nn.sigmoid(p[..., :o0].astype(jnp.float32)).reshape(B, T, N_BRANCHES, D_MODEL)
        pb = token_shift(p[..., o1:o2], mu_shift[l])
        vres = None if l == 0 else (token_shift(p[..., o3:], vres_mu[l - 1]), vres_v0[l - 1], vres_v2[l - 1])
        y_a = pool_mixer(p[..., o0:o1], pool_w[l], pool_scale[l])
        y_b, v_first = rwkv7_mixer(pb, vres, v_first, rwkv_w0[l], rwkv_w2[l], rwkv_a0[l], rwkv_a2[l],
                                   rwkv_g2[l], rwkv_k_k[l], rwkv_k_a[l], rwkv_r_k[l], rwkv_ln_w[l], rwkv_ln_b[l])
        y_c = dsa_mixer(p[..., o2:o3], pos, topk, mla_q_norm[l], mla_kv_norm[l], mla_w_uq[l], mla_w_uk[l],
                        mla_w_uv[l], idx_w_q[l], idx_k_norm_w[l], idx_k_norm_b[l])
        merged = (gates[:, :, 0] * (y_a @ w_proj_a[l]) + gates[:, :, 1] * (y_b @ w_proj_b[l])
                  + gates[:, :, 2] * (y_c @ w_proj_c[l]))
        h = h + merged.astype(h.dtype) @ w_out[l]
        h = h + hier_moe(rms_norm(h, norm_ffn[l]), router_w_group[l], router_b_group[l], router_w_expert[l],
                         router_b_expert[l], expert_w1[l], expert_w3[l], expert_w2[l])
    return rms_norm(h, norm_final)[:, N_META:]


_drawn_inputs = setup_inputs


def setup_inputs(seed=0):
    import zlib

    import numpy as np

    out = dict(_drawn_inputs(seed))
    spreads = {}
    factors = {'rwkv_k_k': 3.275,
     'rwkv_ln_b': 3.542,
     'vres_v0': 106.151,
     'mla_kv_norm': 2.753,
     'router_b_expert': 3.216,
     'norm_final': 24.183,
     'vres_w_down': 8.0,
     'vres_mu': 8.0,
     'vres_v2': 8.0}
    for name, (base, spread) in spreads.items():
        noise = np.random.default_rng([zlib.crc32(name.encode()), seed]).standard_normal(out[name].shape)
        drawn = base * np.exp(spread * noise) if base else spread * noise
        out[name] = __import__('jax').numpy.asarray(drawn.astype(out[name].dtype))
    for name, factor in factors.items():
        out[name] = (out[name] * factor).astype(out[name].dtype)
    return out
```

```python
import numpy as np
import concourse.bass as bass
from concourse import mybir
from contextlib import ExitStack

D, SEQ, N_META, DEPTH = 1024, 512, 16, 2
T = SEQ + N_META
P = 128
KD = D // P
HALF = T // 2
CH = 88
NCH = T // CH
NPAIR = 8
RING = 4
EPS = 1e-6
GN_EPS = 64e-5
TOPK = min(256, SEQ // 4)
LEVELS = [2, 4, 8, 16, 32, 64]
NEG_CAUSAL, TAKEN, NEG_BIAS = -3.0e38, -3.2e38, -1.0e30
IDX_SCALE = 8 ** -0.5 * 64 ** -0.5
ATT_SCALE = (64 + 32) ** -0.5
POOL_WINDOWS = (2, 4, 8, 16)

ROUNDS = {"lowrank": 1, "pairs": 8, "merge_b": 4, "pool": 3, "merge_a": 4, "dsa_in": 2, "heads": 2,
          "merge_c": 4, "out": 2, "moe": 24}
FIRST, _n = {}, 0
for _k, _v in ROUNDS.items():
    FIRST[_k] = _n
    _n += _v
LAYER_ROUNDS = _n

CONSTS, _n = {}, 0
for _k, _v in (("ident", 128), ("ones", 128), ("headones", 128), ("perm", 128), ("cos", T), ("sin", T),
               ("reset", T), ("grams", 5 * CH), ("level", (1 + len(LEVELS)) * CH), ("causal", CH),
               ("bias", CH), ("keys", 4), ("counts", 16)):
    CONSTS[_k] = (_n, _v)
    _n += _v
N_CONST = _n
PARAMS, _n = {}, 0
for _k, _v in (("norm_mix", 8), ("norm_ffn", 8), ("norm_final", 8), ("pool_scale", 8), ("w0", 8), ("a0", 8),
               ("k_k", 8), ("k_a", 8), ("r_k", 8), ("ln_w", 8), ("ln_b", 8), ("v0", 8), ("mu_r", 8),
               ("mu_k", 8), ("mu_v", 8), ("mu_wa", 1), ("mu_g", 1), ("mu_vres", 1), ("q_norm", 2),
               ("kv_norm", 1), ("idx_w", 1), ("idx_b", 1), ("later", 1), ("first", 1), ("router", 160),
               ("router_b", 20)):
    PARAMS[_k] = (_n, _v)
    _n += _v
N_PARAM = _n


class Steps:

    def __init__(self, sem, names):
        self.sem, self.names, self.next = sem, list(names), 0
        self.place = {n: i for i, n in enumerate(self.names)}

    def inc(self, name):
        assert self.names[self.next] == name, (self.names[self.next], name)
        self.next = (self.next + 1) % len(self.names)
        return self.sem

    def at(self, turn, name):
        return (turn + 1) * len(self.names) + self.place[name] + 1

    def before(self, turn, name):
        return turn * len(self.names) + self.place[name] + 1


def trunk_program(nc, x_t, consts, params, stream, out_t):
    f32 = mybir.dt.float32
    ALU = mybir.AluOpType
    ACT = mybir.ActivationFunctionType
    AX = mybir.AxisListType
    ds = bass.ds
    ctx = ExitStack()
    with ctx:
        def sb(name, shape):
            return ctx.enter_context(nc.sbuf_tensor(name, shape, f32))

        def sem(name):
            return ctx.enter_context(nc.semaphore(name))

        h = sb("h", [P, KD, T])
        u = sb("u", [P, KD, T])
        y = sb("y", [P, KD, T])
        m = sb("m", [P, KD, T])
        vf = sb("v_first", [P, KD, T])
        ring = sb("ring", [P, RING, KD * P])
        cst = sb("cst", [P, N_CONST])
        par = sb("par", [P, N_PARAM])
        scratch = sb("scratch", [P, 22400])
        ps = ctx.enter_context(nc.psum_tensor("ps", [P, 8, 512], f32))

        def c(name, rows=P):
            o, n = CONSTS[name]
            return cst[0:rows, o:o + n]

        ident, ones, headones, perm, cos, sin = map(c, ("ident", "ones", "headones", "perm", "cos", "sin"))

        def pc(name, j=0, rows=P):
            o, n = PARAMS[name]
            return par[0:rows, ds(o + j, 1)] if not isinstance(j, int) else par[0:rows, o + j:o + j + 1]

        def area(base=scratch[:, :]):
            at = [0]

            def take(*shape, rows=P):
                n = int(np.prod(shape))
                v = base[0:rows, at[0]:at[0] + n]
                at[0] += n
                assert at[0] <= base.shape[1], (at[0], base.shape)
                if len(shape) == 2:
                    v = v.rearrange("p (a b) -> p a b", a=shape[0])
                if len(shape) == 3:
                    v = v.rearrange("p (a b c) -> p a b c", a=shape[0], b=shape[1])
                return v
            return take

        def acc(bank, rows=slice(0, P)):
            return ps[rows, bank:bank + 2, 0:HALF]

        def two(ap):
            return ap.rearrange("p (a b) -> p a b", a=2)

        w_full = [sem(f"w_full{s}") for s in range(RING)]
        w_free = [sem(f"w_free{s}") for s in range(RING)]
        loaded, stored, par_full = sem("loaded"), sem("stored"), sem("par_full")
        zeroed = sem("zeroed")
        ends = {k: sem(f"{k}_phase_end") for k in ("pe", "dve", "act", "pool")}

        N_PHASES = 14
        passed = {k: sem(f"{k}_passed") for k in ("PE", "DVE", "Activation", "Pool")}

        def alone(eng):
            eng.sem_inc(passed[eng.engine.name], 1)

        phase_of = {"pe": 0, "dve": 0, "act": 0, "pool": 0}

        def next_phase(eng, me, layer):
            phase_of[me] += 1
            k = phase_of[me]
            alone(eng)
            eng.drain().then_inc(ends[me], 1)
            for other in ("pe", "dve", "act", "pool"):
                if other != me:
                    eng.wait_ge(ends[other], layer * N_PHASES + k)
            alone(eng)

        norm_pe = Steps(sem("norm_pe"), ["sum"])
        norm_act = Steps(sem("norm_act"), ["sq0", "sq1", "sq2", "sq3", "sq4", "sq5", "sq6", "sq7", "sqrt"])
        norm_dve = Steps(sem("norm_dve"), ["mean"])
        low_pe = Steps(sem("low_pe"), ["wa", "g", "vres"])
        low_act = Steps(sem("low_act"), ["wa", "g", "vres", "tanh"])
        low_dve = Steps(sem("low_dve"), ["shift"])
        pair_pe = Steps(sem("pair_pe"), ["r", "k", "v", "z", "a", "g", "vres", "kk", "bonus", "tb", "tk", "tv"]
                        + [f"gram{i}" for i in range(NCH)]
                        + [f"{s}{lv}_{x}" for lv in LEVELS for s in ("t", "nm") for x in range(3)]
                        + [f"{s}{i}" for i in range(NCH) for s in ("x", "u", "o", "d")] + ["mean", "var"])
        pair_act = Steps(sem("pair_act"), ["r", "k", "v", "z", "a", "g", "vres", "sq", "G", "Gi", "Gx", "norm",
                                           "tb", "tk", "tv"]
                         + [f"t{lv}_{x}" for lv in LEVELS for x in range(3)]
                         + [f"{s}{i}" for i in range(NCH) for s in ("u", "o")] + ["sq2", "std"])
        pair_dve = Steps(sem("pair_dve"), ["rate", "c", "v", "kk", "rkk", "kkmax", "bonus", "ab", "rbk"]
                         + [f"gram{i}" for i in range(NCH)] + [f"one{x}" for x in range(3)]
                         + [f"nm{lv}_{x}" for lv in LEVELS for x in range(3)]
                         + [f"{s}{i}" for i in range(NCH) for s in ("x", "s")] + ["cen", "var", "y"])
        pair_pool = Steps(sem("pair_pool"), [f"lv{lv}_{x}" for lv in LEVELS for x in range(3)])
        merge_pe = Steps(sem("merge_pe"), ["p0", "g0", "p1", "g1"])
        merge_act = Steps(sem("merge_act"), ["g0", "g1"])
        merge_dve = Steps(sem("merge_dve"), ["m0", "m1"])
        pool_pe = Steps(sem("pool_pe"), [f"p{j}" for j in range(8)] + [f"y{j}" for j in range(8)])
        pool_act = Steps(sem("pool_act"), [f"p{j}" for j in range(8)] + [f"y{j}" for j in range(8)])
        pool_dve = Steps(sem("pool_dve"), [f"p{j}" for j in range(8)])
        lat_pe = Steps(sem("lat_pe"), ["cq0", "cq1", "ckv", "kidx", "kr", "qsum", "kvsum", "mean", "var", "kperm",
                                       "rperm", "q0", "q1", "q2", "q3", "qp0", "qp1", "qp2", "qp3", "w"])
        lat_act = Steps(sem("lat_act"), ["cq0", "cq1", "ckv", "kidx", "kr", "sq", "std", "var", "std2",
                                         "q0", "q1", "q2", "q3", "w"])
        lat_dve = Steps(sem("lat_dve"), ["means", "latents", "center", "var", "kidx", "ropes", "rope0", "rope1",
                                         "rope2", "rope3"])
        IDX = [(i, hd) for i in range(1, NCH) for hd in range(8)]
        idx_pe = Steps(sem("idx_pe"), [f"s{i}_{hd}" for i, hd in IDX])
        idx_act = Steps(sem("idx_act"), [f"s{i}_{hd}" for i, hd in IDX])
        idx_dve = Steps(sem("idx_dve"), [f"s{i}_{hd}" for i, hd in IDX])
        att_pe = Steps(sem("att_pe"), [f"{s}{hd}" for hd in range(8) for s in
                                       ["q", "k", "v", "perm"]
                                       + [x for i in range(NCH + 2) for x in
                                          ([f"s{i}_"] if i < NCH else []) + ([f"pt{i - 1}_"] if 1 <= i <= NCH else [])
                                          + ([f"pv{i - 2}_"] if i >= 2 else [])]])
        att_act = Steps(sem("att_act"), [f"{s}{hd}" for hd in range(8) for s in
                                         ["q", "k", "v"]
                                         + [x for i in range(NCH + 2) for x in
                                            ([f"e{i}_"] if i < NCH else []) + ([f"pt{i - 1}_"] if 1 <= i <= NCH else [])
                                            + ([f"pv{i - 2}_"] if i >= 2 else [])]])
        att_dve = Steps(sem("att_dve"), ["kr"] + [f"{s}{hd}" for hd in range(8) for s in
                                         ["rope"] + [x for i in range(NCH + 1) for x in
                                                     ([f"m{i}_"] if i < NCH else []) + ([f"n{i - 1}_"] if i >= 1 else [])]])
        res_pe = Steps(sem("res_pe"), [f"o{s}" for s in range(4)])
        res_dve = Steps(sem("res_dve"), [f"h{s}" for s in range(4)])
        rt_pe = Steps(sem("rt_pe"), ["logits", "ct"])
        rt_act = Steps(sem("rt_act"), ["gexp", "eexp", "ct"])
        rt_dve = Steps(sem("rt_dve"), ["gmax", "ediff", "combine"])
        grp_pe = Steps(sem("grp_pe"), [f"c{e}" for e in range(4)])
        grp_act = Steps(sem("grp_act"), [f"c{e}" for e in range(4)])
        grp_dve = Steps(sem("grp_dve"), [f"c{e}" for e in range(4)])
        exp_pe = Steps(sem("exp_pe"), ["a0", "b0", "a1", "b1"])
        exp_act = Steps(sem("exp_act"), ["t0", "t1"])
        exp_dve = Steps(sem("exp_dve"), ["h0", "h1"])
        dn_pe = Steps(sem("down_pe"), [f"o{s}" for s in range(4)])
        dn_dve = Steps(sem("down_dve"), [f"h{s}" for s in range(4)])
        out_ready = sem("out_ready")

        PE_STEPS = [norm_pe, low_pe, pair_pe, merge_pe, pool_pe, lat_pe, idx_pe, att_pe, res_pe, rt_pe, grp_pe,
                    exp_pe, dn_pe]
        ACT_STEPS = [norm_act, low_act, pair_act, merge_act, pool_act, lat_act, idx_act, att_act, rt_act, grp_act,
                     exp_act]
        DVE_STEPS = [norm_dve, low_dve, pair_dve, merge_dve, pool_dve, lat_dve, idx_dve, att_dve, res_dve, rt_dve,
                     grp_dve, exp_dve, dn_dve]

        t = area()
        n_sq, n_rs = t(KD, T), t(T)
        t = area()
        lr_wa, lr_g, lr_v = t(T), t(T), t(T)
        raw_r, raw_k, raw_v = t(T + 1), t(T + 1), t(T + 1)
        pr, pk, pv = t(T), t(T), t(T)
        tz, ta, tv, pg = t(T), t(T), t(T), t(T)
        sqk, cum, kk, kh, bonus = t(T), t(T), t(T), t(T), t(T)
        G, Gi, Gx = t(T), t(T), t(T)
        ar = t(2, T)
        bb, kb_ = t(T), t(T)
        tm = t(3, NCH * P, rows=CH)
        state, xs, us = t(P), t(P), t(P)
        gr = t(2 * NCH, 4 * CH, rows=CH)
        half_w0, half_a0, half_v0 = t(8), t(8), t(8)
        area_m = area(m[:, :, :].rearrange("p a b -> p (a b)"))
        inv_t = area_m(2 * NCH, CH, rows=CH)
        inv = area_m(2 * NCH, CH, rows=CH)
        low = area_m(2 * NCH, CH, rows=CH)
        lv_a = area_m(2 * NCH, CH, rows=CH)
        lv_t = t(2 * NCH, CH, rows=CH)
        lv_as = [lv_a[:, 4 * x:4 * x + 4, :] for x in range(3)]
        lv_ts = [lv_t[:, 4 * x:4 * x + 4, :] for x in range(3)]
        pairs_o = raw_r[:, 1:T + 1]
        t = area()
        g_tanh, g_tmp = t(2, T), t(2, T)
        t = area()
        p_raw, p_a, p_b, pooled = t(2, T), t(T), t(T), t(KD, T)
        t = area()
        cq, ckv, kidx, kr = t(2, T), t(T), t(T), t(T)
        qi = t(4, T)
        wtok = t(NCH, 8, rows=CH)
        sel = t(NCH * (NCH + 1) // 2, CH, rows=CH)
        lat_mark = t
        l_sq, l_tmp, l_tmp2, l_rs, l_rs2 = t(3, T), t(T), t(T), t(T), t(T)
        score, score_w, relu_b, top8 = t(T, rows=CH), t(T, rows=CH), t(2, T, rows=CH), t(8, rows=CH)
        qh, kh2, vh = t(2, T, rows=96), t(2, T, rows=96), t(2, NCH * 64, rows=CH)
        es, pts = t(2, T, rows=CH), t(2, T, rows=CH)
        rope_t = t(T)
        mx, rs, ri = t(2, rows=CH), t(2, rows=CH), t(2, rows=CH)
        t = area()
        comb = t(NCH, 16, rows=CH)
        comb_t, comb_sel = t(T, rows=16), t(T, rows=16)
        comb_b, hid, e_tanh, e_tmp = t(4, T), t(8, T), t(2, T), t(2, T)
        lg = t(NCH, 20, rows=CH)
        r1, r2, r3, oh, oh1, oh2, ce = (t(NCH, 4, rows=CH) for _ in range(7))
        r16 = t(NCH, 16, rows=CH)
        s1, s2, s3, s4, s5 = (t(NCH, rows=CH) for _ in range(5))

        def sel_of(i):
            o = i * (i + 1) // 2
            return sel[:, o:o + i + 1, :]

        def n_parts(i):
            return 2 if i >= 3 else 1

        def scores(b, i):
            n = n_parts(i)
            return ps[0:CH, b:b + n, 0:(i + 1) * CH // n]

        def parts(ap, i):
            return ap.rearrange("p (a b) -> p a b", a=n_parts(i))

        block = ctx.enter_context(nc.Block())

        @block.sync
        def _(sp):
            for j in range(KD):
                sp.dma_start(h[:, j, :], x_t[j]).then_inc(loaded, 16)
            for s in range(RING):
                sp.dma_start(ring[:, s, :], stream[s]).then_inc(w_full[s], 16)
            with sp.Fori(1, DEPTH * LAYER_ROUNDS) as n:
                for s in range(RING):
                    sp.wait_ge(w_free[s], n)
                    sp.dma_start(ring[:, s, :], stream[n * RING + s]).then_inc(w_full[s], 16)
            sp.wait_ge(out_ready, 1)
            for j in range(KD):
                sp.dma_start(out_t[j], u[:, j, N_META:]).then_inc(stored, 16)
            sp.wait_ge(stored, 16 * KD)

        @block.tensor
        def _(pe):
            mm = nc.tensor.matmul
            for S in PE_STEPS:
                pe.sem_inc(S.sem, len(S.names))

            def tile(s, rnd):
                pe.wait_ge(w_full[s], (rnd + 1) * 16)
                return ring[:, s, :]

            def project(s, rnd, src, bank, done, kbs=KD, free=True):
                w = tile(s, rnd)
                for kb in range(kbs):
                    for hf in range(2):
                        last = mm(ps[:, bank + hf, 0:HALF], w[:, kb * P:(kb + 1) * P],
                                  src[:, kb, hf * HALF:(hf + 1) * HALF], start=kb == 0, stop=kb == kbs - 1)
                    if kb == 0 and used:
                        last.then_inc(w_free[used.pop()], 1)
                last.then_inc(done, 1)
                used.append(s)

            def let_go():
                pe.drain().then_inc(w_free[used.pop()], 1)

            def release(s, rnd=None):
                if used:
                    let_go()
                if rnd is not None:
                    pe.wait_ge(w_full[s], (rnd + 1) * 16)
                    alone(pe)
                pe.drain().then_inc(w_free[s], 1)

            used = []

            def halves(lhsT, rhs, bank, rows=slice(0, P), start=True, stop=True):
                for hf in range(2):
                    last = mm(ps[rows, bank + hf, 0:HALF], lhsT, rhs[:, hf * HALF:(hf + 1) * HALF],
                              start=start, stop=stop)
                return last

            def norm(turn, n=KD):
                for j in range(n):
                    pe.wait_ge(norm_act.sem, norm_act.at(turn, f"sq{j}"))
                    last = halves(ones, n_sq[:, j, :], 0, start=j == 0, stop=j == n - 1)
                last.then_inc(norm_pe.inc("sum"), 1)

            pe.wait_ge(loaded, 16 * (KD + 1))
            with pe.Fori(0, DEPTH) as l:
                rnd0 = l * LAYER_ROUNDS
                norm(l * 2)
                next_phase(pe, "pe", l)

                rnd = rnd0 + FIRST["lowrank"]
                project(0, rnd, u, 0, low_pe.inc("wa"))
                project(1, rnd, u, 2, low_pe.inc("g"))
                project(2, rnd, u, 4, low_pe.inc("vres"))
                release(3, rnd)
                next_phase(pe, "pe", l)

                with pe.Fori(0, NPAIR) as q:
                    it, rnd = l * NPAIR + q, rnd0 + FIRST["pairs"] + q
                    S, A, V = pair_pe, pair_act, pair_dve

                    def act_did(name):
                        pe.wait_ge(A.sem, A.at(it, name))

                    def dve_did(name):
                        pe.wait_ge(V.sem, V.at(it, name))

                    pe.wait_ge(V.sem, V.before(it, "y"))
                    project(0, rnd, u, 0, S.inc("r"))
                    project(1, rnd, u, 2, S.inc("k"))
                    project(2, rnd, u, 4, S.inc("v"))
                    w = tile(3, rnd)
                    halves(w[0:64, 0:P], lr_wa[0:64, :], 6).then_inc(S.inc("z"), 1)
                    act_did("r")
                    halves(w[64:128, P:2 * P], lr_wa[64:128, :], 0).then_inc(S.inc("a"), 1)
                    act_did("k")
                    halves(w[:, 2 * P:3 * P], lr_g, 2).then_inc(S.inc("g"), 1)
                    act_did("v")
                    halves(w[0:32, 3 * P:4 * P], lr_v[0:32, :], 4).then_inc(S.inc("vres"), 1)
                    release(3)
                    act_did("z")
                    act_did("sq")
                    halves(headones, sqk, 6).then_inc(S.inc("kk"), 1)
                    dve_did("rkk")
                    act_did("a")
                    halves(headones, tz, 0).then_inc(S.inc("bonus"), 1)
                    dve_did("rbk")
                    for name, src, bank, free in (("tb", bb, 2, "g"), ("tk", kb_, 4, "vres"), ("tv", pv, 6, None)):
                        if free:
                            act_did(free)
                        else:
                            dve_did("kkmax")
                        for i in range(NCH):
                            o = bank * 512 + i * P
                            last = nc.tensor.transpose(ps[0:CH, bank + i // 4, (i % 4) * P:(i % 4 + 1) * P],
                                                       src[:, i * CH:(i + 1) * CH], ident)
                        last.then_inc(S.inc(name), 1)
                    dve_did("bonus")
                    for i in range(NCH):
                        if 1 <= i <= 3:
                            act_did(("tb", "tk", "tv")[i - 1])
                        if i >= 4:
                            dve_did(f"gram{i - 4}")
                        b = 2 * (i % 4)
                        cc = slice(i * CH, (i + 1) * CH)
                        for hd in range(2):
                            rw = slice(64 * hd, 64 * hd + 64)
                            mm(ps[0:CH, b + hd, 0:2 * CH], bb[rw, cc], ar[rw, :, cc], start=True, stop=True)
                            mm(ps[0:CH, b + hd, 2 * CH:4 * CH], kb_[rw, cc], ar[rw, :, cc], start=True, stop=True)
                            last = mm(ps[0:CH, b + hd, 4 * CH:5 * CH], ar[rw, 0, cc], bb[rw, cc], start=True, stop=True)
                        last.then_inc(S.inc(f"gram{i}"), 1)
                    for n, lv in enumerate(LEVELS):
                        for x in range(3):
                            pe.wait_ge(pair_pool.sem, pair_pool.at(it, f"lv{lv}_{x}"))
                            if n == 0:
                                dve_did(f"one{x}")
                                dve_did(f"gram{NCH - 1}")
                            else:
                                dve_did(f"nm{LEVELS[n - 1]}_{2 if x == 0 else x}")
                            for k in range(4):
                                last = mm(ps[0:CH, x, k * CH:(k + 1) * CH], lv_as[x][:, k, :],
                                          inv[:, 4 * x + k, :], start=True, stop=True)
                            last.then_inc(S.inc(f"t{lv}_{x}"), 1)
                        for x in range(3):
                            act_did(f"t{lv}_{x}")
                            if x == 2:
                                dve_did(f"nm{lv}_0")
                            for k in range(4):
                                mm(ps[0:CH, 3 + x % 2, k * CH:(k + 1) * CH], lv_ts[x][:, k, :],
                                   inv_t[:, 4 * x + k, :], start=True, stop=True)
                            for k in range(4):
                                last = mm(ps[0:CH, 5 + x % 2, k * CH:(k + 1) * CH], inv_t[:, 4 * x + k, :],
                                          lv_ts[x][:, k, :], start=True, stop=True)
                            last.then_inc(S.inc(f"nm{lv}_{x}"), 1)
                    for i in range(NCH):
                        cc = slice(i * CH, (i + 1) * CH)
                        tmv = tm[:, 2, i * P:(i + 1) * P]
                        dve_did(f"nm{LEVELS[-1]}_2" if i == 0 else f"s{i - 1}")
                        mm(ps[0:CH, 0, 0:P], ar[:, 0, cc], state, start=True, stop=False, skip_group_check=True)
                        for hd in range(2):
                            last = mm(ps[0:CH, 0, 64 * hd:64 * hd + 64], gr[:, 2 * i + hd, 2 * CH:3 * CH],
                                      tmv[:, 64 * hd:64 * hd + 64], start=False, stop=hd == 1, skip_group_check=True)
                        last.then_inc(S.inc(f"x{i}"), 1)
                        dve_did(f"x{i}")
                        for hd in range(2):
                            last = mm(ps[0:CH, 1, 64 * hd:64 * hd + 64], inv_t[:, 2 * i + hd, :],
                                      xs[0:CH, 64 * hd:64 * hd + 64], start=True, stop=True)
                        last.then_inc(S.inc(f"u{i}"), 1)
                        act_did(f"u{i}")
                        if i >= 1:
                            act_did(f"o{i - 1}")
                        mm(ps[:, 2, 0:CH], state, ar[:, 1, cc], start=True, stop=False, skip_group_check=True)
                        for hd in range(2):
                            rw = slice(64 * hd, 64 * hd + 64)
                            mm(ps[rw, 2, 0:CH], us[0:CH, rw], gr[:, 2 * i + hd, CH:2 * CH],
                               start=False, stop=False, skip_group_check=True)
                            last = mm(ps[rw, 2, 0:CH], tmv[:, rw], gr[:, 2 * i + hd, 3 * CH:4 * CH],
                                      start=False, stop=True, skip_group_check=True)
                        last.then_inc(S.inc(f"o{i}"), 1)
                        mm(ps[:, 3, 0:P], tm[:, 0, i * P:(i + 1) * P], us[0:CH, :], start=True, stop=False)
                        mm(ps[:, 3, 0:P], tm[:, 1, i * P:(i + 1) * P], tmv, start=False, stop=True
                           ).then_inc(S.inc(f"d{i}"), 1)
                    act_did(f"o{NCH - 1}")
                    halves(headones, pairs_o, 4).then_inc(S.inc("mean"), 1)
                    act_did("sq2")
                    halves(headones, sqk, 6).then_inc(S.inc("var"), 1)
                next_phase(pe, "pe", l)

                def merge(phase, k):
                    with pe.Fori(0, 4) as q:
                        it, rnd = l * 12 + 4 * k + q, rnd0 + FIRST[phase] + q
                        for n in range(2):
                            pe.wait_ge(merge_dve.sem, merge_dve.before(it, f"m{n}"))
                            project(2 * n, rnd, y, 4 * n, merge_pe.inc(f"p{n}"))
                            project(2 * n + 1, rnd, u, 4 * n + 2, merge_pe.inc(f"g{n}"))
                        let_go()
                    next_phase(pe, "pe", l)

                merge("merge_b", 0)

                for j in range(8):
                    if j >= 4:
                        pe.wait_ge(pool_act.sem, pool_act.at(l, f"p{j - 4}"))
                    project(j % 4, rnd0 + FIRST["pool"] + j // 4, u, 2 * (j % 4), pool_pe.inc(f"p{j}"))
                let_go()
                rnd = rnd0 + FIRST["pool"] + 2
                for j in range(8):
                    g, nb = j // 2, j % 2
                    w = tile(g // 2, rnd)
                    pe.wait_ge(pool_act.sem, pool_act.at(l, f"p{j + 4}" if j < 4 else f"y{j - 4}"))
                    for kb in range(2):
                        pe.wait_ge(pool_dve.sem, pool_dve.at(l, f"p{2 * g + kb}"))
                        blk = (g % 2) * 4 + nb * 2 + kb
                        last = halves(w[:, blk * P:(blk + 1) * P], pooled[:, 2 * g + kb, :], 2 * (j % 4),
                                      start=kb == 0, stop=kb == 1)
                    last.then_inc(pool_pe.inc(f"y{j}"), 1)
                    if j in (3, 7):
                        release(j // 4)
                release(2, rnd)
                release(3, rnd)
                next_phase(pe, "pe", l)
                merge("merge_a", 1)

                S, A, V = lat_pe, lat_act, lat_dve

                def act_did(name):
                    pe.wait_ge(A.sem, A.at(l, name))

                def dve_did(name):
                    pe.wait_ge(V.sem, V.at(l, name))

                rnd = rnd0 + FIRST["dsa_in"]
                for s, name in enumerate(("cq0", "cq1", "ckv", "kidx")):
                    project(s, rnd, u, 2 * s, S.inc(name))
                act_did("cq0")
                project(0, rnd + 1, u, 0, S.inc("kr"))
                let_go()
                act_did("sq")
                act_did("cq1")
                halves(ones, l_sq[:, 0, :], 2, start=True, stop=False)
                halves(ones, l_sq[:, 1, :], 2, start=False, stop=True).then_inc(S.inc("qsum"), 1)
                act_did("ckv")
                halves(ones, l_sq[:, 2, :], 4).then_inc(S.inc("kvsum"), 1)
                act_did("kidx")
                halves(headones, kidx, 6).then_inc(S.inc("mean"), 1)
                act_did("var")
                halves(headones, l_sq[:, 0, :], 6).then_inc(S.inc("var"), 1)
                dve_did("kidx")
                halves(perm, kidx, 2).then_inc(S.inc("kperm"), 1)
                act_did("kr")
                halves(perm, kr, 4).then_inc(S.inc("rperm"), 1)
                w = tile(1, rnd + 1)
                for j in range(4):
                    dve_did("ropes")
                    b = 2 * j
                    for kb in range(2):
                        blk = 2 * j + kb
                        last = halves(w[:, blk * P:(blk + 1) * P], cq[:, kb, :], b, start=kb == 0, stop=kb == 1)
                    last.then_inc(S.inc(f"q{j}"), 1)
                release(1)
                release(2, rnd + 1)
                release(3, rnd + 1)
                for j in range(4):
                    act_did(f"q{j}")
                    halves(perm, qi[:, j, :], 2 * j).then_inc(S.inc(f"qp{j}"), 1)
                dve_did("rope0")
                alone(pe)
                for i in range(NCH):
                    last = nc.tensor.transpose(ps[0:CH, 0, i * 8:(i + 1) * 8], kr[96:104, i * CH:(i + 1) * CH],
                                               ident[96:104, 96:104])
                last.then_inc(S.inc("w"), 1)
                next_phase(pe, "pe", l)

                for n, (i, hd) in enumerate(IDX):
                    if n >= 4:
                        j, g = IDX[n - 4]
                        pe.wait_ge(idx_act.sem, idx_act.at(l, f"s{j}_{g}"))
                    rw = slice(64 * (hd % 2), 64 * (hd % 2) + 64)
                    b = 2 * (n % 4)
                    wd = (i + 1) * CH // n_parts(i)
                    for k in range(n_parts(i)):
                        last = mm(ps[0:CH, b + k, 0:wd], qi[rw, hd // 2, i * CH:(i + 1) * CH],
                                  kidx[rw, k * wd:(k + 1) * wd], start=True, stop=True)
                    last.then_inc(idx_pe.inc(f"s{i}_{hd}"), 1)
                next_phase(pe, "pe", l)

                with pe.Fori(0, 2) as q:
                    it, rnd = l * 2 + q, rnd0 + FIRST["heads"] + q
                    S, A, V = att_pe, att_act, att_dve

                    def act_did(name):
                        pe.wait_ge(A.sem, A.at(it, name))

                    def dve_did(name):
                        pe.wait_ge(V.sem, V.at(it, name))

                    for hd in range(8):
                        b4, hh, z = hd // 4, hd % 4, hd % 2
                        wq, wkv = tile(2 * b4, rnd), tile(2 * b4 + 1, rnd)
                        if hd == 0:
                            pe.wait_ge(A.sem, A.before(it, "pv5_7"))
                            pe.wait_ge(V.sem, V.before(it, "m5_7"))
                        else:
                            act_did(f"pv5_{hd - 1}")
                            dve_did(f"m5_{hd - 1}")
                        for kb in range(2):
                            blk = 2 * hh + kb
                            last = halves(wq[:, blk * P:blk * P + 96], cq[:, kb, :], 0, rows=slice(0, 96),
                                          start=kb == 0, stop=kb == 1)
                        last.then_inc(S.inc(f"q{hd}"), 1)
                        halves(wkv[:, hh * 64:hh * 64 + 64], ckv, 2, rows=slice(0, 64)).then_inc(S.inc(f"k{hd}"), 1)
                        for i in range(NCH):
                            last = mm(ps[0:CH, 4, i * 64:i * 64 + 64], ckv[:, i * CH:(i + 1) * CH],
                                      wkv[:, 256 + hh * 64:256 + hh * 64 + 64], start=True, stop=True)
                        last.then_inc(S.inc(f"v{hd}"), 1)
                        if hh == 3:
                            release(2 * b4)
                            release(2 * b4 + 1)
                        act_did(f"q{hd}")
                        alone(pe)
                        halves(perm[64:96, 64:96], qh[64:96, z, :], 6, rows=slice(64, 96)
                               ).then_inc(S.inc(f"perm{hd}"), 1)
                        dve_did(f"rope{hd}")
                        act_did(f"v{hd}")
                        for step in range(NCH + 2):
                            if step < NCH:
                                i = step
                                if i >= 2:
                                    dve_did(f"m{i - 2}_{hd}")
                                wd = (i + 1) * CH // n_parts(i)
                                for k in range(n_parts(i)):
                                    last = mm(ps[0:CH, 2 * (i % 2) + k, 0:wd], qh[:, z, i * CH:(i + 1) * CH],
                                              kh2[:, z, k * wd:(k + 1) * wd], start=True, stop=True)
                                last.then_inc(S.inc(f"s{i}_{hd}"), 1)
                            if 1 <= step <= NCH:
                                i = step - 1
                                dve_did(f"n{i}_{hd}")
                                if i >= 2:
                                    act_did(f"pv{i - 2}_{hd}")
                                b = 4 + 2 * (i % 2)
                                for k in range(i + 1):
                                    last = nc.tensor.transpose(ps[0:CH, b + k // 3, (k % 3) * CH:(k % 3 + 1) * CH],
                                                               es[:, i % 2, k * CH:(k + 1) * CH], ident[0:CH, 0:CH])
                                last.then_inc(S.inc(f"pt{i}_{hd}"), 1)
                            if step >= 2:
                                i = step - 2
                                act_did(f"pt{i}_{hd}")
                                rw = slice(64 * z, 64 * z + 64)
                                b = 4 + 2 * (i % 2)
                                for k in range(i + 1):
                                    last = mm(ps[rw, b, 3 * CH:4 * CH], vh[:, z, k * 64:k * 64 + 64],
                                              pts[:, i % 2, k * CH:(k + 1) * CH], start=k == 0, stop=k == i)
                                last.then_inc(S.inc(f"pv{i}_{hd}"), 1)
                next_phase(pe, "pe", l)
                merge("merge_c", 2)

                with pe.Fori(0, 2) as q:
                    it, rnd = l * 2 + q, rnd0 + FIRST["out"] + q
                    for s in range(4):
                        pe.wait_ge(res_dve.sem, res_dve.before(it, f"h{s}"))
                        project(s, rnd, m, 2 * s, res_pe.inc(f"o{s}"))
                    let_go()
                next_phase(pe, "pe", l)
                norm(l * 2 + 1)
                next_phase(pe, "pe", l)

                o = PARAMS["router"][0]
                for i in range(NCH):
                    for kb in range(KD):
                        last = mm(ps[0:CH, 0, i * 20:i * 20 + 20], u[:, kb, i * CH:(i + 1) * CH],
                                  par[:, o + kb * 20:o + kb * 20 + 20], start=kb == 0, stop=kb == KD - 1)
                last.then_inc(rt_pe.inc("logits"), 1)
                pe.wait_ge(rt_dve.sem, rt_dve.at(l, "combine"))
                for i in range(NCH):
                    last = nc.tensor.transpose(ps[0:16, 2 + i // 3, (i % 3) * CH:(i % 3 + 1) * CH], comb[:, i, :],
                                               ident[0:CH, 0:CH])
                last.then_inc(rt_pe.inc("ct"), 1)
                next_phase(pe, "pe", l)

                with pe.Fori(0, 4) as g:
                    gi = l * 4 + g
                    for e in range(4):
                        pe.wait_ge(grp_dve.sem, grp_dve.at(gi, f"c{e}"))
                        if e == 0:
                            pe.wait_ge(dn_dve.sem, dn_dve.before(gi * 2, "h3"))
                        halves(ones[0:16, :], comb_sel, 2 * e).then_inc(grp_pe.inc(f"c{e}"), 1)
                        pe.wait_ge(grp_act.sem, grp_act.at(gi, f"c{e}"))
                    alone(pe)
                    with pe.Fori(0, 4) as e:
                        it, rnd = gi * 4 + e, rnd0 + FIRST["moe"] + g * 6 + e
                        for n in range(2):
                            pe.wait_ge(exp_dve.sem, exp_dve.before(it, f"h{n}"))
                            project(2 * n, rnd, u, 4 * n, exp_pe.inc(f"a{n}"))
                            project(2 * n + 1, rnd, u, 4 * n + 2, exp_pe.inc(f"b{n}"))
                        let_go()
                    pe.wait_ge(exp_dve.sem, exp_dve.at(gi * 4 + 3, "h1"))
                    alone(pe)
                    with pe.Fori(0, 2) as q:
                        it, rnd = gi * 2 + q, rnd0 + FIRST["moe"] + g * 6 + 4 + q
                        for s in range(4):
                            pe.wait_ge(dn_dve.sem, dn_dve.before(it, f"h{s}"))
                            project(s, rnd, hid, 2 * s, dn_pe.inc(f"o{s}"))
                        let_go()
                next_phase(pe, "pe", l)
            norm(DEPTH * 2)

        @block.scalar
        def _(act):
            A_ = nc.scalar.activation
            act.dma_start(cst[:, :], consts).then_inc(loaded, 16)
            for S in ACT_STEPS:
                act.sem_inc(S.sem, len(S.names))
            act.wait_ge(loaded, 16 * (KD + 1))

            def norm(turn):
                for j in range(KD):
                    A_(n_sq[:, j, :], h[:, j, :], ACT.Square).then_inc(norm_act.inc(f"sq{j}"), 1)
                act.wait_ge(norm_dve.sem, norm_dve.at(turn, "mean"))
                A_(n_rs, n_rs, ACT.Sqrt).then_inc(norm_act.inc("sqrt"), 1)

            with act.Fori(0, DEPTH) as l:
                act.dma_start(par[:, :], params[l]).then_inc(par_full, 16)
                norm(l * 2)
                next_phase(act, "act", l)

                for name, dst, b in (("wa", raw_r, 0), ("g", raw_k, 2), ("vres", raw_v, 4)):
                    act.wait_ge(low_pe.sem, low_pe.at(l, name))
                    A_(two(dst[:, 1:]), acc(b), ACT.Copy).then_inc(low_act.inc(name), 1)
                act.wait_ge(low_dve.sem, low_dve.at(l, "shift"))
                A_(lr_wa[0:64, :], lr_wa[0:64, :], ACT.Tanh)
                A_(lr_g, lr_g, ACT.Tanh, scale=0.5).then_inc(low_act.inc("tanh"), 1)
                next_phase(act, "act", l)

                with act.Fori(0, NPAIR) as q:
                    it = l * NPAIR + q
                    S, E, V = pair_act, pair_pe, pair_dve

                    def pe_did(name):
                        act.wait_ge(E.sem, E.at(it, name))

                    def dve_did(name):
                        act.wait_ge(V.sem, V.at(it, name))

                    act.wait_ge(V.sem, V.before(it, "y"))
                    for name, dst, b in (("r", raw_r, 0), ("k", raw_k, 2), ("v", raw_v, 4)):
                        pe_did(name)
                        A_(two(dst[:, 1:]), acc(b), ACT.Copy).then_inc(S.inc(name), 1)
                    pe_did("z")
                    A_(two(tz), acc(6), ACT.Tanh, bias=half_w0[:, ds(q, 1)], scale=0.5).then_inc(S.inc("z"), 1)
                    pe_did("a")
                    A_(two(ta), acc(0), ACT.Tanh, bias=half_a0[:, ds(q, 1)], scale=0.5).then_inc(S.inc("a"), 1)
                    pe_did("g")
                    A_(two(pg), acc(2), ACT.Copy).then_inc(S.inc("g"), 1)
                    pe_did("vres")
                    A_(two(tv), acc(4), ACT.Tanh, bias=half_v0[:, ds(q, 1)], scale=0.5).then_inc(S.inc("vres"), 1)
                    dve_did("kk")
                    A_(sqk, kk, ACT.Square).then_inc(S.inc("sq"), 1)
                    dve_did("c")
                    A_(G, cum, ACT.Exp).then_inc(S.inc("G"), 1)
                    A_(Gi, cum, ACT.Exp, scale=-1.0).then_inc(S.inc("Gi"), 1)
                    A_(Gx, Gx, ACT.Exp).then_inc(S.inc("Gx"), 1)
                    dve_did("kkmax")
                    A_(sqk, sqk, ACT.Sqrt).then_inc(S.inc("norm"), 1)
                    for k, (name, b) in enumerate((("tb", 2), ("tk", 4), ("tv", 6))):
                        pe_did(name)
                        A_(tm[:, k, 0:4 * P], ps[0:CH, b, 0:4 * P], ACT.Copy)
                        A_(tm[:, k, 4 * P:6 * P], ps[0:CH, b + 1, 0:2 * P], ACT.Copy).then_inc(S.inc(name), 1)
                    for lv in LEVELS:
                        for x in range(3):
                            pe_did(f"t{lv}_{x}")
                            A_(lv_ts[x], ps[0:CH, x, 0:4 * CH].rearrange("p (a b) -> p a b", a=4), ACT.Copy
                               ).then_inc(S.inc(f"t{lv}_{x}"), 1)
                    for i in range(NCH):
                        pe_did(f"u{i}")
                        if i >= 1:
                            pe_did(f"d{i - 1}")
                        A_(us[0:CH, :], ps[0:CH, 1, 0:P], ACT.Copy).then_inc(S.inc(f"u{i}"), 1)
                        pe_did(f"o{i}")
                        A_(pairs_o[:, i * CH:(i + 1) * CH], ps[:, 2, 0:CH], ACT.Copy).then_inc(S.inc(f"o{i}"), 1)
                    dve_did("cen")
                    A_(sqk, kk, ACT.Square).then_inc(S.inc("sq2"), 1)
                    dve_did("var")
                    A_(G, G, ACT.Sqrt).then_inc(S.inc("std"), 1)
                next_phase(act, "act", l)

                def merge(k):
                    with act.Fori(0, 4) as q:
                        it = l * 12 + 4 * k + q
                        for n in range(2):
                            act.wait_ge(merge_dve.sem, merge_dve.before(it, f"m{n}"))
                            act.wait_ge(merge_pe.sem, merge_pe.at(it, f"g{n}"))
                            A_(two(g_tanh[:, n, :]), acc(4 * n + 2), ACT.Tanh, scale=0.5
                               ).then_inc(merge_act.inc(f"g{n}"), 1)
                    next_phase(act, "act", l)

                merge(0)
                for j in range(8):
                    act.wait_ge(pool_pe.sem, pool_pe.at(l, f"p{j}"))
                    if j >= 2:
                        act.wait_ge(pool_dve.sem, pool_dve.at(l, f"p{j - 2}"))
                    A_(two(p_raw[:, j % 2, :]), acc(2 * (j % 4)), ACT.Copy).then_inc(pool_act.inc(f"p{j}"), 1)
                for j in range(8):
                    act.wait_ge(pool_pe.sem, pool_pe.at(l, f"y{j}"))
                    A_(two(y[:, j, :]), acc(2 * (j % 4)), ACT.Copy, scale=pc("pool_scale", j)
                       ).then_inc(pool_act.inc(f"y{j}"), 1)
                next_phase(act, "act", l)
                merge(1)

                def pe_did(name):
                    act.wait_ge(lat_pe.sem, lat_pe.at(l, name))

                def dve_did(name):
                    act.wait_ge(lat_dve.sem, lat_dve.at(l, name))
                S = lat_act
                for name, dst, b in (("cq0", cq[:, 0, :], 0), ("cq1", cq[:, 1, :], 2), ("ckv", ckv, 4),
                                     ("kidx", kidx, 6), ("kr", kr, 0)):
                    pe_did(name)
                    A_(two(dst), acc(b), ACT.Copy).then_inc(S.inc(name), 1)
                act.drain()
                A_(l_sq[:, 0:2, :], cq, ACT.Square)
                A_(l_sq[:, 2, :], ckv, ACT.Square).then_inc(S.inc("sq"), 1)
                dve_did("means")
                A_(l_rs, l_rs, ACT.Sqrt)
                A_(l_rs2, l_rs2, ACT.Sqrt).then_inc(S.inc("std"), 1)
                dve_did("center")
                pe_did("qsum")
                A_(l_sq[:, 0, :], kidx, ACT.Square).then_inc(S.inc("var"), 1)
                dve_did("var")
                A_(l_tmp, l_tmp, ACT.Sqrt).then_inc(S.inc("std2"), 1)
                for j in range(4):
                    pe_did(f"q{j}")
                    A_(two(qi[:, j, :]), acc(2 * j), ACT.Copy).then_inc(S.inc(f"q{j}"), 1)
                pe_did("w")
                A_(wtok, ps[0:CH, 0, 0:8 * NCH].rearrange("p (a b) -> p a b", a=NCH), ACT.Copy, scale=IDX_SCALE
                   ).then_inc(S.inc("w"), 1)
                next_phase(act, "act", l)

                for n, (i, hd) in enumerate(IDX):
                    act.wait_ge(idx_pe.sem, idx_pe.at(l, f"s{i}_{hd}"))
                    if n >= 2:
                        j, g = IDX[n - 2]
                        act.wait_ge(idx_dve.sem, idx_dve.at(l, f"s{j}_{g}"))
                    b, z, wd = 2 * (n % 4), n % 2, (i + 1) * CH
                    A_(parts(relu_b[:, z, 0:wd], i), scores(b, i), ACT.Relu).then_inc(idx_act.inc(f"s{i}_{hd}"), 1)
                next_phase(act, "act", l)

                with act.Fori(0, 2) as q:
                    it = l * 2 + q
                    S = att_act

                    def pe_did(name):
                        act.wait_ge(att_pe.sem, att_pe.at(it, name))

                    def dve_did(name):
                        act.wait_ge(att_dve.sem, att_dve.at(it, name))

                    for hd in range(8):
                        z = hd % 2
                        pe_did(f"q{hd}")
                        A_(two(qh[:, z, :]), acc(0, slice(0, 96)), ACT.Copy).then_inc(S.inc(f"q{hd}"), 1)
                        pe_did(f"k{hd}")
                        A_(two(kh2[0:64, z, :]), acc(2, slice(0, 64)), ACT.Copy).then_inc(S.inc(f"k{hd}"), 1)
                        pe_did(f"v{hd}")
                        A_(vh[:, z, :], ps[0:CH, 4, 0:NCH * 64], ACT.Copy).then_inc(S.inc(f"v{hd}"), 1)
                        for step in range(NCH + 2):
                            if step < NCH:
                                i = step
                                wd = (i + 1) * CH
                                dve_did(f"m{i}_{hd}")
                                A_(es[:, i % 2, 0:wd], es[:, i % 2, 0:wd], ACT.Exp, bias=mx[:, i % 2:i % 2 + 1],
                                   scale=ATT_SCALE, accum_out=rs[:, i % 2:i % 2 + 1]).then_inc(S.inc(f"e{i}_{hd}"), 1)
                            if 1 <= step <= NCH:
                                i = step - 1
                                wd, b = (i + 1) * CH, 4 + 2 * (i % 2)
                                pe_did(f"pt{i}_{hd}")
                                if i < 3:
                                    last = A_(pts[:, i % 2, 0:wd], ps[0:CH, b, 0:wd], ACT.Copy)
                                else:
                                    A_(pts[:, i % 2, 0:HALF], ps[0:CH, b, 0:HALF], ACT.Copy)
                                    last = A_(pts[:, i % 2, HALF:wd], ps[0:CH, b + 1, 0:wd - HALF], ACT.Copy)
                                last.then_inc(S.inc(f"pt{i}_{hd}"), 1)
                            if step >= 2:
                                i = step - 2
                                b = 4 + 2 * (i % 2)
                                rw = slice(64 * z, 64 * z + 64)
                                pe_did(f"pv{i}_{hd}")
                                A_(y[rw, ds(q * 4 + hd // 2, 1), i * CH:(i + 1) * CH],
                                   ps[rw, b:b + 1, 3 * CH:4 * CH], ACT.Copy).then_inc(S.inc(f"pv{i}_{hd}"), 1)
                next_phase(act, "act", l)
                merge(2)
                next_phase(act, "act", l)
                norm(l * 2 + 1)
                next_phase(act, "act", l)

                S = rt_act
                act.wait_ge(rt_dve.sem, rt_dve.at(l, "gmax"))
                A_(r1, r1, ACT.Exp).then_inc(S.inc("gexp"), 1)
                act.wait_ge(rt_dve.sem, rt_dve.at(l, "ediff"))
                A_(s4, s4, ACT.Exp).then_inc(S.inc("eexp"), 1)
                act.wait_ge(rt_pe.sem, rt_pe.at(l, "ct"))
                A_(two(comb_t), acc(2, slice(0, 16)), ACT.Copy).then_inc(S.inc("ct"), 1)
                next_phase(act, "act", l)

                with act.Fori(0, 4) as g:
                    gi = l * 4 + g
                    for e in range(4):
                        act.wait_ge(grp_pe.sem, grp_pe.at(gi, f"c{e}"))
                        A_(two(comb_b[:, e, :]), acc(2 * e), ACT.Copy).then_inc(grp_act.inc(f"c{e}"), 1)
                    with act.Fori(0, 4) as e:
                        it = gi * 4 + e
                        for n in range(2):
                            act.wait_ge(exp_pe.sem, exp_pe.at(it, f"a{n}"))
                            act.wait_ge(exp_dve.sem, exp_dve.before(it, f"h{n}"))
                            A_(two(e_tanh[:, n, :]), acc(4 * n), ACT.Tanh, scale=0.5).then_inc(exp_act.inc(f"t{n}"), 1)
                next_phase(act, "act", l)
            norm(DEPTH * 2)

        @block.gpsimd
        def _(pool):
            pool.memset(vf[:, :, :], 0.0).then_inc(zeroed, 1)
            pool.sem_inc(pair_pool.sem, len(pair_pool.names))
            pool.wait_ge(loaded, 16 * (KD + 1))
            with pool.Fori(0, DEPTH) as l:
                for _ in range(2):
                    next_phase(pool, "pool", l)
                with pool.Fori(0, NPAIR) as q:
                    it = l * NPAIR + q
                    for n, lv in enumerate(LEVELS):
                        o = CONSTS["level"][0] + (n + 1) * CH
                        mask = cst[0:CH, o:o + CH].rearrange("p (a b) -> p a b", a=1).to_broadcast([CH, 4, CH])
                        for x in range(3):
                            if n == 0:
                                pool.wait_ge(pair_dve.sem, pair_dve.at(it, f"gram{2 * x + 1}"))
                            else:
                                pool.wait_ge(pair_pe.sem, pair_pe.at(it, f"t{LEVELS[n - 1]}_{x}"))
                            nc.gpsimd.tensor_tensor(lv_as[x], gr[:, 4 * x:4 * x + 4, 0:CH], mask, ALU.mult
                                                    ).then_inc(pair_pool.inc(f"lv{lv}_{x}"), 1)
                for _ in range(N_PHASES - 2):
                    next_phase(pool, "pool", l)

        @block.vector
        def _(dve):
            V = nc.vector
            for S in DVE_STEPS:
                dve.sem_inc(S.sem, len(S.names))
            dve.wait_ge(loaded, 16 * (KD + 1))
            dve.wait_ge(zeroed, 1)

            def norm(turn, gains):
                dve.wait_ge(norm_pe.sem, norm_pe.at(turn, "sum"))
                V.tensor_scalar(two(n_rs), acc(0), 1.0 / D, EPS, ALU.mult, ALU.add).then_inc(norm_dve.inc("mean"), 1)
                dve.wait_ge(norm_act.sem, norm_act.at(turn, "sqrt"))
                V.reciprocal(n_rs, n_rs)
                dve.drain()
                for j in range(KD):
                    V.scalar_tensor_tensor(u[:, j, :], h[:, j, :], pc(gains, j), n_rs, ALU.mult, ALU.mult)
                dve.drain()

            def rope(dst, src, rotated, tmp, rows=slice(0, P)):
                V.tensor_tensor(tmp, rotated, two(sin[rows, :]), ALU.mult)
                V.tensor_tensor(src, src, cos[rows, :], ALU.mult)
                dve.drain()
                return V.tensor_tensor(dst, src, tmp.rearrange("p a b -> p (a b)"), ALU.add)

            def shift(dst, raw, mu, tmp):
                V.tensor_tensor(tmp, raw[:, 0:T], raw[:, 1:T + 1], ALU.subtract)
                dve.drain()
                return V.scalar_tensor_tensor(dst, tmp, mu, raw[:, 1:T + 1], ALU.mult, ALU.add)

            with dve.Fori(0, DEPTH) as l:
                dve.wait_ge(par_full, (l + 1) * 16)
                norm(l * 2, "norm_mix")
                next_phase(dve, "dve", l)

                V.memset(raw_r[:, 0:1], 0.0)
                V.memset(raw_k[:, 0:1], 0.0)
                V.memset(raw_v[:, 0:1], 0.0)
                V.tensor_scalar(half_w0, par[:, PARAMS["w0"][0]:PARAMS["w0"][0] + 8], 0.5, None, ALU.mult)
                V.tensor_scalar(half_a0, par[:, PARAMS["a0"][0]:PARAMS["a0"][0] + 8], 0.5, None, ALU.mult)
                V.tensor_scalar(half_v0, par[:, PARAMS["v0"][0]:PARAMS["v0"][0] + 8], 0.5, None, ALU.mult)
                dve.drain()
                dve.wait_ge(low_act.sem, low_act.at(l, "wa"))
                shift(lr_wa, raw_r, pc("mu_wa"), tz)
                dve.wait_ge(low_act.sem, low_act.at(l, "g"))
                shift(lr_g, raw_k, pc("mu_g"), ta)
                dve.wait_ge(low_act.sem, low_act.at(l, "vres"))
                shift(lr_v, raw_v, pc("mu_vres"), tv).then_inc(low_dve.inc("shift"), 1)
                dve.wait_ge(low_act.sem, low_act.at(l, "tanh"))
                V.tensor_scalar(lr_g, lr_g, 0.5, 0.5, ALU.mult, ALU.add)
                next_phase(dve, "dve", l)

                with dve.Fori(0, NPAIR) as q:
                    it = l * NPAIR + q
                    S = pair_dve

                    def pe_did(name):
                        dve.wait_ge(pair_pe.sem, pair_pe.at(it, name))

                    def act_did(name):
                        dve.wait_ge(pair_act.sem, pair_act.at(it, name))

                    vfq = vf[:, ds(q, 1), :].rearrange("p a b -> p (a b)")
                    V.memset(state, 0.0)
                    act_did("r")
                    shift(pr, raw_r, pc("mu_r", q), G)
                    act_did("k")
                    shift(pk, raw_k, pc("mu_k", q), Gi)
                    act_did("v")
                    shift(pv, raw_v, pc("mu_v", q), bonus)
                    act_did("z")
                    rate = -0.5 * float(np.exp(-0.5))
                    V.tensor_scalar(tz, tz, rate, rate, ALU.mult, ALU.add).then_inc(S.inc("rate"), 1)
                    dve.drain()
                    V.tensor_tensor_scan(cum, c("reset"), tz, 0.0, ALU.mult, ALU.add)
                    dve.drain()
                    V.tensor_tensor(Gx, cum, tz, ALU.subtract).then_inc(S.inc("c"), 1)
                    act_did("a")
                    V.tensor_scalar(ta, ta, 0.5, 0.5, ALU.mult, ALU.add)
                    act_did("vres")
                    V.tensor_scalar(tv, tv, 0.5, 0.5, ALU.mult, ALU.add)
                    V.tensor_tensor(bonus, vfq, pv, ALU.subtract)
                    dve.drain()
                    V.scalar_tensor_tensor(bonus, bonus, pc("later"), tv, ALU.mult, ALU.mult)
                    dve.drain()
                    V.tensor_tensor(pv, pv, bonus, ALU.add)
                    dve.drain()
                    V.tensor_tensor(tv, pv, vfq, ALU.subtract)
                    dve.drain()
                    V.scalar_tensor_tensor(vfq, tv, pc("first"), vfq, ALU.mult, ALU.add).then_inc(S.inc("v"), 1)
                    V.tensor_scalar(kk, pk, pc("k_k", q), None, ALU.mult).then_inc(S.inc("kk"), 1)
                    V.tensor_scalar(kh, ta, -1.0, pc("k_a", q), ALU.add, ALU.mult)
                    dve.drain()
                    V.scalar_tensor_tensor(kh, kh, 1.0, pk, ALU.add, ALU.mult)
                    dve.drain()
                    V.scalar_tensor_tensor(tz, pr, pc("r_k", q), kh, ALU.mult, ALU.mult).then_inc(S.inc("rkk"), 1)
                    pe_did("kk")
                    V.tensor_scalar(two(sqk), acc(6), 1e-24, None, ALU.max).then_inc(S.inc("kkmax"), 1)
                    pe_did("bonus")
                    V.tensor_tensor(two(bonus), acc(0), two(pv), ALU.mult).then_inc(S.inc("bonus"), 1)
                    act_did("norm")
                    V.reciprocal(sqk, sqk)
                    dve.drain()
                    V.tensor_tensor(kk, kk, sqk, ALU.mult)
                    dve.drain()
                    V.scalar_tensor_tensor(ar[:, 0, :], kk, -1.0, Gx, ALU.mult, ALU.mult)
                    V.tensor_tensor(bb, kk, ta, ALU.mult)
                    V.tensor_tensor(ar[:, 1, :], pr, G, ALU.mult)
                    dve.drain()
                    V.tensor_tensor(bb, bb, Gi, ALU.mult).then_inc(S.inc("ab"), 1)
                    V.tensor_tensor(kb_, kh, Gi, ALU.mult)
                    dve.drain().then_inc(S.inc("rbk"), 1)
                    gmask = c("grams", CH)
                    for i in range(NCH):
                        pe_did(f"gram{i}")
                        b = 2 * (i % 4)
                        V.tensor_tensor(gr[:, 2 * i:2 * i + 2, :], ps[0:CH, b:b + 2, 0:4 * CH],
                                        gmask[:, 0:4 * CH].rearrange("p (a b) -> p a b", a=1).to_broadcast([CH, 2, 4 * CH]),
                                        ALU.mult)
                        V.tensor_tensor(low[:, 2 * i:2 * i + 2, :], ps[0:CH, b:b + 2, 4 * CH:5 * CH],
                                        gmask[:, 4 * CH:5 * CH].rearrange("p (a b) -> p a b", a=1).to_broadcast([CH, 2, CH]),
                                        ALU.mult)
                        dve.drain().then_inc(S.inc(f"gram{i}"), 1)
                    o = CONSTS["level"][0]
                    lv1 = cst[0:CH, o:o + CH].rearrange("p (a b) -> p a b", a=1).to_broadcast([CH, 4, CH])
                    i88 = ident[0:CH, 0:CH].rearrange("p (a b) -> p a b", a=1).to_broadcast([CH, 4, CH])
                    for x in range(3):
                        V.tensor_tensor(inv_t[:, 4 * x:4 * x + 4, :], gr[:, 4 * x:4 * x + 4, 0:CH], lv1, ALU.mult)
                        V.tensor_tensor(inv[:, 4 * x:4 * x + 4, :], low[:, 4 * x:4 * x + 4, :], lv1, ALU.mult)
                        dve.drain()
                        V.tensor_tensor(inv_t[:, 4 * x:4 * x + 4, :], inv_t[:, 4 * x:4 * x + 4, :], i88, ALU.add)
                        V.tensor_tensor(inv[:, 4 * x:4 * x + 4, :], inv[:, 4 * x:4 * x + 4, :], i88, ALU.add)
                        dve.drain().then_inc(S.inc(f"one{x}"), 1)
                    for lv in LEVELS:
                        for x in range(3):
                            pe_did(f"nm{lv}_{x}")
                            for dst, b in ((inv_t, 3 + x % 2), (inv, 5 + x % 2)):
                                V.tensor_tensor(dst[:, 4 * x:4 * x + 4, :], dst[:, 4 * x:4 * x + 4, :],
                                                ps[0:CH, b, 0:4 * CH].rearrange("p (a b) -> p a b", a=4), ALU.add)
                            dve.drain().then_inc(S.inc(f"nm{lv}_{x}"), 1)
                    for i in range(NCH):
                        pe_did(f"x{i}")
                        V.tensor_copy(xs[0:CH, :], ps[0:CH, 0, 0:P]).then_inc(S.inc(f"x{i}"), 1)
                        pe_did(f"d{i}")
                        V.tensor_tensor(state, state, ps[:, 3, 0:P], ALU.add)
                        dve.drain()
                        V.scalar_tensor_tensor(state, state, G[:, i * CH + CH - 1:i * CH + CH], headones, ALU.mult,
                                               ALU.mult).then_inc(S.inc(f"s{i}"), 1)
                    pe_did("mean")
                    V.scalar_tensor_tensor(two(kk), acc(4), -1.0 / 64, two(pairs_o), ALU.mult, ALU.add
                                           ).then_inc(S.inc("cen"), 1)
                    pe_did("var")
                    V.tensor_scalar(two(G), acc(6), 1.0 / 64, GN_EPS, ALU.mult, ALU.add).then_inc(S.inc("var"), 1)
                    act_did("std")
                    V.reciprocal(G, G)
                    dve.drain()
                    V.tensor_tensor(kk, kk, G, ALU.mult)
                    dve.drain()
                    V.tensor_scalar(kk, kk, pc("ln_w", q), pc("ln_b", q), ALU.mult, ALU.add)
                    dve.drain()
                    V.tensor_tensor(kk, kk, bonus, ALU.add)
                    dve.drain()
                    V.tensor_tensor(y[:, ds(q, 1), :].rearrange("p a b -> p (a b)"), kk, pg, ALU.mult
                                    ).then_inc(S.inc("y"), 1)
                next_phase(dve, "dve", l)

                def merge(k):
                    with dve.Fori(0, 4) as q:
                        it = l * 12 + 4 * k + q
                        for n in range(2):
                            dve.wait_ge(merge_act.sem, merge_act.at(it, f"g{n}"))
                            dve.wait_ge(merge_pe.sem, merge_pe.at(it, f"p{n}"))
                            V.scalar_tensor_tensor(two(g_tmp[:, n, :]), two(g_tanh[:, n, :]), 1.0, acc(4 * n),
                                                   ALU.add, ALU.mult)
                            dve.drain()
                            dst = m[:, ds(2 * q + n, 1), :].rearrange("p a b -> p (a b)")
                            if k == 0:
                                last = V.tensor_scalar(dst, g_tmp[:, n, :], 0.5, None, ALU.mult)
                            else:
                                last = V.scalar_tensor_tensor(dst, g_tmp[:, n, :], 0.5, dst, ALU.mult, ALU.add)
                            last.then_inc(merge_dve.inc(f"m{n}"), 1)
                    next_phase(dve, "dve", l)

                merge(0)
                o = CONSTS["counts"][0]
                for j in range(8):
                    w = POOL_WINDOWS[j // 2]
                    dve.wait_ge(pool_act.sem, pool_act.at(l, f"p{j}"))
                    src, k = p_raw[:, j % 2, :], 1
                    bufs = [p_a, p_b]
                    while k < w:
                        dst = bufs[0]
                        V.tensor_tensor(dst[:, k:T], src[:, k:T], src[:, 0:T - k], ALU.add)
                        V.tensor_copy(dst[:, 0:k], src[:, 0:k])
                        dve.drain()
                        src, k = dst, 2 * k
                        bufs.reverse()
                    dst = bufs[0]
                    V.scalar_tensor_tensor(pooled[:, j, w:T], src[:, w:T], 1.0 / w, p_raw[:, j % 2, w:T], ALU.mult,
                                           ALU.subtract)
                    V.tensor_tensor(dst[:, 0:w], src[:, 0:w], cst[:, o:o + w], ALU.mult)
                    dve.drain()
                    V.tensor_tensor(pooled[:, j, 0:w], dst[:, 0:w], p_raw[:, j % 2, 0:w], ALU.subtract)
                    dve.drain().then_inc(pool_dve.inc(f"p{j}"), 1)
                next_phase(dve, "dve", l)
                merge(1)

                def pe_did(name):
                    dve.wait_ge(lat_pe.sem, lat_pe.at(l, name))

                def act_did(name):
                    dve.wait_ge(lat_act.sem, lat_act.at(l, name))
                S = lat_dve
                pe_did("qsum")
                V.tensor_scalar(two(l_rs), acc(2), 1.0 / 256, EPS, ALU.mult, ALU.add)
                pe_did("kvsum")
                V.tensor_scalar(two(l_rs2), acc(4), 1.0 / 128, EPS, ALU.mult, ALU.add)
                dve.drain().then_inc(S.inc("means"), 1)
                act_did("std")
                V.reciprocal(l_rs, l_rs)
                V.reciprocal(l_rs2, l_rs2)
                dve.drain()
                for j in range(2):
                    V.scalar_tensor_tensor(cq[:, j, :], cq[:, j, :], pc("q_norm", j), l_rs, ALU.mult, ALU.mult)
                V.scalar_tensor_tensor(ckv, ckv, pc("kv_norm"), l_rs2, ALU.mult, ALU.mult)
                dve.drain().then_inc(S.inc("latents"), 1)
                pe_did("mean")
                V.scalar_tensor_tensor(two(kidx), acc(6), -1.0 / 64, two(kidx), ALU.mult, ALU.add
                                       ).then_inc(S.inc("center"), 1)
                pe_did("var")
                V.tensor_scalar(two(l_tmp), acc(6), 1.0 / 64, EPS, ALU.mult, ALU.add).then_inc(S.inc("var"), 1)
                act_did("std2")
                V.reciprocal(l_tmp, l_tmp)
                dve.drain()
                V.tensor_tensor(kidx, kidx, l_tmp, ALU.mult)
                dve.drain()
                V.tensor_scalar(kidx, kidx, pc("idx_w"), pc("idx_b"), ALU.mult, ALU.add).then_inc(S.inc("kidx"), 1)
                pe_did("kperm")
                rope(kidx, kidx, acc(2), two(l_tmp))
                pe_did("rperm")
                rope(kr, kr, acc(4), two(l_tmp2))
                dve.drain().then_inc(S.inc("ropes"), 1)
                for j in range(4):
                    pe_did(f"qp{j}")
                    rope(qi[:, j, :], qi[:, j, :], acc(2 * j), two((l_tmp, l_tmp2)[j % 2])
                         ).then_inc(S.inc(f"rope{j}"), 1)
                next_phase(dve, "dve", l)

                tri, tri_b = c("causal", CH), c("bias", CH)
                V.tensor_copy(sel_of(0), tri_b.rearrange("p (a b) -> p a b", a=1))
                for n, (i, hd) in enumerate(IDX):
                    z, wd = n % 2, (i + 1) * CH
                    dve.wait_ge(idx_act.sem, idx_act.at(l, f"s{i}_{hd}"))
                    if hd == 0:
                        last = V.tensor_scalar(score[:, 0:wd], relu_b[:, z, 0:wd], wtok[:, i, 0:1], None, ALU.mult)
                    else:
                        last = V.scalar_tensor_tensor(score[:, 0:wd], relu_b[:, z, 0:wd], wtok[:, i, hd:hd + 1],
                                                      score[:, 0:wd], ALU.mult, ALU.add)
                    last.then_inc(idx_dve.inc(f"s{i}_{hd}"), 1)
                    dve.drain()
                    if hd < 7:
                        continue
                    V.tensor_tensor(score[:, i * CH:wd], score[:, i * CH:wd], tri, ALU.add)
                    dve.drain()
                    for _ in range(TOPK // 8):
                        V.max(top8, score[:, 0:wd])
                        dve.drain()
                        V.match_replace(score[:, 0:wd], top8, score[:, 0:wd], TAKEN)
                        dve.drain()
                    s_i = sel_of(i)
                    V.tensor_scalar(s_i, score[:, 0:wd].rearrange("p (a b) -> p a b", b=CH), TAKEN, NEG_BIAS,
                                    ALU.is_gt, ALU.mult)
                    dve.drain()
                    V.tensor_tensor(s_i[:, i, :], s_i[:, i, :], tri_b, ALU.add)
                next_phase(dve, "dve", l)

                with dve.Fori(0, 2) as q:
                    it = l * 2 + q
                    S = att_dve

                    def pe_did(name):
                        dve.wait_ge(att_pe.sem, att_pe.at(it, name))

                    def act_did(name):
                        dve.wait_ge(att_act.sem, att_act.at(it, name))

                    V.tensor_copy(kh2[64:96, 0, :], kr[64:96, :])
                    V.tensor_copy(kh2[64:96, 1, :], kr[64:96, :])
                    dve.drain().then_inc(S.inc("kr"), 1)
                    for hd in range(8):
                        z = hd % 2
                        pe_did(f"perm{hd}")
                        rope(qh[64:96, z, :], qh[64:96, z, :], acc(6, slice(64, 96)), two(rope_t[64:96, :]),
                             slice(64, 96)).then_inc(S.inc(f"rope{hd}"), 1)
                        for step in range(NCH + 1):
                            if step < NCH:
                                i = step
                                wd, b, k = (i + 1) * CH, 2 * (i % 2), i % 2
                                pe_did(f"s{i}_{hd}")
                                if i >= 2:
                                    pe_did(f"pt{i - 2}_{hd}")
                                elif hd >= 1:
                                    pe_did(f"pt{i + 4}_{hd - 1}")
                                else:
                                    dve.wait_ge(att_pe.sem, att_pe.before(it, f"pt{i + 4}_7"))
                                alone(dve)
                                V.tensor_tensor_reduce(
                                    out=parts(es[:, k, 0:wd], i), in0=scores(b, i),
                                    in1=parts(sel_of(i).rearrange("p a b -> p (a b)"), i), scale=1.0,
                                    scalar=NEG_CAUSAL, op0=ALU.add, op1=ALU.max, accum_out=mx[:, k:k + 1])
                                dve.drain()
                                V.tensor_scalar(mx[:, k:k + 1], mx[:, k:k + 1], -ATT_SCALE, None, ALU.mult
                                                ).then_inc(S.inc(f"m{i}_{hd}"), 1)
                            if step >= 1:
                                i = step - 1
                                wd, k = (i + 1) * CH, i % 2
                                act_did(f"e{i}_{hd}")
                                V.reciprocal(ri[:, k:k + 1], rs[:, k:k + 1])
                                dve.drain()
                                V.tensor_scalar(es[:, k, 0:wd], es[:, k, 0:wd], ri[:, k:k + 1], None, ALU.mult
                                                ).then_inc(S.inc(f"n{i}_{hd}"), 1)
                next_phase(dve, "dve", l)
                merge(2)

                with dve.Fori(0, 2) as q:
                    it = l * 2 + q
                    for s in range(4):
                        dve.wait_ge(res_pe.sem, res_pe.at(it, f"o{s}"))
                        dst = h[:, ds(4 * q + s, 1), :].rearrange("p a b -> p (a b)")
                        V.tensor_tensor(two(dst), two(dst), acc(2 * s), ALU.add).then_inc(res_dve.inc(f"h{s}"), 1)
                next_phase(dve, "dve", l)
                norm(l * 2 + 1, "norm_ffn")
                next_phase(dve, "dve", l)

                S = rt_dve
                dve.wait_ge(rt_pe.sem, rt_pe.at(l, "logits"))
                ob = PARAMS["router_b"][0]
                V.tensor_tensor(lg, ps[0:CH, 0, 0:20 * NCH].rearrange("p (a b) -> p a b", a=NCH),
                                par[0:CH, ob:ob + 20].rearrange("p (a b) -> p a b", a=1).to_broadcast([CH, NCH, 20]),
                                ALU.add)
                dve.drain()
                keys = c("keys", CH).rearrange("p (a b) -> p a b", a=1).to_broadcast([CH, NCH, 4])

                def over(v):
                    return v.rearrange("p (a b) -> p a b", b=1).to_broadcast([CH, NCH, 4])

                def first_max(dst, src, top):
                    V.tensor_reduce(top, src, AX.X, ALU.max)
                    dve.drain()
                    V.tensor_tensor(r2, src, over(top), ALU.is_ge)
                    dve.drain()
                    V.tensor_tensor(r2, r2, keys, ALU.mult)
                    dve.drain()
                    V.tensor_reduce(s5, r2, AX.X, ALU.max)
                    dve.drain()
                    V.tensor_tensor(dst, r2, over(s5), ALU.is_equal)
                    dve.drain()

                first_max(oh, lg[:, :, 0:4], s1)
                V.tensor_tensor(r1, lg[:, :, 0:4], over(s1), ALU.subtract)
                dve.drain().then_inc(S.inc("gmax"), 1)
                e16 = lg[:, :, 4:20].rearrange("p a (g e) -> p a g e", g=4)
                r16v = r16.rearrange("p a (g e) -> p a g e", g=4)
                for g in range(4):
                    V.tensor_tensor(r16v[:, :, g, :], e16[:, :, g, :], oh[:, :, g:g + 1].to_broadcast([CH, NCH, 4]),
                                    ALU.mult)
                dve.drain()
                V.tensor_reduce(r3, r16.rearrange("p a (g e) -> p a e g", g=4), AX.X, ALU.add)
                dve.drain()
                first_max(oh1, r3, s2)
                V.scalar_tensor_tensor(r3, oh1, NEG_CAUSAL, r3, ALU.mult, ALU.add)
                dve.drain()
                first_max(oh2, r3, s3)
                V.tensor_tensor(s4, s3, s2, ALU.subtract).then_inc(S.inc("ediff"), 1)
                dve.wait_ge(rt_act.sem, rt_act.at(l, "gexp"))
                V.tensor_reduce(s1, r1, AX.X, ALU.add)
                dve.wait_ge(rt_act.sem, rt_act.at(l, "eexp"))
                V.tensor_scalar(s2, s4, 1.0, None, ALU.add)
                dve.drain()
                V.tensor_tensor(s2, s2, s1, ALU.mult)
                dve.drain()
                V.reciprocal(s2, s2)
                dve.drain()
                V.tensor_tensor(s3, s2, s4, ALU.mult)
                V.tensor_tensor(oh1, oh1, over(s2), ALU.mult)
                dve.drain()
                V.tensor_tensor(oh2, oh2, over(s3), ALU.mult)
                dve.drain()
                V.tensor_tensor(ce, oh1, oh2, ALU.add)
                dve.drain()
                for g in range(4):
                    V.tensor_tensor(comb[:, :, 4 * g:4 * g + 4], ce, oh[:, :, g:g + 1].to_broadcast([CH, NCH, 4]),
                                    ALU.mult)
                dve.drain().then_inc(S.inc("combine"), 1)
                next_phase(dve, "dve", l)

                with dve.Fori(0, 4) as g:
                    gi = l * 4 + g
                    for e in range(4):
                        if e == 0:
                            dve.wait_ge(grp_pe.sem, grp_pe.before(gi, "c3"))
                        else:
                            dve.wait_ge(grp_pe.sem, grp_pe.at(gi, f"c{e - 1}"))
                        V.tensor_scalar(comb_sel, comb_t, ident[0:16, ds(4 * g + e, 1)], None, ALU.mult
                                        ).then_inc(grp_dve.inc(f"c{e}"), 1)
                    dve.wait_ge(grp_act.sem, grp_act.at(gi, "c3"))
                    alone(dve)
                    with dve.Fori(0, 4) as e:
                        it = gi * 4 + e
                        for n in range(2):
                            dve.wait_ge(exp_act.sem, exp_act.at(it, f"t{n}"))
                            dve.wait_ge(exp_pe.sem, exp_pe.at(it, f"b{n}"))
                            tmp = two(e_tmp[:, n, :])
                            V.scalar_tensor_tensor(tmp, two(e_tanh[:, n, :]), 1.0, acc(4 * n), ALU.add, ALU.mult)
                            dve.drain()
                            V.tensor_tensor(tmp, tmp, acc(4 * n + 2), ALU.mult)
                            dve.drain()
                            V.scalar_tensor_tensor(hid[:, ds(2 * e + n, 1), :].rearrange("p a b -> p (a b)"),
                                                   e_tmp[:, n, :], 0.5,
                                                   comb_b[:, ds(e, 1), :].rearrange("p a b -> p (a b)"),
                                                   ALU.mult, ALU.mult)
                            dve.drain().then_inc(exp_dve.inc(f"h{n}"), 1)
                    with dve.Fori(0, 2) as q:
                        it = gi * 2 + q
                        for s in range(4):
                            dve.wait_ge(dn_pe.sem, dn_pe.at(it, f"o{s}"))
                            dst = h[:, ds(4 * q + s, 1), :].rearrange("p a b -> p (a b)")
                            V.tensor_tensor(two(dst), two(dst), acc(2 * s), ALU.add).then_inc(dn_dve.inc(f"h{s}"), 1)
                next_phase(dve, "dve", l)
            norm(DEPTH * 2, "norm_final")
            dve.drain().then_inc(out_ready, 1)


def constant_table():
    t = np.zeros((P, N_CONST), np.float32)

    def put(name, a, rows=P):
        o, n = CONSTS[name]
        t[:rows, o:o + n] = a

    p = np.arange(P)
    put("ident", np.eye(P))
    put("ones", 1.0)
    put("headones", (p[:, None] // 64 == p[None, :] // 64))
    rot = p % 64 < 32
    partner = np.where(rot, np.where(p % 32 < 16, p + 16, p - 16), p)
    put("perm", partner[:, None] == p[None, :])
    inv = np.float32(10000.0) ** (-np.arange(0, 32, 2, dtype=np.float32) / np.float32(32))
    ang = np.arange(T, dtype=np.float32)[None, :] * inv.astype(np.float32)[p % 16][:, None]
    put("cos", np.where(rot[:, None], np.cos(ang), 1.0))
    put("sin", np.where(rot[:, None], np.where((p % 32 < 16)[:, None], -1.0, 1.0) * np.sin(ang), 0.0))
    put("reset", (np.arange(T) % CH != 0)[None, :])
    a, b = np.arange(CH)[:, None], np.arange(CH)[None, :]
    put("grams", np.concatenate([a < b, a <= b, a < b, a <= b, a > b], 1), CH)
    put("level", np.concatenate([(a // (2 * n) == b // (2 * n)) & (a // n != b // n) for n in [1] + LEVELS], 1), CH)
    put("causal", np.where(b > a, NEG_CAUSAL, 0.0), CH)
    put("bias", np.where(b > a, NEG_BIAS, 0.0), CH)
    put("keys", np.array([[4.0, 3.0, 2.0, 1.0]]))
    put("counts", 1.0 / np.arange(1, 17)[None, :])
    return t


def param_table(w):
    t = np.zeros((DEPTH, P, N_PARAM), np.float32)
    for l in range(DEPTH):
        def put(name, v):
            o, n = PARAMS[name]
            t[l, :, o:o + n] = np.asarray(v).reshape(n, P).T

        def padded(v):
            out = np.zeros(P, np.float32)
            out[:len(v)] = v
            return out

        for name, key in (("norm_mix", "norm_mix"), ("norm_ffn", "norm_ffn"), ("pool_scale", "pool_scale"),
                          ("w0", "rwkv_w0"), ("a0", "rwkv_a0"), ("k_k", "rwkv_k_k"), ("k_a", "rwkv_k_a"),
                          ("r_k", "rwkv_r_k"), ("ln_w", "rwkv_ln_w"), ("ln_b", "rwkv_ln_b"),
                          ("q_norm", "mla_q_norm"), ("kv_norm", "mla_kv_norm")):
            put(name, w[key][l])
        put("norm_final", w["norm_final"])
        put("v0", w["vres_v0"][max(l - 1, 0)])
        mu = w["mu_shift"][l]
        put("mu_r", mu[0:D])
        put("mu_k", mu[D:2 * D])
        put("mu_v", mu[2 * D:3 * D])
        put("mu_wa", mu[3 * D:3 * D + 128])
        put("mu_g", mu[3 * D + 128:])
        put("mu_vres", padded(w["vres_mu"][max(l - 1, 0)]))
        put("idx_w", np.concatenate([w["idx_k_norm_w"][l]] * 2))
        put("idx_b", np.concatenate([w["idx_k_norm_b"][l]] * 2))
        put("later", np.full(P, float(l > 0), np.float32))
        put("first", np.full(P, float(l == 0), np.float32))
        rt = np.concatenate([w["router_w_group"][l], w["router_w_expert"][l]], 1)
        o, n = PARAMS["router"]
        t[l, :, o:o + n] = rt.reshape(KD, P, 20).transpose(1, 0, 2).reshape(P, 160)
        o, n = PARAMS["router_b"]
        t[l, :, o:o + n] = np.concatenate([w["router_b_group"][l], w["router_b_expert"][l]])[None, :]
    return t


def weight_stream(w):
    out = np.zeros((DEPTH * LAYER_ROUNDS * RING, P, KD * P), np.float32)
    n = 0
    o_a = 3 * D
    o_s = o_a + D
    o_c = o_s + 3 * D + 256

    def columns(mat):
        nonlocal n
        v = out[n].reshape(P, KD, P)
        v[:, :, :mat.shape[1]] = mat.reshape(KD, P, -1).transpose(1, 0, 2)
        n += 1

    def blocks(*mats):
        nonlocal n
        for mat, row, col in mats:
            out[n, row:row + mat.shape[0], col:col + mat.shape[1]] = mat
        n += 1

    for l in range(DEPTH):
        wi, lv = w["w_in"][l], max(l - 1, 0)

        def start(phase):
            assert n == (l * LAYER_ROUNDS + FIRST[phase]) * RING, (phase, n)

        def merge(phase, proj, gate):
            start(phase)
            for j in range(8):
                columns(proj[:, j * P:(j + 1) * P])
                columns(wi[:, gate * D + j * P:gate * D + (j + 1) * P])

        start("lowrank")
        columns(wi[:, o_s + 3 * D:o_s + 3 * D + 128])
        columns(wi[:, o_s + 3 * D + 128:o_s + 3 * D + 256])
        columns(w["vres_w_down"][lv])
        n += 1
        start("pairs")
        for q in range(NPAIR):
            cq = slice(q * P, (q + 1) * P)
            for k in range(3):
                columns(wi[:, o_s + k * D + q * P:o_s + k * D + (q + 1) * P])
            blocks((w["rwkv_w2"][l][:, cq], 0, 0), (w["rwkv_a2"][l][:, cq], 64, P),
                   (w["rwkv_g2"][l][:, cq], 0, 2 * P), (w["vres_v2"][lv][:, cq], 0, 3 * P))
        merge("merge_b", w["w_proj_b"][l], 1)
        start("pool")
        for j in range(8):
            columns(wi[:, o_a + j * P:o_a + (j + 1) * P])
        for half in range(2):
            blocks(*((w["pool_w"][l, 2 * half + g, kb * P:(kb + 1) * P, nb * P:(nb + 1) * P], 0,
                      (g * 4 + nb * 2 + kb) * P) for g in range(2) for nb in range(2) for kb in range(2)))
        n += 2
        merge("merge_a", w["w_proj_a"][l], 0)
        start("dsa_in")
        columns(wi[:, o_c:o_c + 128])
        columns(wi[:, o_c + 128:o_c + 256])
        columns(wi[:, o_c + 256:o_c + 384])
        kidx = wi[:, o_c + 416:o_c + 480]
        columns(np.concatenate([kidx, kidx], 1))
        columns(np.concatenate([np.zeros((D, 64), np.float32), wi[:, o_c + 384:o_c + 416],
                                wi[:, o_c + 480:o_c + 488]], 1))
        iq = w["idx_w_q"][l]
        blocks(*((iq[kb * P:(kb + 1) * P, j * P:(j + 1) * P], 0, (2 * j + kb) * P)
                 for j in range(4) for kb in range(2)))
        n += 2
        start("heads")
        for b in range(4):
            uq = w["mla_w_uq"][l]
            blocks(*((uq[kb * P:(kb + 1) * P, (4 * b + k) * 96:(4 * b + k + 1) * 96], 0, (2 * k + kb) * P)
                     for k in range(4) for kb in range(2)))
            blocks(*((w["mla_w_uk"][l, 4 * b + k], 0, 64 * k) for k in range(4)),
                   *((w["mla_w_uv"][l, 4 * b + k], 0, 256 + 64 * k) for k in range(4)))
        merge("merge_c", w["w_proj_c"][l], 2)
        start("out")
        for j in range(8):
            columns(w["w_out"][l][:, j * P:(j + 1) * P])
        start("moe")
        for g in range(4):
            for e in range(4 * g, 4 * g + 4):
                for f in range(2):
                    columns(w["expert_w1"][l, e][:, f * P:(f + 1) * P])
                    columns(w["expert_w3"][l, e][:, f * P:(f + 1) * P])
            down = np.concatenate([w["expert_w2"][l, e] for e in range(4 * g, 4 * g + 4)], 0)
            for j in range(8):
                columns(down[:, j * P:(j + 1) * P])
    assert n == out.shape[0], (n, out.shape)
    return out


def kernel(**inputs):
    import concourse.bacc as bacc
    from concourse.bass_utils import run_bass_kernel_spmd

    w = {k: np.asarray(v) for k, v in inputs.items()}
    tokens = np.concatenate([w["meta_tokens"], w["x"][0]], 0)
    arrays = {
        "x_t": np.ascontiguousarray(tokens.T.reshape(KD, P, T)),
        "consts": constant_table(),
        "params": param_table(w),
        "stream": weight_stream(w),
    }
    nc = bacc.Bacc("TRN2", target_bir_lowering=False, num_devices=1)
    args = [nc.dram_tensor(k, a.shape, mybir.dt.from_np(a.dtype), kind="ExternalInput").ap()
            for k, a in arrays.items()]
    args.append(nc.dram_tensor("out_t", (KD, P, SEQ), mybir.dt.float32, kind="ExternalOutput").ap())
    trunk_program(nc, *args)
    r = run_bass_kernel_spmd(nc, [arrays], core_ids=[0])
    return r.results[0]["out_t"].reshape(D, SEQ).T.reshape(1, SEQ, D)
```

```python
import numpy as np
import concourse.bass as bass
from concourse import mybir
from contextlib import ExitStack

D, SEQ, N_META, DEPTH = 1024, 512, 16, 2
T = SEQ + N_META
P = 128
KD = D // P
HALF = T // 2
CH = 96
NCH = -(-T // CH)
TP = NCH * CH
GROUP_COLS = 192
NPAIR = 8
RING = 4
EPS = 1e-6
GN_EPS = 64e-5
TOPK = min(256, SEQ // 4)
LEVELS = [2, 4, 8, 16, 32, 64]
NEG_CAUSAL, TAKEN, NEG_BIAS = -3.0e38, -3.2e38, -1.0e30
IDX_SCALE = 8 ** -0.5 * 64 ** -0.5
ATT_SCALE = (64 + 32) ** -0.5
GRAM_BANKS = (4, 6, 2, 0)
POOL_WINDOWS = (2, 4, 8, 16)

ROUNDS = {"lowrank": 1, "pairs": 8, "merge_b": 4, "pool": 3, "merge_a": 4, "dsa_in": 2, "heads": 2,
          "merge_c": 4, "out": 2, "moe": 24}
FIRST, _n = {}, 0
for _k, _v in ROUNDS.items():
    FIRST[_k] = _n
    _n += _v
LAYER_ROUNDS = _n

CONSTS, _n = {}, 0
for _k, _v in (("ident", 128), ("ones", 128), ("headones", 128), ("perm", 128), ("cos", T), ("sin", T),
               ("reset", T), ("grams", 4 * CH), ("low1", CH), ("level", (1 + len(LEVELS)) * CH), ("causal", CH),
               ("bias", CH), ("keys", 4), ("counts", 16), ("slot", NCH), ("own", NCH)):
    CONSTS[_k] = (_n, _v)
    _n += _v
N_CONST = _n
PARAMS, _n = {}, 0
for _k, _v in (("norm_mix", 8), ("norm_ffn", 8), ("norm_final", 8), ("pool_scale", 8), ("w0", 8), ("a0", 8),
               ("k_k", 8), ("k_a", 8), ("r_k", 8), ("ln_w", 8), ("ln_b", 8), ("v0", 8), ("mu_r", 8),
               ("mu_k", 8), ("mu_v", 8), ("mu_wa", 1), ("mu_g", 1), ("mu_vres", 1), ("q_norm", 2),
               ("kv_norm", 1), ("idx_w", 1), ("idx_b", 1), ("later", 1), ("first", 1), ("router", 160),
               ("router_b", 20)):
    PARAMS[_k] = (_n, _v)
    _n += _v
N_PARAM = _n


def tile_rows(i):
    return min(CH, T - i * CH)


def tile_keys(i):
    return min((i + 1) * CH, T)


def window(i):
    return min(i * CH, T - CH)


class Steps:

    def __init__(self, sem, names):
        self.sem, self.names, self.next = sem, list(names), 0
        self.place = {n: i for i, n in enumerate(self.names)}

    def inc(self, name):
        assert self.names[self.next] == name, (self.names[self.next], name)
        self.next = (self.next + 1) % len(self.names)
        return self.sem

    def at(self, turn, name):
        return (turn + 1) * len(self.names) + self.place[name] + 1

    def before(self, turn, name):
        return turn * len(self.names) + self.place[name] + 1


def trunk_program(nc, x_t, consts, params, stream, out_t):
    f32 = mybir.dt.float32
    ALU = mybir.AluOpType
    ACT = mybir.ActivationFunctionType
    AX = mybir.AxisListType
    ds = bass.ds
    ctx = ExitStack()
    with ctx:
        def sb(name, shape):
            return ctx.enter_context(nc.sbuf_tensor(name, shape, f32))

        def sem(name):
            return ctx.enter_context(nc.semaphore(name))

        h = sb("h", [P, KD, T])
        u = sb("u", [P, KD, T])
        y = sb("y", [P, KD, T])
        m = sb("m", [P, KD, T])
        v_first = nc.dram_tensor("v_first", (NPAIR, P, T), f32, kind="Internal").ap()
        ring = sb("ring", [P, RING, KD * P])
        cst = sb("cst", [P, N_CONST])
        par = sb("par", [P, N_PARAM])
        scratch = sb("scratch", [P, 26400])
        ps = ctx.enter_context(nc.psum_tensor("ps", [P, 8, 512], f32))

        def c(name, rows=P):
            o, n = CONSTS[name]
            return cst[0:rows, o:o + n]

        ident, ones, headones, perm, cos, sin = map(c, ("ident", "ones", "headones", "perm", "cos", "sin"))

        def pc(name, j=0, rows=P):
            o, n = PARAMS[name]
            return par[0:rows, ds(o + j, 1)] if not isinstance(j, int) else par[0:rows, o + j:o + j + 1]

        def area(base=scratch[:, :]):
            at = [0]

            def take(*shape, rows=P):
                n = int(np.prod(shape))
                v = base[0:rows, at[0]:at[0] + n]
                at[0] += n
                assert at[0] <= base.shape[1], (at[0], base.shape)
                if len(shape) == 2:
                    v = v.rearrange("p (a b) -> p a b", a=shape[0])
                if len(shape) == 3:
                    v = v.rearrange("p (a b c) -> p a b c", a=shape[0], b=shape[1])
                return v
            return take

        def acc(bank, rows=slice(0, P)):
            return ps[rows, bank:bank + 2, 0:HALF]

        def two(ap):
            return ap.rearrange("p (a b) -> p a b", a=2)

        w_full = [sem(f"w_full{s}") for s in range(RING)]
        w_free = [sem(f"w_free{s}") for s in range(RING)]
        loaded, stored, par_full = sem("loaded"), sem("stored"), sem("par_full")
        zeroed = sem("zeroed")
        ends = {k: sem(f"{k}_phase_end") for k in ("pe", "dve", "act", "pool")}

        N_PHASES = 15
        passed = {k: sem(f"{k}_passed") for k in ("PE", "DVE", "Activation", "Pool")}

        def alone(eng):
            eng.sem_inc(passed[eng.engine.name], 1)

        phase_of = {"pe": 0, "dve": 0, "act": 0, "pool": 0}

        def next_phase(eng, me, layer):
            phase_of[me] += 1
            k = phase_of[me]
            alone(eng)
            eng.drain().then_inc(ends[me], 1)
            for other in ("pe", "dve", "act", "pool"):
                if other != me:
                    eng.wait_ge(ends[other], layer * N_PHASES + k)
            alone(eng)

        norm_pe = Steps(sem("norm_pe"), ["sum"])
        norm_act = Steps(sem("norm_act"), ["sq0", "sq1", "sq2", "sq3", "sq4", "sq5", "sq6", "sq7", "sqrt"])
        norm_dve = Steps(sem("norm_dve"), ["mean"])
        low_pe = Steps(sem("low_pe"), ["wa", "g", "vres"])
        low_act = Steps(sem("low_act"), ["wa", "g", "vres", "tanh"])
        low_dve = Steps(sem("low_dve"), ["shift"])
        prep_pe = Steps(sem("prep_pe"), ["z", "a", "g", "vres", "r", "k", "kk", "v"])
        prep_act = Steps(sem("prep_act"), ["z", "a", "g", "vres", "G", "r", "k", "sq", "norm", "v"])
        prep_dve = Steps(sem("prep_dve"), ["c", "r", "kk", "rkk", "kkmax", "a", "rbk", "v"])
        prep_pool = Steps(sem("prep_pool"), ["r"])
        pair_pe = Steps(sem("pair_pe"), ["tb", "tk", "gram0", "gram1", "tv", "bonus"] + [f"gram{i}" for i in range(2, NCH)]
                        + [f"{s}{lv}_{x}" for lv in LEVELS for s in ("t", "nm") for x in range(3)]
                        + [f"{s}{i}" for i in range(NCH) for s in "xuod" if (s, i) != ("d", NCH - 1)]
                        + ["mean", "var"])
        pair_act = Steps(sem("pair_act"), ["tb", "tk", "tv"] + [f"t{lv}_{x}" for lv in LEVELS for x in range(3)]
                         + [f"{s}{i}" for i in range(NCH) for s in ("u", "o")] + ["sq", "std"])
        pair_dve = Steps(sem("pair_dve"), ["gram0", "gram1", "bonus"] + [f"gram{i}" for i in range(2, NCH)] + [f"one{x}" for x in range(3)]
                         + [f"nm{lv}_{x}" for lv in LEVELS for x in range(3)]
                         + [f"{s}{i}" for i in range(NCH) for s in "xs" if (s, i) != ("s", NCH - 1)]
                         + ["cen", "var", "y"])
        vf_in, vf_out = sem("vf_in"), sem("vf_out")
        pair_pool = Steps(sem("pair_pool"), ["ar"] + [f"lv{lv}_{x}" for lv in LEVELS for x in range(3)])
        merge_pe = Steps(sem("merge_pe"), ["p0", "g0", "p1", "g1"])
        merge_act = Steps(sem("merge_act"), ["g0", "g1"])
        merge_dve = Steps(sem("merge_dve"), ["m0", "m1"])
        pool_pe = Steps(sem("pool_pe"), [f"p{j}" for j in range(8)] + [f"y{j}" for j in range(8)])
        pool_act = Steps(sem("pool_act"), [f"p{j}" for j in range(8)] + [f"y{j}" for j in range(8)])
        pool_dve = Steps(sem("pool_dve"), [f"p{j}" for j in range(8)])
        lat_pe = Steps(sem("lat_pe"), ["cq0", "cq1", "ckv", "kidx", "kr", "qsum", "kvsum", "mean", "var", "kperm",
                                       "rperm", "q0", "q1", "q2", "q3", "qp0", "qp1", "qp2", "qp3", "w"])
        lat_act = Steps(sem("lat_act"), ["cq0", "cq1", "ckv", "kidx", "kr", "sq", "std", "var", "std2",
                                         "q0", "q1", "q2", "q3", "w"])
        lat_dve = Steps(sem("lat_dve"), ["means", "latents", "center", "var", "kidx", "ropes", "rope0", "rope1",
                                         "rope2", "rope3"])
        IDX = [(i, hd) for i in range(1, NCH) for hd in range(8)]
        idx_pe = Steps(sem("idx_pe"), [f"s{i}_{hd}" for i, hd in IDX])
        idx_act = Steps(sem("idx_act"), [f"s{i}_{hd}" for i, hd in IDX])
        idx_dve = Steps(sem("idx_dve"), [f"s{i}_{hd}" for i, hd in IDX])
        att_pe = Steps(sem("att_pe"), [f"{s}{hd}" for hd in range(8) for s in
                                       ["q", "k", "v", "perm"]
                                       + [x for i in range(NCH + 2) for x in
                                          ([f"s{i}_"] if i < NCH else []) + ([f"pt{i - 1}_"] if 1 <= i <= NCH else [])
                                          + ([f"pv{i - 2}_"] if i >= 2 else [])]])
        att_act = Steps(sem("att_act"), [f"{s}{hd}" for hd in range(8) for s in
                                         ["q", "k", "v"]
                                         + [x for i in range(NCH + 2) for x in
                                            ([f"e{i}_"] if i < NCH else []) + ([f"pt{i - 1}_"] if 1 <= i <= NCH else [])
                                            + ([f"pv{i - 2}_"] if i >= 2 else [])]])
        att_dve = Steps(sem("att_dve"), ["kr"] + [f"{s}{hd}" for hd in range(8) for s in
                                         ["rope"] + [x for i in range(NCH + 1) for x in
                                                     ([f"m{i}_"] if i < NCH else []) + ([f"n{i - 1}_"] if i >= 1 else [])]])
        res_pe = Steps(sem("res_pe"), [f"o{s}" for s in range(4)])
        res_dve = Steps(sem("res_dve"), [f"h{s}" for s in range(4)])
        rt_pe = Steps(sem("rt_pe"), ["logits"] + [f"ut{i}" for i in range(NCH)] + ["oh", "start", "pos", "ct"]
                      + [f"su{j}" for j in range(KD)])
        rt_act = Steps(sem("rt_act"), ["ut0", "ut1", "ut2", "gexp", "ut3", "eexp", "ut4", "ut5", "pos", "ct"]
                       + [f"su{j}" for j in range(0, KD, 2)])
        rt_dve = Steps(sem("rt_dve"), ["gmax", "ediff", "oh", "rank", "pos", "take"] + [f"perm{i}" for i in range(NCH)]
                       + [f"su{j}" for j in range(1, KD, 2)])
        back_pe = Steps(sem("back_pe"), [f"yt{i}" for i in range(NCH)] + [f"h{j}" for j in range(KD)])
        back_act = Steps(sem("back_act"), [f"yt{i}" for i in range(NCH)])
        back_dve = Steps(sem("back_dve"), [f"h{j}" for j in range(KD)])
        grp_pe = Steps(sem("grp_pe"), [f"c{e}" for e in range(4)])
        grp_act = Steps(sem("grp_act"), [f"c{e}" for e in range(4)])
        grp_dve = Steps(sem("grp_dve"), [f"c{e}" for e in range(4)])
        exp_pe = Steps(sem("exp_pe"), ["a0", "b0", "a1", "b1"])
        exp_act = Steps(sem("exp_act"), ["t0", "t1"])
        exp_dve = Steps(sem("exp_dve"), ["h0", "h1"])
        dn_pe = Steps(sem("down_pe"), [f"o{s}" for s in range(4)])
        dn_dve = Steps(sem("down_dve"), [f"h{s}" for s in range(4)])
        out_ready = sem("out_ready")

        PE_STEPS = [norm_pe, low_pe, prep_pe, pair_pe, merge_pe, pool_pe, lat_pe, idx_pe, att_pe, res_pe, rt_pe, grp_pe,
                    exp_pe, dn_pe, back_pe]
        ACT_STEPS = [norm_act, low_act, prep_act, pair_act, merge_act, pool_act, lat_act, idx_act, att_act, rt_act, grp_act,
                     exp_act, back_act]
        DVE_STEPS = [norm_dve, low_dve, prep_dve, pair_dve, merge_dve, pool_dve, lat_dve, idx_dve, att_dve, res_dve, rt_dve,
                     grp_dve, exp_dve, dn_dve, back_dve]

        t = area()
        n_sq, n_rs = t(KD, T), t(T)
        t = area()
        lr_wa, lr_g, lr_v = t(T), t(T), t(T)
        raw_r, raw_k, raw_v = t(T + 1), t(T + 1), t(T + 1)
        pr, pk, pv = t(T), t(T), t(TP)
        tz, ta, tv, pg, pg_now = t(T), t(T), t(T), t(T), t(T)
        sqk, cum, kk, kh, bonus = t(T), t(T), t(T), t(T), t(T)
        G, Gi, Gx, vfb = t(T), t(T), t(T), t(T)
        ar = t(2, TP)
        bb, kb_ = t(TP), t(TP)
        arh = t(4, TP)
        tm = t(3, NCH * P, rows=CH)
        state, xs, us = t(P), t(P), t(P)
        gend = t(NCH - 1)
        gr = t(2 * NCH, 4 * CH, rows=CH)
        half_w0, half_a0, half_v0 = t(8), t(8), t(8)
        lv_t = t(2 * NCH, CH, rows=CH)
        pairs_o, otmp = t(T), t(T)
        area_m = area(m[:, :, :].rearrange("p a b -> p (a b)"))
        inv_t = area_m(2 * NCH, CH, rows=CH)
        inv = area_m(2 * NCH, CH, rows=CH)
        lv_a = area_m(2 * NCH, CH, rows=CH)
        lv_as = [lv_a[:, 4 * x:4 * x + 4, :] for x in range(3)]
        lv_ts = [lv_t[:, 4 * x:4 * x + 4, :] for x in range(3)]
        t = area()
        g_tanh, g_tmp = t(2, T), t(2, T)
        t = area()
        p_raw, p_a, p_b, pooled = t(2, T), t(T), t(T), t(KD, T)
        t = area()
        cq, ckv, kidx, kr = t(2, T), t(T), t(T), t(T)
        qi = t(4, T)
        wtok = t(NCH, 8, rows=CH)
        sel = t(sum(tile_keys(i) for i in range(NCH)), rows=CH)
        lat_mark = t
        l_sq, l_tmp, l_tmp2, l_rs, l_rs2 = t(3, T), t(T), t(T), t(T), t(T)
        score, score_w, relu_b, top8 = t(T, rows=CH), t(T, rows=CH), t(2, T, rows=CH), t(8, rows=CH)
        qh, kh2, vh = t(2, T, rows=96), t(2, T, rows=96), t(2, NCH * 64, rows=CH)
        es, pts = t(2, T, rows=CH), t(2, T, rows=CH)
        rope_t = t(T)
        mx, rs, ri = t(2, rows=CH), t(2, rows=CH), t(2, rows=CH)
        t = area()
        comb = t(NCH, 16, rows=CH)
        comb_t, comb_sel = t(T, rows=16), t(T, rows=16)
        comb_b, hid, e_tanh, e_tmp = t(4, T), t(8, T), t(2, T), t(2, T)
        lg = t(NCH, 20, rows=CH)
        r1, r2, r3, oh, oh1, oh2, ce = (t(NCH, 4, rows=CH) for _ in range(7))
        r16 = t(NCH, 16, rows=CH)
        s1, s2, s3, s4, s5 = (t(NCH, rows=CH) for _ in range(5))
        tok = t(NCH, D, rows=CH)
        take, give = t(NCH, T, rows=CH), t(NCH, T, rows=CH)
        place = t(T)
        place_tok = t(NCH, rows=CH)
        count1 = t(T)
        all1, oh_t, rank, place4 = t(T), t(T, rows=4), t(T, rows=4), t(T, rows=4)
        start4, start_row, most = t(1, rows=4), t(8, rows=1), t(1, rows=1)
        starts = ctx.enter_context(nc.sbuf_tensor("starts", [1, 4], mybir.dt.int32))
        fits = ctx.enter_context(nc.sbuf_tensor("fits", [1, 1], mybir.dt.int32))

        def sel_of(i):
            o = sum(tile_keys(k) for k in range(i))
            return sel[0:tile_rows(i), o:o + tile_keys(i)]

        def n_parts(i):
            return -(-tile_keys(i) // 512)

        def scores(b, i):
            n = n_parts(i)
            return ps[0:tile_rows(i), b:b + n, 0:tile_keys(i) // n]

        def parts(ap, i):
            return ap.rearrange("p (a b) -> p a b", a=n_parts(i))

        block = ctx.enter_context(nc.Block())

        @block.sync
        def _(sp):
            for j in range(KD):
                sp.dma_start(h[:, j, :], x_t[j]).then_inc(loaded, 16)
            for s in range(RING):
                sp.dma_start(ring[:, s, :], stream[s]).then_inc(w_full[s], 16)
            with sp.Fori(1, DEPTH * LAYER_ROUNDS) as n:
                for s in range(RING):
                    sp.wait_ge(w_free[s], n)
                    sp.dma_start(ring[:, s, :], stream[n * RING + s]).then_inc(w_full[s], 16)
            sp.wait_ge(out_ready, 1)
            for j in range(KD):
                sp.dma_start(out_t[j], u[:, j, N_META:]).then_inc(stored, 16)
            sp.wait_ge(stored, 16 * KD)

        @block.tensor
        def _(pe):
            mm = nc.tensor.matmul
            for S in PE_STEPS:
                pe.sem_inc(S.sem, len(S.names))

            def tile(s, rnd):
                pe.wait_ge(w_full[s], (rnd + 1) * 16)
                return ring[:, s, :]

            def project(s, rnd, src, bank, done, kbs=KD, free=True):
                w = tile(s, rnd)
                for kb in range(kbs):
                    for hf in range(2):
                        last = mm(ps[:, bank + hf, 0:HALF], w[:, kb * P:(kb + 1) * P],
                                  src[:, kb, hf * HALF:(hf + 1) * HALF], start=kb == 0, stop=kb == kbs - 1)
                    if kb == 0 and used:
                        last.then_inc(w_free[used.pop()], 1)
                last.then_inc(done, 1)
                used.append(s)

            def let_go():
                pe.drain().then_inc(w_free[used.pop()], 1)

            def release(s, rnd=None):
                if used:
                    let_go()
                if rnd is not None:
                    pe.wait_ge(w_full[s], (rnd + 1) * 16)
                    alone(pe)
                pe.drain().then_inc(w_free[s], 1)

            used = []

            def halves(lhsT, rhs, bank, rows=slice(0, P), start=True, stop=True):
                for hf in range(2):
                    last = mm(ps[rows, bank + hf, 0:HALF], lhsT, rhs[:, hf * HALF:(hf + 1) * HALF],
                              start=start, stop=stop)
                return last

            def norm(turn, n=KD):
                for j in range(n):
                    pe.wait_ge(norm_act.sem, norm_act.at(turn, f"sq{j}"))
                    last = halves(ones, n_sq[:, j, :], 0, start=j == 0, stop=j == n - 1)
                last.then_inc(norm_pe.inc("sum"), 1)

            pe.wait_ge(loaded, 16 * (KD + 1))
            with pe.Fori(0, DEPTH) as l:
                rnd0 = l * LAYER_ROUNDS
                norm(l * 2)
                next_phase(pe, "pe", l)

                rnd = rnd0 + FIRST["lowrank"]
                project(0, rnd, u, 0, low_pe.inc("wa"))
                project(1, rnd, u, 2, low_pe.inc("g"))
                project(2, rnd, u, 4, low_pe.inc("vres"))
                release(3, rnd)
                next_phase(pe, "pe", l)

                def prepare(turn, rnd, first, last):
                    A = prep_act
                    for n in range(first, last):
                        if n < 4:
                            name, rw, src, b, free = (("z", slice(0, 64), lr_wa, 6, None), ("a", slice(64, 128), lr_wa, 6, "z"),
                                                      ("g", slice(0, P), lr_g, 6, "a"), ("vres", slice(0, 32), lr_v, 6, "g"))[n]
                            if n == 0:
                                tile(0, rnd)
                            if free:
                                pe.wait_ge(A.sem, A.at(turn, free))
                            halves(ring[rw, 0, n * P:(n + 1) * P], src[rw, :], b).then_inc(prep_pe.inc(name), 1)
                            if n == 3:
                                used.append(0)
                            continue
                        k, kb = (n - 4) // 8, (n - 4) % 8
                        name, free = (("r", "vres"), ("k", "r"), ("v", "k"))[k]
                        if kb == 0:
                            pe.wait_ge(A.sem, A.at(turn, free))
                            tile(1 + k, rnd)
                        for hf in range(2):
                            mm_ = mm(ps[:, 6 + hf, 0:HALF], ring[:, 1 + k, kb * P:(kb + 1) * P],
                                     u[:, kb, hf * HALF:(hf + 1) * HALF], start=kb == 0, stop=kb == 7)
                            if kb == 0 and used:
                                mm_.then_inc(w_free[used.pop()], 1)
                        if kb == 7:
                            mm_.then_inc(prep_pe.inc(name), 1)
                            used.append(1 + k)

                def key_norm(turn):
                    pe.wait_ge(prep_act.sem, prep_act.at(turn, "sq"))
                    halves(headones, sqk, 4).then_inc(prep_pe.inc("kk"), 1)

                def pair(q, more):
                    it, rnd = l * NPAIR + q, rnd0 + FIRST["pairs"] + q
                    S, A, V = pair_pe, pair_act, pair_dve

                    def act_did(name):
                        pe.wait_ge(A.sem, A.at(it, name))

                    def dve_did(name):
                        pe.wait_ge(V.sem, V.at(it, name))

                    pe.wait_ge(prep_dve.sem, prep_dve.at(it, "rbk"))
                    def token_major(name, src, bank):
                        for i in range(NCH):
                            last = nc.tensor.transpose(ps[0:CH, bank + i // 4, (i % 4) * P:(i % 4 + 1) * P],
                                                       src[:, i * CH:(i + 1) * CH], ident)
                        last.then_inc(S.inc(name), 1)

                    token_major("tb", bb, 4)
                    pe.wait_ge(prep_act.sem, prep_act.at(it, "v"))
                    token_major("tk", kb_, 6)
                    pe.wait_ge(prep_pool.sem, prep_pool.at(it, "r"))
                    pe.wait_ge(prep_dve.sem, prep_dve.at(it, "a"))
                    for i in range(NCH):
                        if i == 2:
                            pe.wait_ge(V.sem, V.before(it, "var"))
                            pe.wait_ge(prep_dve.sem, prep_dve.at(it, "v"))
                            token_major("tv", pv, 2)
                            halves(headones, tz, 0).then_inc(S.inc("bonus"), 1)
                        if i < 3:
                            act_did(("tb", "tk", "tv")[i])
                        else:
                            dve_did("bonus" if i == 3 else f"gram{i - 4}")
                        b = GRAM_BANKS[i % 4]
                        cc = slice(i * CH, (i + 1) * CH)
                        for hd in range(2):
                            a_r = arh[:, 2 * hd:2 * hd + 2, cc]
                            mm(ps[0:CH, b + hd, 0:2 * CH], bb[:, cc], a_r, start=True, stop=True)
                            mm(ps[0:CH, b + hd, 2 * CH:4 * CH], kb_[:, cc], a_r, start=True, stop=True)
                            last = mm(ps[0:CH, b + hd, 4 * CH:5 * CH], arh[:, 2 * hd, cc], bb[:, cc], start=True, stop=True)
                        last.then_inc(S.inc(f"gram{i}"), 1)
                    gap_units = [0, 1, 2, 3, 4, 8, 12, 12, 16, 20, 20, 20, 20]

                    def fill(upto, first):
                        if more:
                            prepare(it + 1, rnd + 1, first, upto)

                    for n, lv in enumerate(LEVELS):
                        for x in range(3):
                            pe.wait_ge(pair_pool.sem, pair_pool.at(it, f"lv{lv}_{x}"))
                            dve_did(f"one{x}" if n == 0 else f"nm{LEVELS[n - 1]}_{x}")
                            if x == 2:
                                act_did(f"t{lv}_0")
                            for k in range(4):
                                last = mm(ps[0:CH, x % 2, k * CH:(k + 1) * CH], lv_as[x][:, k, :],
                                          inv[:, 4 * x + k, :], start=True, stop=True)
                            last.then_inc(S.inc(f"t{lv}_{x}"), 1)
                        fill(gap_units[2 * n + 1], gap_units[2 * n])
                        for x in range(3):
                            act_did(f"t{lv}_{x}")
                            if x != 1:
                                if x == 2:
                                    dve_did(f"nm{lv}_0")
                                elif n > 0:
                                    dve_did(f"nm{LEVELS[n - 1]}_2")
                            for k in range(4):
                                last = mm(ps[0:CH, 2 + x % 2, k * CH:(k + 1) * CH], lv_ts[x][:, k, :],
                                          inv_t[:, 4 * x + k, :], start=True, stop=True)
                            if lv != LEVELS[-1]:
                                for k in range(4):
                                    last = mm(ps[0:CH, 4 + x % 2, k * CH:(k + 1) * CH], inv_t[:, 4 * x + k, :],
                                              lv_ts[x][:, k, :], start=True, stop=True)
                            last.then_inc(S.inc(f"nm{lv}_{x}"), 1)
                        fill(gap_units[2 * n + 2], gap_units[2 * n + 1])
                    for i in range(NCH):
                        cc = slice(i * CH, (i + 1) * CH)
                        tmv = tm[:, 2, i * P:(i + 1) * P]
                        dve_did(f"nm{LEVELS[-1]}_2" if i == 0 else f"s{i - 1}")
                        mm(ps[0:CH, 0, 0:P], ar[:, 0, cc], state, start=True, stop=False, skip_group_check=True)
                        for hd in range(2):
                            last = mm(ps[0:CH, 0, 64 * hd:64 * hd + 64], gr[:, 2 * i + hd, 2 * CH:3 * CH],
                                      tmv[:, 64 * hd:64 * hd + 64], start=False, stop=hd == 1, skip_group_check=True)
                        last.then_inc(S.inc(f"x{i}"), 1)
                        if i == 0 and more:
                            key_norm(it + 1)
                        elif i < NCH - 1:
                            fill(20 + 2 * i, 18 + 2 * i)
                        dve_did(f"x{i}")
                        for hd in range(2):
                            last = mm(ps[0:CH, 1, 64 * hd:64 * hd + 64], inv_t[:, 2 * i + hd, :],
                                      xs[0:CH, 64 * hd:64 * hd + 64], start=True, stop=True)
                        last.then_inc(S.inc(f"u{i}"), 1)
                        act_did(f"u{i}")
                        if i >= 1:
                            act_did(f"o{i - 1}")
                        tr = tile_rows(i)
                        c2 = slice(i * CH, i * CH + tr)
                        mm(ps[:, 2, 0:tr], state, ar[:, 1, c2], start=True, stop=False, skip_group_check=True)
                        for hd in range(2):
                            rw = slice(64 * hd, 64 * hd + 64)
                            mm(ps[rw, 2, 0:tr], us[0:CH, rw], gr[:, 2 * i + hd, CH:CH + tr],
                               start=False, stop=False, skip_group_check=True)
                            last = mm(ps[rw, 2, 0:tr], tmv[:, rw], gr[:, 2 * i + hd, 3 * CH:3 * CH + tr],
                                      start=False, stop=True, skip_group_check=True)
                        last.then_inc(S.inc(f"o{i}"), 1)
                        if i < NCH - 1:
                            mm(ps[:, 3, 0:P], tm[:, 0, i * P:(i + 1) * P], us[0:CH, :], start=True, stop=False)
                            mm(ps[:, 3, 0:P], tm[:, 1, i * P:(i + 1) * P], tmv, start=False, stop=True
                               ).then_inc(S.inc(f"d{i}"), 1)
                    act_did(f"o{NCH - 1}")
                    halves(headones, pairs_o, 0).then_inc(S.inc("mean"), 1)
                    if more:
                        let_go()
                    act_did("sq")
                    halves(headones, otmp, 2).then_inc(S.inc("var"), 1)

                rnd = rnd0 + FIRST["pairs"]
                prepare(l * NPAIR, rnd, 0, 20)
                key_norm(l * NPAIR)
                prepare(l * NPAIR, rnd, 20, 28)
                let_go()
                with pe.Fori(0, NPAIR - 1) as q:
                    pair(q, True)
                pair(NPAIR - 1, False)
                next_phase(pe, "pe", l)

                def merge(phase, k):
                    with pe.Fori(0, 4) as q:
                        it, rnd = l * 12 + 4 * k + q, rnd0 + FIRST[phase] + q
                        for n in range(2):
                            pe.wait_ge(merge_dve.sem, merge_dve.before(it, f"m{n}"))
                            project(2 * n, rnd, y, 4 * n, merge_pe.inc(f"p{n}"))
                            project(2 * n + 1, rnd, u, 4 * n + 2, merge_pe.inc(f"g{n}"))
                        let_go()
                    next_phase(pe, "pe", l)

                merge("merge_b", 0)

                for j in range(8):
                    if j >= 4:
                        pe.wait_ge(pool_act.sem, pool_act.at(l, f"p{j - 4}"))
                    project(j % 4, rnd0 + FIRST["pool"] + j // 4, u, 2 * (j % 4), pool_pe.inc(f"p{j}"))
                let_go()
                rnd = rnd0 + FIRST["pool"] + 2
                for j in range(8):
                    g, nb = j // 2, j % 2
                    w = tile(g // 2, rnd)
                    pe.wait_ge(pool_act.sem, pool_act.at(l, f"p{j + 4}" if j < 4 else f"y{j - 4}"))
                    for kb in range(2):
                        pe.wait_ge(pool_dve.sem, pool_dve.at(l, f"p{2 * g + kb}"))
                        blk = (g % 2) * 4 + nb * 2 + kb
                        last = halves(w[:, blk * P:(blk + 1) * P], pooled[:, 2 * g + kb, :], 2 * (j % 4),
                                      start=kb == 0, stop=kb == 1)
                    last.then_inc(pool_pe.inc(f"y{j}"), 1)
                    if j in (3, 7):
                        release(j // 4)
                release(2, rnd)
                release(3, rnd)
                next_phase(pe, "pe", l)
                merge("merge_a", 1)

                S, A, V = lat_pe, lat_act, lat_dve

                def act_did(name):
                    pe.wait_ge(A.sem, A.at(l, name))

                def dve_did(name):
                    pe.wait_ge(V.sem, V.at(l, name))

                rnd = rnd0 + FIRST["dsa_in"]
                for s, name in enumerate(("cq0", "cq1", "ckv", "kidx")):
                    project(s, rnd, u, 2 * s, S.inc(name))
                act_did("cq0")
                project(0, rnd + 1, u, 0, S.inc("kr"))
                let_go()
                act_did("sq")
                act_did("cq1")
                halves(ones, l_sq[:, 0, :], 2, start=True, stop=False)
                halves(ones, l_sq[:, 1, :], 2, start=False, stop=True).then_inc(S.inc("qsum"), 1)
                act_did("ckv")
                halves(ones, l_sq[:, 2, :], 4).then_inc(S.inc("kvsum"), 1)
                act_did("kidx")
                halves(headones, kidx, 6).then_inc(S.inc("mean"), 1)
                act_did("var")
                halves(headones, l_sq[:, 0, :], 6).then_inc(S.inc("var"), 1)
                dve_did("kidx")
                halves(perm, kidx, 2).then_inc(S.inc("kperm"), 1)
                act_did("kr")
                halves(perm, kr, 4).then_inc(S.inc("rperm"), 1)
                w = tile(1, rnd + 1)
                for j in range(4):
                    dve_did("ropes")
                    b = 2 * j
                    for kb in range(2):
                        blk = 2 * j + kb
                        last = halves(w[:, blk * P:(blk + 1) * P], cq[:, kb, :], b, start=kb == 0, stop=kb == 1)
                    last.then_inc(S.inc(f"q{j}"), 1)
                release(1)
                release(2, rnd + 1)
                release(3, rnd + 1)
                for j in range(4):
                    act_did(f"q{j}")
                    halves(perm, qi[:, j, :], 2 * j).then_inc(S.inc(f"qp{j}"), 1)
                dve_did("rope0")
                alone(pe)
                for i in range(NCH):
                    last = nc.tensor.transpose(ps[0:tile_rows(i), 0, i * 8:(i + 1) * 8],
                                               kr[96:104, i * CH:tile_keys(i)], ident[96:104, 96:104])
                last.then_inc(S.inc("w"), 1)
                next_phase(pe, "pe", l)

                for n, (i, hd) in enumerate(IDX):
                    if n >= 4:
                        j, g = IDX[n - 4]
                        pe.wait_ge(idx_act.sem, idx_act.at(l, f"s{j}_{g}"))
                        if tile_rows(i) < CH:
                            alone(pe)
                    rw = slice(64 * (hd % 2), 64 * (hd % 2) + 64)
                    b = 2 * (n % 4)
                    wd = tile_keys(i) // n_parts(i)
                    for k in range(n_parts(i)):
                        last = mm(ps[0:tile_rows(i), b + k, 0:wd], qi[rw, hd // 2, i * CH:tile_keys(i)],
                                  kidx[rw, k * wd:(k + 1) * wd], start=True, stop=True)
                    last.then_inc(idx_pe.inc(f"s{i}_{hd}"), 1)
                next_phase(pe, "pe", l)

                with pe.Fori(0, 2) as q:
                    it, rnd = l * 2 + q, rnd0 + FIRST["heads"] + q
                    S, A, V = att_pe, att_act, att_dve

                    def act_did(name):
                        pe.wait_ge(A.sem, A.at(it, name))

                    def dve_did(name):
                        pe.wait_ge(V.sem, V.at(it, name))

                    for hd in range(8):
                        b4, hh, z = hd // 4, hd % 4, hd % 2
                        wq, wkv = tile(2 * b4, rnd), tile(2 * b4 + 1, rnd)
                        if hd == 0:
                            pe.wait_ge(A.sem, A.before(it, "pv5_7"))
                            pe.wait_ge(V.sem, V.before(it, "m5_7"))
                        else:
                            act_did(f"pv5_{hd - 1}")
                            dve_did(f"m5_{hd - 1}")
                        for kb in range(2):
                            blk = 2 * hh + kb
                            last = halves(wq[:, blk * P:blk * P + 96], cq[:, kb, :], 0, rows=slice(0, 96),
                                          start=kb == 0, stop=kb == 1)
                        last.then_inc(S.inc(f"q{hd}"), 1)
                        halves(wkv[:, hh * 64:hh * 64 + 64], ckv, 2, rows=slice(0, 64)).then_inc(S.inc(f"k{hd}"), 1)
                        for i in range(NCH):
                            last = mm(ps[0:tile_rows(i), 4, i * 64:i * 64 + 64], ckv[:, i * CH:tile_keys(i)],
                                      wkv[:, 256 + hh * 64:256 + hh * 64 + 64], start=True, stop=True)
                        last.then_inc(S.inc(f"v{hd}"), 1)
                        if hh == 3:
                            release(2 * b4)
                            release(2 * b4 + 1)
                        act_did(f"q{hd}")
                        alone(pe)
                        halves(perm[64:96, 64:96], qh[64:96, z, :], 6, rows=slice(64, 96)
                               ).then_inc(S.inc(f"perm{hd}"), 1)
                        dve_did(f"rope{hd}")
                        act_did(f"v{hd}")
                        for step in range(NCH + 2):
                            if step < NCH:
                                i = step
                                if i >= 2:
                                    dve_did(f"m{i - 2}_{hd}")
                                wd = tile_keys(i) // n_parts(i)
                                for k in range(n_parts(i)):
                                    last = mm(ps[0:tile_rows(i), 2 * (i % 2) + k, 0:wd], qh[:, z, i * CH:tile_keys(i)],
                                              kh2[:, z, k * wd:(k + 1) * wd], start=True, stop=True)
                                last.then_inc(S.inc(f"s{i}_{hd}"), 1)
                            if 1 <= step <= NCH:
                                i = step - 1
                                dve_did(f"n{i}_{hd}")
                                if i >= 2:
                                    act_did(f"pv{i - 2}_{hd}")
                                b, tr = 4 + 2 * (i % 2), tile_rows(i)
                                if tr < CH:
                                    alone(pe)
                                for k in range(i + 1):
                                    last = nc.tensor.transpose(ps[0:tile_rows(k), b, k * tr:(k + 1) * tr],
                                                               es[0:tr, i % 2, k * CH:tile_keys(k)],
                                                               ident[0:tr, 0:tr])
                                last.then_inc(S.inc(f"pt{i}_{hd}"), 1)
                            if step >= 2:
                                i = step - 2
                                act_did(f"pt{i}_{hd}")
                                rw = slice(64 * z, 64 * z + 64)
                                b, tr = 5 + 2 * (i % 2), tile_rows(i)
                                for k in range(i + 1):
                                    last = mm(ps[rw, b, 0:tr], vh[0:tile_rows(k), z, k * 64:k * 64 + 64],
                                              pts[0:tile_rows(k), i % 2, k * tr:(k + 1) * tr], start=k == 0, stop=k == i)
                                last.then_inc(S.inc(f"pv{i}_{hd}"), 1)
                next_phase(pe, "pe", l)
                merge("merge_c", 2)

                with pe.Fori(0, 2) as q:
                    it, rnd = l * 2 + q, rnd0 + FIRST["out"] + q
                    for s in range(4):
                        pe.wait_ge(res_dve.sem, res_dve.before(it, f"h{s}"))
                        project(s, rnd, m, 2 * s, res_pe.inc(f"o{s}"))
                    let_go()
                next_phase(pe, "pe", l)
                norm(l * 2 + 1)
                next_phase(pe, "pe", l)

                S, A, V = rt_pe, rt_act, rt_dve

                def act_did(name):
                    pe.wait_ge(A.sem, A.at(l, name))

                def dve_did(name):
                    pe.wait_ge(V.sem, V.at(l, name))

                o = PARAMS["router"][0]
                for i in range(NCH):
                    for kb in range(KD):
                        last = mm(ps[0:CH, 0, i * 20:i * 20 + 20], u[:, kb, window(i):window(i) + CH],
                                  par[:, o + kb * 20:o + kb * 20 + 20], start=kb == 0, stop=kb == KD - 1)
                last.then_inc(S.inc("logits"), 1)
                for i in range(NCH):
                    if i >= 3:
                        act_did(f"ut{i - 3}")
                    for j in range(KD):
                        last = nc.tensor.transpose(ps[0:CH, 2 + 2 * (i % 3) + j // 4, (j % 4) * P:(j % 4 + 1) * P],
                                                   u[:, j, window(i):window(i) + CH], ident)
                    last.then_inc(S.inc(f"ut{i}"), 1)
                dve_did("oh")
                for i in range(NCH):
                    last = nc.tensor.transpose(ps[0:4, i // 5, (i % 5) * CH:(i % 5 + 1) * CH], oh[:, i, :],
                                               ident[0:CH, 0:CH])
                last.then_inc(S.inc("oh"), 1)
                dve_did("rank")
                alone(pe)
                below = c("grams", 4)[:, 0:4]
                mm(ps[0:4, 0, 0:1], below, rank[:, T - 1:T], start=True, stop=True)
                mm(ps[0:1, 0, 4:8], rank[:, T - 1:T], below, start=True, stop=True)
                mm(ps[0:1, 0, 8:12], rank[:, T - 1:T], ident[0:4, 0:4], start=True, stop=True
                   ).then_inc(S.inc("start"), 1)
                dve_did("pos")
                act_did("ut3")
                alone(pe)
                halves(ones[0:4, :], place4, 2)
                for i in range(NCH):
                    last = mm(ps[0:CH, 1, i:i + 1], place4[:, window(i):window(i) + CH], ones[0:4, 0:1],
                              start=True, stop=True)
                last.then_inc(S.inc("pos"), 1)
                act_did("ut4")
                for i in range(NCH):
                    dve_did(f"perm{i}")
                    last = halves(comb[:, i, :], take[:, i, :], 4, rows=slice(0, 16), start=i == 0, stop=i == NCH - 1)
                last.then_inc(S.inc("ct"), 1)
                for j in range(KD):
                    if j < 4:
                        act_did(("ut5", "ut5", "pos", "ct")[j])
                    elif j % 2 == 0:
                        act_did(f"su{j - 4}")
                    else:
                        dve_did(f"su{j - 4}")
                    for i in range(NCH):
                        last = halves(tok[:, i, j * P:(j + 1) * P], take[:, i, :], (6, 0, 2, 4)[j % 4],
                                      start=i == 0, stop=i == NCH - 1)
                    last.then_inc(S.inc(f"su{j}"), 1)
                next_phase(pe, "pe", l)

                def experts(all_columns):
                    def product(s, rnd, src, off, bank, done):
                        if all_columns:
                            project(s, rnd, src, bank, done)
                            return
                        w = tile(s, rnd)
                        alone(pe)
                        for kb in range(KD):
                            last = mm(ps[:, bank, 0:GROUP_COLS], w[:, kb * P:(kb + 1) * P],
                                      src[:, kb, ds(off, GROUP_COLS)] if off is not None else src[:, kb, 0:GROUP_COLS],
                                      start=kb == 0, stop=kb == KD - 1)
                            if kb == 0 and used:
                                last.then_inc(w_free[used.pop()], 1)
                        last.then_inc(done, 1)
                        used.append(s)

                    with pe.Fori(0, 4) as g:
                        gi = l * 4 + g
                        off = None if all_columns else pe.value_load(starts[0:1, ds(g, 1)], min_val=0,
                                                                     max_val=T - GROUP_COLS)
                        for e in range(4):
                            pe.wait_ge(grp_dve.sem, grp_dve.at(gi, f"c{e}"))
                            if e == 0:
                                pe.wait_ge(dn_dve.sem, dn_dve.before(gi * 2, "h3"))
                            if all_columns:
                                last = halves(ones[0:16, :], comb_sel, 2 * e)
                            else:
                                last = mm(ps[:, 2 * e, 0:GROUP_COLS], ones[0:16, :], comb_sel[:, 0:GROUP_COLS],
                                          start=True, stop=True)
                            last.then_inc(grp_pe.inc(f"c{e}"), 1)
                            pe.wait_ge(grp_act.sem, grp_act.at(gi, f"c{e}"))
                        alone(pe)
                        with pe.Fori(0, 4) as e:
                            it, rnd = gi * 4 + e, rnd0 + FIRST["moe"] + g * 6 + e
                            for n in range(2):
                                pe.wait_ge(exp_dve.sem, exp_dve.before(it, f"h{n}"))
                                product(2 * n, rnd, u, off, 4 * n, exp_pe.inc(f"a{n}"))
                                product(2 * n + 1, rnd, u, off, 4 * n + 2, exp_pe.inc(f"b{n}"))
                            let_go()
                        pe.wait_ge(exp_dve.sem, exp_dve.at(gi * 4 + 3, "h1"))
                        alone(pe)
                        with pe.Fori(0, 2) as q:
                            it, rnd = gi * 2 + q, rnd0 + FIRST["moe"] + g * 6 + 4 + q
                            for s in range(4):
                                pe.wait_ge(dn_dve.sem, dn_dve.before(it, f"h{s}"))
                                product(s, rnd, hid, None, 2 * s, dn_pe.inc(f"o{s}"))
                            let_go()

                with pe.If(pe.value_load(fits[0:1, 0:1], min_val=0, max_val=1)):
                    experts(False)
                with pe.Else():
                    experts(True)
                next_phase(pe, "pe", l)

                for i in range(NCH):
                    if i >= 4:
                        pe.wait_ge(back_act.sem, back_act.at(l, f"yt{i - 4}"))
                        alone(pe)
                    tr = tile_rows(i)
                    for j in range(KD):
                        last = nc.tensor.transpose(ps[0:tr, 2 * (i % 4) + j // 4, (j % 4) * P:(j % 4 + 1) * P],
                                                   y[:, j, i * CH:i * CH + tr], ident)
                    last.then_inc(back_pe.inc(f"yt{i}"), 1)
                for j in range(KD):
                    if j < 4:
                        pe.wait_ge(back_act.sem, back_act.at(l, f"yt{NCH - 1}"))
                    else:
                        pe.wait_ge(back_dve.sem, back_dve.at(l, f"h{j - 4}"))
                    for i in range(NCH):
                        tr = tile_rows(i)
                        last = halves(tok[0:tr, i, j * P:(j + 1) * P], give[0:tr, i, :], 2 * (j % 4),
                                      start=i == 0, stop=i == NCH - 1)
                    last.then_inc(back_pe.inc(f"h{j}"), 1)
                next_phase(pe, "pe", l)
            norm(DEPTH * 2)

        @block.scalar
        def _(act):
            A_ = nc.scalar.activation
            act.dma_start(cst[:, :], consts).then_inc(loaded, 16)
            for S in ACT_STEPS:
                act.sem_inc(S.sem, len(S.names))
            act.wait_ge(loaded, 16 * (KD + 1))

            def norm(turn):
                for j in range(KD):
                    A_(n_sq[:, j, :], h[:, j, :], ACT.Square).then_inc(norm_act.inc(f"sq{j}"), 1)
                act.wait_ge(norm_dve.sem, norm_dve.at(turn, "mean"))
                A_(n_rs, n_rs, ACT.Sqrt).then_inc(norm_act.inc("sqrt"), 1)

            with act.Fori(0, DEPTH) as l:
                act.dma_start(par[:, :], params[l]).then_inc(par_full, 16)
                norm(l * 2)
                next_phase(act, "act", l)

                for name, dst, b in (("wa", raw_r, 0), ("g", raw_k, 2), ("vres", raw_v, 4)):
                    act.wait_ge(low_pe.sem, low_pe.at(l, name))
                    A_(two(dst[:, 1:]), acc(b), ACT.Copy).then_inc(low_act.inc(name), 1)
                act.wait_ge(low_dve.sem, low_dve.at(l, "shift"))
                A_(lr_wa[0:64, :], lr_wa[0:64, :], ACT.Tanh)
                A_(lr_g, lr_g, ACT.Tanh, scale=0.5).then_inc(low_act.inc("tanh"), 1)
                next_phase(act, "act", l)

                def evacuate(turn, q, *names):
                    for name in names:
                        act.wait_ge(prep_pe.sem, prep_pe.at(turn, name))
                        if name == "z":
                            last = A_(two(tz), acc(6), ACT.Tanh, bias=col(half_w0, q), scale=0.5)
                        elif name == "a":
                            last = A_(two(ta), acc(6), ACT.Tanh, bias=col(half_a0, q), scale=0.5)
                        elif name == "vres":
                            last = A_(two(tv), acc(6), ACT.Tanh, bias=col(half_v0, q), scale=0.5)
                        else:
                            dst = {"g": pg, "r": raw_r[:, 1:], "k": raw_k[:, 1:], "v": raw_v[:, 1:]}[name]
                            last = A_(two(dst), acc(6), ACT.Copy)
                        last.then_inc(prep_act.inc(name), 1)

                def decays(turn):
                    act.wait_ge(prep_dve.sem, prep_dve.at(turn, "c"))
                    A_(G, cum, ACT.Exp)
                    A_(Gi, cum, ACT.Exp, scale=-1.0)
                    A_(Gx, Gx, ACT.Exp).then_inc(prep_act.inc("G"), 1)

                def key_squares(turn):
                    act.wait_ge(prep_dve.sem, prep_dve.at(turn, "kk"))
                    A_(sqk, kk, ACT.Square).then_inc(prep_act.inc("sq"), 1)

                def key_norm(turn):
                    act.wait_ge(prep_dve.sem, prep_dve.at(turn, "kkmax"))
                    A_(sqk, sqk, ACT.Sqrt).then_inc(prep_act.inc("norm"), 1)

                def pair(q, more):
                    it = l * NPAIR + q
                    S, E, V = pair_act, pair_pe, pair_dve

                    def pe_did(name):
                        act.wait_ge(E.sem, E.at(it, name))

                    for k, (name, b) in enumerate((("tb", 4), ("tk", 6), ("tv", 2))):
                        pe_did(name)
                        A_(tm[:, k, 0:4 * P], ps[0:CH, b, 0:4 * P], ACT.Copy)
                        A_(tm[:, k, 4 * P:6 * P], ps[0:CH, b + 1, 0:2 * P], ACT.Copy).then_inc(S.inc(name), 1)
                    for lv in LEVELS:
                        if more:
                            evacuate(it + 1, q + 1, *{4: ("a",), 8: ("vres",)}.get(lv, ()))
                        for x in range(3):
                            pe_did(f"t{lv}_{x}")
                            A_(lv_ts[x], ps[0:CH, x % 2, 0:4 * CH].rearrange("p (a b) -> p a b", a=4), ACT.Copy
                               ).then_inc(S.inc(f"t{lv}_{x}"), 1)
                        if more:
                            if lv == 8:
                                decays(it + 1)
                            evacuate(it + 1, q + 1, *{2: ("z",), 4: ("g",), 16: ("r",), 32: ("k",)}.get(lv, ()))
                    if more:
                        key_squares(it + 1)
                    for i in range(NCH):
                        pe_did(f"u{i}")
                        if i >= 1:
                            pe_did(f"d{i - 1}")
                        A_(us[0:CH, :], ps[0:CH, 1, 0:P], ACT.Copy).then_inc(S.inc(f"u{i}"), 1)
                        pe_did(f"o{i}")
                        tr = tile_rows(i)
                        A_(pairs_o[:, i * CH:i * CH + tr], ps[:, 2, 0:tr], ACT.Copy).then_inc(S.inc(f"o{i}"), 1)
                        if more and i == 1:
                            key_norm(it + 1)
                        if more and i == NCH - 2:
                            evacuate(it + 1, q + 1, "v")
                    act.wait_ge(V.sem, V.at(it, "cen"))
                    A_(otmp, pairs_o, ACT.Square).then_inc(S.inc("sq"), 1)
                    act.wait_ge(V.sem, V.at(it, "var"))
                    A_(otmp, otmp, ACT.Sqrt).then_inc(S.inc("std"), 1)

                def col(ap, q):
                    return ap[:, q:q + 1] if isinstance(q, int) else ap[:, ds(q, 1)]

                evacuate(l * NPAIR, 0, "z", "a", "g", "vres")
                decays(l * NPAIR)
                evacuate(l * NPAIR, 0, "r", "k")
                key_squares(l * NPAIR)
                key_norm(l * NPAIR)
                evacuate(l * NPAIR, 0, "v")
                with act.Fori(0, NPAIR - 1) as q:
                    pair(q, True)
                pair(NPAIR - 1, False)
                next_phase(act, "act", l)

                def merge(k):
                    with act.Fori(0, 4) as q:
                        it = l * 12 + 4 * k + q
                        for n in range(2):
                            act.wait_ge(merge_dve.sem, merge_dve.before(it, f"m{n}"))
                            act.wait_ge(merge_pe.sem, merge_pe.at(it, f"g{n}"))
                            A_(two(g_tanh[:, n, :]), acc(4 * n + 2), ACT.Tanh, scale=0.5
                               ).then_inc(merge_act.inc(f"g{n}"), 1)
                    next_phase(act, "act", l)

                merge(0)
                for j in range(8):
                    act.wait_ge(pool_pe.sem, pool_pe.at(l, f"p{j}"))
                    if j >= 2:
                        act.wait_ge(pool_dve.sem, pool_dve.at(l, f"p{j - 2}"))
                    A_(two(p_raw[:, j % 2, :]), acc(2 * (j % 4)), ACT.Copy).then_inc(pool_act.inc(f"p{j}"), 1)
                for j in range(8):
                    act.wait_ge(pool_pe.sem, pool_pe.at(l, f"y{j}"))
                    A_(two(y[:, j, :]), acc(2 * (j % 4)), ACT.Copy, scale=pc("pool_scale", j)
                       ).then_inc(pool_act.inc(f"y{j}"), 1)
                next_phase(act, "act", l)
                merge(1)

                def pe_did(name):
                    act.wait_ge(lat_pe.sem, lat_pe.at(l, name))

                def dve_did(name):
                    act.wait_ge(lat_dve.sem, lat_dve.at(l, name))
                S = lat_act
                for name, dst, b in (("cq0", cq[:, 0, :], 0), ("cq1", cq[:, 1, :], 2), ("ckv", ckv, 4),
                                     ("kidx", kidx, 6), ("kr", kr, 0)):
                    pe_did(name)
                    A_(two(dst), acc(b), ACT.Copy).then_inc(S.inc(name), 1)
                act.drain()
                A_(l_sq[:, 0:2, :], cq, ACT.Square)
                A_(l_sq[:, 2, :], ckv, ACT.Square).then_inc(S.inc("sq"), 1)
                dve_did("means")
                A_(l_rs, l_rs, ACT.Sqrt)
                A_(l_rs2, l_rs2, ACT.Sqrt).then_inc(S.inc("std"), 1)
                dve_did("center")
                pe_did("qsum")
                A_(l_sq[:, 0, :], kidx, ACT.Square).then_inc(S.inc("var"), 1)
                dve_did("var")
                A_(l_tmp, l_tmp, ACT.Sqrt).then_inc(S.inc("std2"), 1)
                for j in range(4):
                    pe_did(f"q{j}")
                    A_(two(qi[:, j, :]), acc(2 * j), ACT.Copy).then_inc(S.inc(f"q{j}"), 1)
                pe_did("w")
                A_(wtok[:, 0:NCH - 1, :], ps[0:CH, 0, 0:8 * (NCH - 1)].rearrange("p (a b) -> p a b", a=NCH - 1),
                   ACT.Copy, scale=IDX_SCALE)
                tr = tile_rows(NCH - 1)
                A_(wtok[0:tr, NCH - 1, :], ps[0:tr, 0, 8 * (NCH - 1):8 * NCH], ACT.Copy, scale=IDX_SCALE
                   ).then_inc(S.inc("w"), 1)
                next_phase(act, "act", l)

                for n, (i, hd) in enumerate(IDX):
                    act.wait_ge(idx_pe.sem, idx_pe.at(l, f"s{i}_{hd}"))
                    if n >= 2:
                        j, g = IDX[n - 2]
                        act.wait_ge(idx_dve.sem, idx_dve.at(l, f"s{j}_{g}"))
                    b, z, wd = 2 * (n % 4), n % 2, tile_keys(i)
                    A_(parts(relu_b[0:tile_rows(i), z, 0:wd], i), scores(b, i), ACT.Relu).then_inc(idx_act.inc(f"s{i}_{hd}"), 1)
                next_phase(act, "act", l)

                with act.Fori(0, 2) as q:
                    it = l * 2 + q
                    S = att_act

                    def pe_did(name):
                        act.wait_ge(att_pe.sem, att_pe.at(it, name))

                    def dve_did(name):
                        act.wait_ge(att_dve.sem, att_dve.at(it, name))

                    for hd in range(8):
                        z = hd % 2
                        pe_did(f"q{hd}")
                        A_(two(qh[:, z, :]), acc(0, slice(0, 96)), ACT.Copy).then_inc(S.inc(f"q{hd}"), 1)
                        pe_did(f"k{hd}")
                        A_(two(kh2[0:64, z, :]), acc(2, slice(0, 64)), ACT.Copy).then_inc(S.inc(f"k{hd}"), 1)
                        pe_did(f"v{hd}")
                        A_(vh[:, z, 0:(NCH - 1) * 64], ps[0:CH, 4, 0:(NCH - 1) * 64], ACT.Copy)
                        tr = tile_rows(NCH - 1)
                        A_(vh[0:tr, z, (NCH - 1) * 64:NCH * 64], ps[0:tr, 4, (NCH - 1) * 64:NCH * 64], ACT.Copy
                           ).then_inc(S.inc(f"v{hd}"), 1)
                        for step in range(NCH + 2):
                            if step < NCH:
                                i = step
                                wd, tr, k = tile_keys(i), tile_rows(i), i % 2
                                dve_did(f"m{i}_{hd}")
                                A_(es[0:tr, k, 0:wd], es[0:tr, k, 0:wd], ACT.Exp, bias=mx[0:tr, k:k + 1],
                                   scale=ATT_SCALE, accum_out=rs[0:tr, k:k + 1]).then_inc(S.inc(f"e{i}_{hd}"), 1)
                            if 1 <= step <= NCH:
                                i = step - 1
                                b, tr = 4 + 2 * (i % 2), tile_rows(i)
                                wd = min(i + 1, NCH - 1) * tr
                                pe_did(f"pt{i}_{hd}")
                                last = A_(pts[:, i % 2, 0:wd], ps[0:CH, b, 0:wd], ACT.Copy)
                                if i == NCH - 1:
                                    last = A_(pts[0:tr, i % 2, wd:wd + tr], ps[0:tr, b, wd:wd + tr], ACT.Copy)
                                last.then_inc(S.inc(f"pt{i}_{hd}"), 1)
                            if step >= 2:
                                i = step - 2
                                b, tr = 5 + 2 * (i % 2), tile_rows(i)
                                rw = slice(64 * z, 64 * z + 64)
                                pe_did(f"pv{i}_{hd}")
                                A_(y[rw, ds(q * 4 + hd // 2, 1), i * CH:tile_keys(i)],
                                   ps[rw, b:b + 1, 0:tr], ACT.Copy).then_inc(S.inc(f"pv{i}_{hd}"), 1)
                next_phase(act, "act", l)
                merge(2)
                next_phase(act, "act", l)
                norm(l * 2 + 1)
                next_phase(act, "act", l)

                S = rt_act

                def rows_out(i, tr, pe_steps, steps):
                    b = (2 + 2 * (i % 3)) if steps is rt_act else 2 * (i % 4)
                    name = ("ut" if steps is rt_act else "yt") + str(i)
                    act.wait_ge(pe_steps.sem, pe_steps.at(l, name))
                    A_(tok[0:tr, i, :].rearrange("p (a b) -> p a b", a=2), ps[0:tr, b:b + 2, :], ACT.Copy
                       ).then_inc(steps.inc(name), 1)

                for i in range(3):
                    rows_out(i, CH, rt_pe, rt_act)
                act.wait_ge(rt_dve.sem, rt_dve.at(l, "gmax"))
                A_(r1, r1, ACT.Exp).then_inc(S.inc("gexp"), 1)
                rows_out(3, CH, rt_pe, rt_act)
                act.wait_ge(rt_dve.sem, rt_dve.at(l, "ediff"))
                A_(s4, s4, ACT.Exp).then_inc(S.inc("eexp"), 1)
                rows_out(4, CH, rt_pe, rt_act)
                rows_out(5, CH, rt_pe, rt_act)
                act.wait_ge(rt_pe.sem, rt_pe.at(l, "pos"))
                A_(two(place), acc(2), ACT.Copy).then_inc(S.inc("pos"), 1)
                act.wait_ge(rt_pe.sem, rt_pe.at(l, "ct"))
                A_(two(comb_t), acc(4, slice(0, 16)), ACT.Copy).then_inc(S.inc("ct"), 1)
                for j in range(0, KD, 2):
                    act.wait_ge(rt_pe.sem, rt_pe.at(l, f"su{j}"))
                    A_(two(u[:, j, :]), acc((6, 0, 2, 4)[j % 4]), ACT.Copy).then_inc(S.inc(f"su{j}"), 1)
                next_phase(act, "act", l)

                def experts(all_columns):
                    def out(x):
                        return two(x) if all_columns else x[:, 0:GROUP_COLS]

                    def bank(b):
                        return acc(b) if all_columns else ps[:, b, 0:GROUP_COLS]

                    with act.Fori(0, 4) as g:
                        gi = l * 4 + g
                        for e in range(4):
                            act.wait_ge(grp_pe.sem, grp_pe.at(gi, f"c{e}"))
                            A_(out(comb_b[:, e, :]), bank(2 * e), ACT.Copy).then_inc(grp_act.inc(f"c{e}"), 1)
                        with act.Fori(0, 4) as e:
                            it = gi * 4 + e
                            for n in range(2):
                                act.wait_ge(exp_pe.sem, exp_pe.at(it, f"a{n}"))
                                act.wait_ge(exp_dve.sem, exp_dve.before(it, f"h{n}"))
                                A_(out(e_tanh[:, n, :]), bank(4 * n), ACT.Tanh, scale=0.5
                                   ).then_inc(exp_act.inc(f"t{n}"), 1)

                with act.If(act.value_load(fits[0:1, 0:1], min_val=0, max_val=1)):
                    experts(False)
                with act.Else():
                    experts(True)
                next_phase(act, "act", l)
                for i in range(NCH):
                    rows_out(i, tile_rows(i), back_pe, back_act)
                next_phase(act, "act", l)
            norm(DEPTH * 2)

        @block.gpsimd
        def _(pool):
            for S in (prep_pool, pair_pool):
                pool.sem_inc(S.sem, len(S.names))
            pool.memset(vfb, 0.0)
            pool.drain().then_inc(zeroed, 1)
            pool.wait_ge(zeroed, 1)
            for q in range(NPAIR):
                pool.dma_start(v_first[q], vfb).then_inc(vf_out, 16)
            pool.wait_ge(loaded, 16 * (KD + 1))
            pool.wait_ge(vf_out, 16 * NPAIR)
            with pool.Fori(0, DEPTH) as l:
                for _ in range(2):
                    next_phase(pool, "pool", l)

                def receptance(turn):
                    pool.drain()
                    pool.wait_ge(prep_act.sem, prep_act.at(turn, "G"))
                    pool.wait_ge(prep_dve.sem, prep_dve.at(turn, "r"))
                    nc.gpsimd.tensor_tensor(arh[0:64, 1, 0:T], pr[0:64, :], G[0:64, :], ALU.mult)
                    nc.gpsimd.tensor_tensor(arh[64:128, 3, 0:T], pr[64:128, :], G[64:128, :], ALU.mult)
                    pool.drain().then_inc(prep_pool.inc("r"), 1)

                def pair(q, more):
                    it = l * NPAIR + q
                    pool.drain()
                    pool.wait_ge(pair_pe.sem, pair_pe.before(it, f"o{NCH - 1}"))
                    pool.wait_ge(prep_dve.sem, prep_dve.at(it, "a"))
                    alone(pool)
                    nc.gpsimd.tensor_copy(ar[0:64, :, :], arh[0:64, 0:2, :])
                    nc.gpsimd.tensor_copy(ar[64:128, :, :], arh[64:128, 2:4, :])
                    pool.drain().then_inc(pair_pool.inc("ar"), 1)
                    pool.wait_ge(prep_dve.sem, prep_dve.at(it, "v"))
                    alone(pool)
                    pool.dma_start(v_first[ds(q, 1)].rearrange("a p b -> p (a b)") if more else v_first[q], vfb
                                   ).then_inc(vf_out, 16)
                    if more:
                        pool.wait_ge(vf_out, 16 * (NPAIR + 1) + 16 * it)
                        alone(pool)
                        pool.dma_start(vfb, v_first[ds(q + 1, 1)].rearrange("a p b -> p (a b)")).then_inc(vf_in, 16)
                    for n, lv in enumerate(LEVELS):
                        o = CONSTS["level"][0] + (n + 1) * CH
                        mask = cst[0:CH, o:o + CH].rearrange("p (a b) -> p a b", a=1).to_broadcast([CH, 4, CH])
                        for x in range(3):
                            if n == 0:
                                pool.wait_ge(pair_dve.sem, pair_dve.at(it, f"gram{2 * x + 1}"))
                            else:
                                pool.wait_ge(pair_pe.sem, pair_pe.at(it, f"t{LEVELS[n - 1]}_{x}"))
                            nc.gpsimd.tensor_tensor(lv_as[x], gr[:, 4 * x:4 * x + 4, 0:CH], mask, ALU.mult
                                                    ).then_inc(pair_pool.inc(f"lv{lv}_{x}"), 1)
                    if more:
                        receptance(it + 1)

                pool.wait_ge(vf_out, 16 * NPAIR + 16 * NPAIR * l)
                alone(pool)
                pool.dma_start(vfb, v_first[0]).then_inc(vf_in, 16)
                receptance(l * NPAIR)
                with pool.Fori(0, NPAIR - 1) as q:
                    pair(q, True)
                pair(NPAIR - 1, False)
                for _ in range(N_PHASES - 2):
                    next_phase(pool, "pool", l)

        @block.vector
        def _(dve):
            V = nc.vector
            for S in DVE_STEPS:
                dve.sem_inc(S.sem, len(S.names))
            dve.wait_ge(loaded, 16 * (KD + 1))
            dve.wait_ge(zeroed, 1)

            def norm(turn, gains):
                dve.wait_ge(norm_pe.sem, norm_pe.at(turn, "sum"))
                V.tensor_scalar(two(n_rs), acc(0), 1.0 / D, EPS, ALU.mult, ALU.add).then_inc(norm_dve.inc("mean"), 1)
                dve.wait_ge(norm_act.sem, norm_act.at(turn, "sqrt"))
                V.reciprocal(n_rs, n_rs)
                dve.drain()
                for j in range(KD):
                    V.scalar_tensor_tensor(u[:, j, :], h[:, j, :], pc(gains, j), n_rs, ALU.mult, ALU.mult)
                dve.drain()

            def rope(dst, src, rotated, tmp, rows=slice(0, P)):
                V.tensor_tensor(tmp, rotated, two(sin[rows, :]), ALU.mult)
                V.tensor_tensor(src, src, cos[rows, :], ALU.mult)
                dve.drain()
                return V.tensor_tensor(dst, src, tmp.rearrange("p a b -> p (a b)"), ALU.add)

            def shift(dst, raw, mu, tmp):
                V.tensor_tensor(tmp, raw[:, 0:T], raw[:, 1:T + 1], ALU.subtract)
                dve.drain()
                return V.scalar_tensor_tensor(dst, tmp, mu, raw[:, 1:T + 1], ALU.mult, ALU.add)

            with dve.Fori(0, DEPTH) as l:
                dve.wait_ge(par_full, (l + 1) * 16)
                norm(l * 2, "norm_mix")
                next_phase(dve, "dve", l)

                V.memset(raw_r[:, 0:1], 0.0)
                V.memset(raw_k[:, 0:1], 0.0)
                V.memset(raw_v[:, 0:1], 0.0)
                V.tensor_scalar(half_w0, par[:, PARAMS["w0"][0]:PARAMS["w0"][0] + 8], 0.5, None, ALU.mult)
                V.tensor_scalar(half_a0, par[:, PARAMS["a0"][0]:PARAMS["a0"][0] + 8], 0.5, None, ALU.mult)
                V.tensor_scalar(half_v0, par[:, PARAMS["v0"][0]:PARAMS["v0"][0] + 8], 0.5, None, ALU.mult)
                dve.drain()
                dve.wait_ge(low_act.sem, low_act.at(l, "wa"))
                shift(lr_wa, raw_r, pc("mu_wa"), tz)
                dve.wait_ge(low_act.sem, low_act.at(l, "g"))
                shift(lr_g, raw_k, pc("mu_g"), ta)
                dve.wait_ge(low_act.sem, low_act.at(l, "vres"))
                shift(lr_v, raw_v, pc("mu_vres"), tv).then_inc(low_dve.inc("shift"), 1)
                dve.wait_ge(low_act.sem, low_act.at(l, "tanh"))
                V.tensor_scalar(lr_g, lr_g, 0.5, 0.5, ALU.mult, ALU.add)
                next_phase(dve, "dve", l)

                P_ = prep_dve

                def decay(turn):
                    dve.wait_ge(prep_act.sem, prep_act.at(turn, "z"))
                    rate = -0.5 * float(np.exp(-0.5))
                    V.tensor_scalar(tz, tz, rate, rate, ALU.mult, ALU.add)
                    dve.drain()
                    V.tensor_tensor_scan(cum, c("reset"), tz, 0.0, ALU.mult, ALU.add)
                    dve.drain()
                    V.tensor_tensor(Gx, cum, tz, ALU.subtract).then_inc(P_.inc("c"), 1)

                def sigmoids(turn):
                    dve.wait_ge(prep_act.sem, prep_act.at(turn, "vres"))
                    V.tensor_scalar(ta, ta, 0.5, 0.5, ALU.mult, ALU.add)
                    V.tensor_scalar(tv, tv, 0.5, 0.5, ALU.mult, ALU.add)

                def receptance(turn, q):
                    dve.wait_ge(prep_act.sem, prep_act.at(turn, "r"))
                    shift(pr, raw_r, pc("mu_r", q), kh).then_inc(P_.inc("r"), 1)

                def keys_of(turn, q):
                    dve.drain()
                    dve.wait_ge(prep_act.sem, prep_act.at(turn, "k"))
                    shift(pk, raw_k, pc("mu_k", q), kh)
                    dve.drain()
                    V.tensor_scalar(kk, pk, pc("k_k", q), None, ALU.mult).then_inc(P_.inc("kk"), 1)

                def decayed_keys(turn, q):
                    V.tensor_scalar(kh, ta, -1.0, pc("k_a", q), ALU.add, ALU.mult)
                    dve.drain()
                    V.scalar_tensor_tensor(kh, kh, 1.0, pk, ALU.add, ALU.mult)
                    dve.drain()

                def bonus_terms(turn, q):
                    V.scalar_tensor_tensor(tz, pr, pc("r_k", q), kh, ALU.mult, ALU.mult).then_inc(P_.inc("rkk"), 1)
                    dve.wait_ge(prep_pe.sem, prep_pe.at(turn, "kk"))
                    V.tensor_scalar(two(sqk), acc(4), 1e-24, None, ALU.max).then_inc(P_.inc("kkmax"), 1)

                def unit_keys(turn, q):
                    dve.wait_ge(prep_act.sem, prep_act.at(turn, "norm"))
                    V.reciprocal(sqk, sqk)
                    dve.drain()
                    V.tensor_tensor(kk, kk, sqk, ALU.mult)
                    dve.drain()

                def abar(turn, q):
                    V.scalar_tensor_tensor(arh[0:64, 0, 0:T], kk[0:64, :], -1.0, Gx[0:64, :], ALU.mult, ALU.mult)
                    V.scalar_tensor_tensor(arh[64:128, 2, 0:T], kk[64:128, :], -1.0, Gx[64:128, :], ALU.mult,
                                           ALU.mult)
                    dve.drain().then_inc(P_.inc("a"), 1)

                def bbar_kbar(turn, q):
                    V.tensor_tensor(kk, kk, ta, ALU.mult)
                    V.tensor_tensor(kb_[:, 0:T], kh, Gi, ALU.mult)
                    dve.drain()
                    V.tensor_tensor(bb[:, 0:T], kk, Gi, ALU.mult)
                    dve.drain().then_inc(P_.inc("rbk"), 1)

                def shifted_values(turn, q):
                    dve.wait_ge(prep_act.sem, prep_act.at(turn, "v"))
                    shift(pv[:, 0:T], raw_v, pc("mu_v", q), pk)

                def values(turn):
                    v, tmp = pv[:, 0:T], raw_v[:, 1:T + 1]
                    dve.drain()
                    dve.wait_ge(vf_in, 16 * (turn + 1))
                    V.tensor_tensor(tmp, vfb, v, ALU.subtract)
                    dve.drain()
                    V.scalar_tensor_tensor(tmp, tmp, pc("later"), tv, ALU.mult, ALU.mult)
                    dve.drain()
                    V.tensor_tensor(v, v, tmp, ALU.add)
                    dve.drain()
                    V.tensor_tensor(tv, v, vfb, ALU.subtract)
                    dve.drain()
                    V.scalar_tensor_tensor(vfb, tv, pc("first"), vfb, ALU.mult, ALU.add)
                    dve.drain().then_inc(P_.inc("v"), 1)

                CHUNK_PARTS = (decayed_keys, bonus_terms, unit_keys, abar, bbar_kbar, shifted_values)

                def pair(q, more):
                    it = l * NPAIR + q
                    S = pair_dve

                    def pe_did(name):
                        dve.wait_ge(pair_pe.sem, pair_pe.at(it, name))

                    def act_did(name):
                        dve.wait_ge(pair_act.sem, pair_act.at(it, name))

                    dve.drain()
                    V.memset(state, 0.0)
                    V.tensor_copy(gend.rearrange("p (a b) -> p a b", b=1),
                                  G[:, 0:(NCH - 1) * CH].rearrange("p (a b) -> p a b", b=CH)[:, :, CH - 1:CH])
                    V.tensor_copy(pg_now, pg)
                    gmask = c("grams", CH).rearrange("p (a b) -> p a b", a=1).to_broadcast([CH, 2, 4 * CH])
                    low1 = c("low1", CH).rearrange("p (a b) -> p a b", a=1).to_broadcast([CH, 2, CH])
                    for i in range(NCH):
                        if i == 2:
                            pe_did("bonus")
                            V.tensor_tensor(two(bonus), acc(0), two(pv[:, 0:T]), ALU.mult).then_inc(S.inc("bonus"), 1)
                        pe_did(f"gram{i}")
                        b = GRAM_BANKS[i % 4]
                        V.tensor_tensor(gr[:, 2 * i:2 * i + 2, :], ps[0:CH, b:b + 2, 0:4 * CH], gmask, ALU.mult)
                        V.tensor_tensor(inv[:, 2 * i:2 * i + 2, :], ps[0:CH, b:b + 2, 4 * CH:5 * CH], low1, ALU.mult)
                        dve.drain().then_inc(S.inc(f"gram{i}"), 1)
                    o = CONSTS["level"][0]
                    lv1 = cst[0:CH, o:o + CH].rearrange("p (a b) -> p a b", a=1).to_broadcast([CH, 4, CH])
                    i96 = ident[0:CH, 0:CH].rearrange("p (a b) -> p a b", a=1).to_broadcast([CH, 4, CH])
                    for x in range(3):
                        it4, iv4 = inv_t[:, 4 * x:4 * x + 4, :], inv[:, 4 * x:4 * x + 4, :]
                        V.tensor_tensor(it4, gr[:, 4 * x:4 * x + 4, 0:CH], lv1, ALU.mult)
                        V.tensor_tensor(iv4, iv4, i96, ALU.add)
                        dve.drain()
                        V.tensor_tensor(it4, it4, i96, ALU.add)
                        dve.drain().then_inc(S.inc(f"one{x}"), 1)
                    for lv in LEVELS:
                        for x in range(3):
                            pe_did(f"nm{lv}_{x}")
                            for dst, b in ((inv_t, 2 + x % 2), (inv, 4 + x % 2))[0:1 if lv == LEVELS[-1] else 2]:
                                V.tensor_tensor(dst[:, 4 * x:4 * x + 4, :], dst[:, 4 * x:4 * x + 4, :],
                                                ps[0:CH, b, 0:4 * CH].rearrange("p (a b) -> p a b", a=4), ALU.add)
                            dve.drain().then_inc(S.inc(f"nm{lv}_{x}"), 1)
                        if more and lv == 2:
                            decay(it + 1)
                        if more and lv == 8:
                            sigmoids(it + 1)
                        if more and lv == 16:
                            receptance(it + 1, q + 1)
                        if more and lv == 32:
                            keys_of(it + 1, q + 1)
                    for i in range(NCH):
                        pe_did(f"x{i}")
                        V.tensor_copy(xs[0:CH, :], ps[0:CH, 0, 0:P]).then_inc(S.inc(f"x{i}"), 1)
                        if more:
                            CHUNK_PARTS[i](it + 1, q + 1)
                        if i < NCH - 1:
                            pe_did(f"d{i}")
                            V.tensor_tensor(state, state, ps[:, 3, 0:P], ALU.add)
                            dve.drain()
                            V.scalar_tensor_tensor(state, state, gend[:, i:i + 1], headones, ALU.mult,
                                                   ALU.mult).then_inc(S.inc(f"s{i}"), 1)
                    pe_did("mean")
                    V.scalar_tensor_tensor(two(pairs_o), acc(0), -1.0 / 64, two(pairs_o), ALU.mult, ALU.add
                                           ).then_inc(S.inc("cen"), 1)
                    if more:
                        values(it + 1)
                    pe_did("var")
                    V.tensor_scalar(two(otmp), acc(2), 1.0 / 64, GN_EPS, ALU.mult, ALU.add).then_inc(S.inc("var"), 1)
                    act_did("std")
                    V.reciprocal(otmp, otmp)
                    dve.drain()
                    V.tensor_tensor(pairs_o, pairs_o, otmp, ALU.mult)
                    dve.drain()
                    V.tensor_scalar(pairs_o, pairs_o, pc("ln_w", q), pc("ln_b", q), ALU.mult, ALU.add)
                    dve.drain()
                    V.tensor_tensor(pairs_o, pairs_o, bonus, ALU.add)
                    dve.drain()
                    y_q = y[:, q, :] if isinstance(q, int) else y[:, ds(q, 1), :].rearrange("p a b -> p (a b)")
                    V.tensor_tensor(y_q, pairs_o, pg_now, ALU.mult).then_inc(S.inc("y"), 1)

                V.memset(bb[:, T:TP], 0.0)
                V.memset(kb_[:, T:TP], 0.0)
                V.memset(pv[:, T:TP], 0.0)
                V.memset(arh, 0.0)
                dve.drain()
                first = l * NPAIR
                decay(first)
                sigmoids(first)
                receptance(first, 0)
                keys_of(first, 0)
                dve.drain()
                for part in CHUNK_PARTS:
                    part(first, 0)
                values(first)
                with dve.Fori(0, NPAIR - 1) as q:
                    pair(q, True)
                pair(NPAIR - 1, False)
                next_phase(dve, "dve", l)

                def merge(k):
                    with dve.Fori(0, 4) as q:
                        it = l * 12 + 4 * k + q
                        for n in range(2):
                            dve.wait_ge(merge_act.sem, merge_act.at(it, f"g{n}"))
                            dve.wait_ge(merge_pe.sem, merge_pe.at(it, f"p{n}"))
                            V.scalar_tensor_tensor(two(g_tmp[:, n, :]), two(g_tanh[:, n, :]), 1.0, acc(4 * n),
                                                   ALU.add, ALU.mult)
                            dve.drain()
                            dst = m[:, ds(2 * q + n, 1), :].rearrange("p a b -> p (a b)")
                            if k == 0:
                                last = V.tensor_scalar(dst, g_tmp[:, n, :], 0.5, None, ALU.mult)
                            else:
                                last = V.scalar_tensor_tensor(dst, g_tmp[:, n, :], 0.5, dst, ALU.mult, ALU.add)
                            last.then_inc(merge_dve.inc(f"m{n}"), 1)
                    next_phase(dve, "dve", l)

                merge(0)
                o = CONSTS["counts"][0]
                for j in range(8):
                    w = POOL_WINDOWS[j // 2]
                    dve.wait_ge(pool_act.sem, pool_act.at(l, f"p{j}"))
                    src, k = p_raw[:, j % 2, :], 1
                    bufs = [p_a, p_b]
                    while k < w:
                        dst = bufs[0]
                        V.tensor_tensor(dst[:, k:T], src[:, k:T], src[:, 0:T - k], ALU.add)
                        V.tensor_copy(dst[:, 0:k], src[:, 0:k])
                        dve.drain()
                        src, k = dst, 2 * k
                        bufs.reverse()
                    dst = bufs[0]
                    V.scalar_tensor_tensor(pooled[:, j, w:T], src[:, w:T], 1.0 / w, p_raw[:, j % 2, w:T], ALU.mult,
                                           ALU.subtract)
                    V.tensor_tensor(dst[:, 0:w], src[:, 0:w], cst[:, o:o + w], ALU.mult)
                    dve.drain()
                    V.tensor_tensor(pooled[:, j, 0:w], dst[:, 0:w], p_raw[:, j % 2, 0:w], ALU.subtract)
                    dve.drain().then_inc(pool_dve.inc(f"p{j}"), 1)
                next_phase(dve, "dve", l)
                merge(1)

                def pe_did(name):
                    dve.wait_ge(lat_pe.sem, lat_pe.at(l, name))

                def act_did(name):
                    dve.wait_ge(lat_act.sem, lat_act.at(l, name))
                S = lat_dve
                pe_did("qsum")
                V.tensor_scalar(two(l_rs), acc(2), 1.0 / 256, EPS, ALU.mult, ALU.add)
                pe_did("kvsum")
                V.tensor_scalar(two(l_rs2), acc(4), 1.0 / 128, EPS, ALU.mult, ALU.add)
                dve.drain().then_inc(S.inc("means"), 1)
                act_did("std")
                V.reciprocal(l_rs, l_rs)
                V.reciprocal(l_rs2, l_rs2)
                dve.drain()
                for j in range(2):
                    V.scalar_tensor_tensor(cq[:, j, :], cq[:, j, :], pc("q_norm", j), l_rs, ALU.mult, ALU.mult)
                V.scalar_tensor_tensor(ckv, ckv, pc("kv_norm"), l_rs2, ALU.mult, ALU.mult)
                dve.drain().then_inc(S.inc("latents"), 1)
                pe_did("mean")
                V.scalar_tensor_tensor(two(kidx), acc(6), -1.0 / 64, two(kidx), ALU.mult, ALU.add
                                       ).then_inc(S.inc("center"), 1)
                pe_did("var")
                V.tensor_scalar(two(l_tmp), acc(6), 1.0 / 64, EPS, ALU.mult, ALU.add).then_inc(S.inc("var"), 1)
                act_did("std2")
                V.reciprocal(l_tmp, l_tmp)
                dve.drain()
                V.tensor_tensor(kidx, kidx, l_tmp, ALU.mult)
                dve.drain()
                V.tensor_scalar(kidx, kidx, pc("idx_w"), pc("idx_b"), ALU.mult, ALU.add).then_inc(S.inc("kidx"), 1)
                pe_did("kperm")
                rope(kidx, kidx, acc(2), two(l_tmp))
                pe_did("rperm")
                rope(kr, kr, acc(4), two(l_tmp2))
                dve.drain().then_inc(S.inc("ropes"), 1)
                for j in range(4):
                    pe_did(f"qp{j}")
                    rope(qi[:, j, :], qi[:, j, :], acc(2 * j), two((l_tmp, l_tmp2)[j % 2])
                         ).then_inc(S.inc(f"rope{j}"), 1)
                next_phase(dve, "dve", l)

                tri, tri_b = c("causal", CH), c("bias", CH)
                V.tensor_copy(sel_of(0), tri_b)
                for n, (i, hd) in enumerate(IDX):
                    z, wd, tr = n % 2, tile_keys(i), tile_rows(i)
                    dve.wait_ge(idx_act.sem, idx_act.at(l, f"s{i}_{hd}"))
                    sc = score[0:tr, 0:wd]
                    if hd == 0:
                        last = V.tensor_scalar(sc, relu_b[0:tr, z, 0:wd], wtok[0:tr, i, 0:1], None, ALU.mult)
                    else:
                        last = V.scalar_tensor_tensor(sc, relu_b[0:tr, z, 0:wd], wtok[0:tr, i, hd:hd + 1], sc,
                                                      ALU.mult, ALU.add)
                    last.then_inc(idx_dve.inc(f"s{i}_{hd}"), 1)
                    dve.drain()
                    if hd < 7:
                        continue
                    V.tensor_tensor(sc[:, i * CH:wd], sc[:, i * CH:wd], tri[0:tr, 0:tr], ALU.add)
                    dve.drain()
                    for _ in range(TOPK // 8):
                        V.max(top8[0:tr, :], sc)
                        dve.drain()
                        V.match_replace(sc, top8[0:tr, :], sc, TAKEN)
                        dve.drain()
                    s_i = sel_of(i)
                    V.tensor_scalar(s_i, sc, TAKEN, NEG_BIAS, ALU.is_gt, ALU.mult)
                    dve.drain()
                    V.tensor_tensor(s_i[:, i * CH:wd], s_i[:, i * CH:wd], tri_b[0:tr, 0:tr], ALU.add)
                next_phase(dve, "dve", l)

                with dve.Fori(0, 2) as q:
                    it = l * 2 + q
                    S = att_dve

                    def pe_did(name):
                        dve.wait_ge(att_pe.sem, att_pe.at(it, name))

                    def act_did(name):
                        dve.wait_ge(att_act.sem, att_act.at(it, name))

                    V.tensor_copy(kh2[64:96, 0, :], kr[64:96, :])
                    V.tensor_copy(kh2[64:96, 1, :], kr[64:96, :])
                    dve.drain().then_inc(S.inc("kr"), 1)
                    for hd in range(8):
                        z = hd % 2
                        pe_did(f"perm{hd}")
                        rope(qh[64:96, z, :], qh[64:96, z, :], acc(6, slice(64, 96)), two(rope_t[64:96, :]),
                             slice(64, 96)).then_inc(S.inc(f"rope{hd}"), 1)
                        for step in range(NCH + 1):
                            if step < NCH:
                                i = step
                                wd, b, k, tr = tile_keys(i), 2 * (i % 2), i % 2, tile_rows(i)
                                pe_did(f"s{i}_{hd}")
                                if i >= 2:
                                    pe_did(f"pt{i - 2}_{hd}")
                                elif hd >= 1:
                                    pe_did(f"pt{i + 4}_{hd - 1}")
                                else:
                                    dve.wait_ge(att_pe.sem, att_pe.before(it, f"pt{i + 4}_7"))
                                alone(dve)
                                V.tensor_tensor_reduce(
                                    out=parts(es[0:tr, k, 0:wd], i), in0=scores(b, i), in1=parts(sel_of(i), i),
                                    scale=1.0, scalar=NEG_CAUSAL, op0=ALU.add, op1=ALU.max,
                                    accum_out=mx[0:tr, k:k + 1])
                                dve.drain()
                                V.tensor_scalar(mx[0:tr, k:k + 1], mx[0:tr, k:k + 1], -ATT_SCALE, None, ALU.mult
                                                ).then_inc(S.inc(f"m{i}_{hd}"), 1)
                            if step >= 1:
                                i = step - 1
                                wd, k, tr = tile_keys(i), i % 2, tile_rows(i)
                                act_did(f"e{i}_{hd}")
                                V.reciprocal(ri[0:tr, k:k + 1], rs[0:tr, k:k + 1])
                                dve.drain()
                                V.tensor_scalar(es[0:tr, k, 0:wd], es[0:tr, k, 0:wd], ri[0:tr, k:k + 1], None, ALU.mult
                                                ).then_inc(S.inc(f"n{i}_{hd}"), 1)
                next_phase(dve, "dve", l)
                merge(2)

                with dve.Fori(0, 2) as q:
                    it = l * 2 + q
                    for s in range(4):
                        dve.wait_ge(res_pe.sem, res_pe.at(it, f"o{s}"))
                        dst = h[:, ds(4 * q + s, 1), :].rearrange("p a b -> p (a b)")
                        V.tensor_tensor(two(dst), two(dst), acc(2 * s), ALU.add).then_inc(res_dve.inc(f"h{s}"), 1)
                next_phase(dve, "dve", l)
                norm(l * 2 + 1, "norm_ffn")
                next_phase(dve, "dve", l)

                S = rt_dve
                V.memset(y[:, :, :], 0.0)
                V.memset(all1, 1.0)
                dve.drain()
                V.tensor_tensor_scan(count1, all1, all1, 0.0, ALU.mult, ALU.add)
                dve.wait_ge(rt_pe.sem, rt_pe.at(l, "logits"))
                ob = PARAMS["router_b"][0]
                V.tensor_tensor(lg, ps[0:CH, 0, 0:20 * NCH].rearrange("p (a b) -> p a b", a=NCH),
                                par[0:CH, ob:ob + 20].rearrange("p (a b) -> p a b", a=1).to_broadcast([CH, NCH, 20]),
                                ALU.add)
                dve.drain()
                keys = c("keys", CH).rearrange("p (a b) -> p a b", a=1).to_broadcast([CH, NCH, 4])

                def over(v):
                    return v.rearrange("p (a b) -> p a b", b=1).to_broadcast([CH, NCH, 4])

                def first_max(dst, src, top):
                    V.tensor_reduce(top, src, AX.X, ALU.max)
                    dve.drain()
                    V.tensor_tensor(r2, src, over(top), ALU.is_ge)
                    dve.drain()
                    V.tensor_tensor(r2, r2, keys, ALU.mult)
                    dve.drain()
                    V.tensor_reduce(s5, r2, AX.X, ALU.max)
                    dve.drain()
                    V.tensor_tensor(dst, r2, over(s5), ALU.is_equal)
                    dve.drain()

                first_max(oh, lg[:, :, 0:4], s1)
                V.tensor_tensor(r1, lg[:, :, 0:4], over(s1), ALU.subtract)
                dve.drain().then_inc(S.inc("gmax"), 1)
                e16 = lg[:, :, 4:20].rearrange("p a (g e) -> p a g e", g=4)
                r16v = r16.rearrange("p a (g e) -> p a g e", g=4)
                for g in range(4):
                    V.tensor_tensor(r16v[:, :, g, :], e16[:, :, g, :], oh[:, :, g:g + 1].to_broadcast([CH, NCH, 4]),
                                    ALU.mult)
                dve.drain()
                V.tensor_reduce(r3, r16.rearrange("p a (g e) -> p a e g", g=4), AX.X, ALU.add)
                dve.drain()
                first_max(oh1, r3, s2)
                V.scalar_tensor_tensor(r3, oh1, NEG_CAUSAL, r3, ALU.mult, ALU.add)
                dve.drain()
                first_max(oh2, r3, s3)
                V.tensor_tensor(s4, s3, s2, ALU.subtract).then_inc(S.inc("ediff"), 1)
                dve.wait_ge(rt_act.sem, rt_act.at(l, "gexp"))
                V.tensor_reduce(s1, r1, AX.X, ALU.add)
                dve.wait_ge(rt_act.sem, rt_act.at(l, "eexp"))
                V.tensor_scalar(s2, s4, 1.0, None, ALU.add)
                dve.drain()
                V.tensor_tensor(s2, s2, s1, ALU.mult)
                dve.drain()
                V.reciprocal(s2, s2)
                dve.drain()
                V.tensor_tensor(s3, s2, s4, ALU.mult)
                V.tensor_tensor(oh1, oh1, over(s2), ALU.mult)
                dve.drain()
                V.tensor_tensor(oh2, oh2, over(s3), ALU.mult)
                dve.drain()
                V.tensor_tensor(ce, oh1, oh2, ALU.add)
                dve.drain()
                for g in range(4):
                    V.tensor_tensor(comb[:, :, 4 * g:4 * g + 4], ce, oh[:, :, g:g + 1].to_broadcast([CH, NCH, 4]),
                                    ALU.mult)
                dve.drain().then_inc(S.inc("oh"), 1)
                dve.wait_ge(rt_pe.sem, rt_pe.at(l, "oh"))
                V.tensor_copy(oh_t[:, 0:5 * CH], ps[0:4, 0, 0:5 * CH])
                V.tensor_copy(oh_t[:, 5 * CH:T], ps[0:4, 1, 5 * CH - window(5):CH])
                dve.drain()
                V.tensor_tensor_scan(rank, all1[0:4, :], oh_t, 0.0, ALU.mult, ALU.add)
                dve.drain().then_inc(S.inc("rank"), 1)
                dve.wait_ge(rt_pe.sem, rt_pe.at(l, "start"))
                V.tensor_copy(start4, ps[0:4, 0, 0:1])
                V.tensor_copy(start_row, ps[0:1, 0, 4:12])
                dve.drain()
                V.scalar_tensor_tensor(place4, rank, start4, oh_t, ALU.add, ALU.mult)
                dve.drain().then_inc(S.inc("pos"), 1)
                V.tensor_scalar(starts[0:1, :], start_row[:, 0:4], float(T - GROUP_COLS), None, ALU.min)
                V.tensor_reduce(most, start_row[:, 4:8], AX.X, ALU.max)
                dve.drain()
                V.tensor_scalar(fits[0:1, :], most, GROUP_COLS + 0.5, None, ALU.is_lt)
                dve.wait_ge(rt_pe.sem, rt_pe.at(l, "pos"))
                V.tensor_tensor(place_tok, ps[0:CH, 1, 0:NCH], c("own", CH), ALU.mult)
                dve.drain().then_inc(S.inc("take"), 1)
                for i in range(NCH):
                    V.tensor_scalar(take[:, i, :], count1[0:CH, :], place_tok[:, i:i + 1], None, ALU.is_equal
                                    ).then_inc(S.inc(f"perm{i}"), 1)
                dve.wait_ge(rt_act.sem, rt_act.at(l, "pos"))
                slot = c("slot", CH)
                for i in range(NCH):
                    V.tensor_scalar(give[:, i, :], place[0:CH, :], slot[:, i:i + 1], None, ALU.is_equal)
                for j in range(1, KD, 2):
                    dve.wait_ge(rt_pe.sem, rt_pe.at(l, f"su{j}"))
                    V.tensor_copy(two(u[:, j, :]), acc((6, 0, 2, 4)[j % 4])).then_inc(S.inc(f"su{j}"), 1)
                next_phase(dve, "dve", l)

                def experts(all_columns):
                    n_cols = T if all_columns else GROUP_COLS
                    y_flat = y[:, :, :].rearrange("p a b -> p (a b)")

                    def out(x):
                        return two(x) if all_columns else x[:, 0:GROUP_COLS]

                    def bank(b):
                        return acc(b) if all_columns else ps[:, b, 0:GROUP_COLS]

                    with dve.Fori(0, 4) as g:
                        gi = l * 4 + g
                        off = 0 if all_columns else dve.value_load(starts[0:1, ds(g, 1)], min_val=0,
                                                                   max_val=T - GROUP_COLS)
                        for e in range(4):
                            if e == 0:
                                dve.wait_ge(grp_pe.sem, grp_pe.before(gi, "c3"))
                            else:
                                dve.wait_ge(grp_pe.sem, grp_pe.at(gi, f"c{e - 1}"))
                            if e == 0:
                                alone(dve)
                            src = comb_t if all_columns else comb_t[:, ds(off, GROUP_COLS)]
                            V.tensor_scalar(comb_sel[:, 0:n_cols], src, ident[0:16, ds(4 * g + e, 1)], None, ALU.mult
                                            ).then_inc(grp_dve.inc(f"c{e}"), 1)
                        dve.wait_ge(grp_act.sem, grp_act.at(gi, "c3"))
                        alone(dve)
                        with dve.Fori(0, 4) as e:
                            it = gi * 4 + e
                            for n in range(2):
                                dve.wait_ge(exp_act.sem, exp_act.at(it, f"t{n}"))
                                dve.wait_ge(exp_pe.sem, exp_pe.at(it, f"b{n}"))
                                tmp = out(e_tmp[:, n, :])
                                V.scalar_tensor_tensor(tmp, out(e_tanh[:, n, :]), 1.0, bank(4 * n), ALU.add, ALU.mult)
                                dve.drain()
                                V.tensor_tensor(tmp, tmp, bank(4 * n + 2), ALU.mult)
                                dve.drain()
                                V.scalar_tensor_tensor(
                                    hid[:, ds(2 * e + n, 1), 0:n_cols].rearrange("p a b -> p (a b)"),
                                    e_tmp[:, n, 0:n_cols], 0.5,
                                    comb_b[:, ds(e, 1), 0:n_cols].rearrange("p a b -> p (a b)"), ALU.mult, ALU.mult)
                                dve.drain().then_inc(exp_dve.inc(f"h{n}"), 1)
                        with dve.Fori(0, 2) as q:
                            it = gi * 2 + q
                            for s in range(4):
                                dve.wait_ge(dn_pe.sem, dn_pe.at(it, f"o{s}"))
                                dst = y_flat[:, ds((4 * q + s) * T + off, n_cols)]
                                if all_columns:
                                    dst = two(dst)
                                V.tensor_tensor(dst, dst, bank(2 * s), ALU.add).then_inc(dn_dve.inc(f"h{s}"), 1)

                with dve.If(dve.value_load(fits[0:1, 0:1], min_val=0, max_val=1)):
                    experts(False)
                with dve.Else():
                    experts(True)
                next_phase(dve, "dve", l)
                for j in range(KD):
                    dve.wait_ge(back_pe.sem, back_pe.at(l, f"h{j}"))
                    V.tensor_tensor(two(h[:, j, :]), two(h[:, j, :]), acc(2 * (j % 4)), ALU.add
                                    ).then_inc(back_dve.inc(f"h{j}"), 1)
                next_phase(dve, "dve", l)
            norm(DEPTH * 2, "norm_final")
            dve.drain().then_inc(out_ready, 1)


def constant_table():
    t = np.zeros((P, N_CONST), np.float32)

    def put(name, a, rows=P):
        o, n = CONSTS[name]
        t[:rows, o:o + n] = a

    p = np.arange(P)
    put("ident", np.eye(P))
    put("ones", 1.0)
    put("headones", (p[:, None] // 64 == p[None, :] // 64))
    rot = p % 64 < 32
    partner = np.where(rot, np.where(p % 32 < 16, p + 16, p - 16), p)
    put("perm", partner[:, None] == p[None, :])
    inv = np.float32(10000.0) ** (-np.arange(0, 32, 2, dtype=np.float32) / np.float32(32))
    ang = np.arange(T, dtype=np.float32)[None, :] * inv.astype(np.float32)[p % 16][:, None]
    put("cos", np.where(rot[:, None], np.cos(ang), 1.0))
    put("sin", np.where(rot[:, None], np.where((p % 32 < 16)[:, None], -1.0, 1.0) * np.sin(ang), 0.0))
    put("reset", (np.arange(T) % CH != 0)[None, :])
    a, b = np.arange(CH)[:, None], np.arange(CH)[None, :]
    put("grams", np.concatenate([a < b, a <= b, a < b, a <= b], 1), CH)
    put("low1", (a > b) & (a // 2 == b // 2), CH)
    put("level", np.concatenate([(a // (2 * n) == b // (2 * n)) & (a // n != b // n) for n in [1] + LEVELS], 1), CH)
    put("causal", np.where(b > a, NEG_CAUSAL, 0.0), CH)
    put("bias", np.where(b > a, NEG_BIAS, 0.0), CH)
    put("keys", np.array([[4.0, 3.0, 2.0, 1.0]]))
    put("counts", 1.0 / np.arange(1, 17)[None, :])
    put("slot", p[:, None] + CH * np.arange(NCH)[None, :] + 1.0)
    put("own", (p[:, None] + np.array([window(i) for i in range(NCH)])[None, :]) >= CH * np.arange(NCH)[None, :])
    return t


def param_table(w):
    t = np.zeros((DEPTH, P, N_PARAM), np.float32)
    for l in range(DEPTH):
        def put(name, v):
            o, n = PARAMS[name]
            t[l, :, o:o + n] = np.asarray(v).reshape(n, P).T

        def padded(v):
            out = np.zeros(P, np.float32)
            out[:len(v)] = v
            return out

        for name, key in (("norm_mix", "norm_mix"), ("norm_ffn", "norm_ffn"), ("pool_scale", "pool_scale"),
                          ("w0", "rwkv_w0"), ("a0", "rwkv_a0"), ("k_k", "rwkv_k_k"), ("k_a", "rwkv_k_a"),
                          ("r_k", "rwkv_r_k"), ("ln_w", "rwkv_ln_w"), ("ln_b", "rwkv_ln_b"),
                          ("q_norm", "mla_q_norm"), ("kv_norm", "mla_kv_norm")):
            put(name, w[key][l])
        put("norm_final", w["norm_final"])
        put("v0", w["vres_v0"][max(l - 1, 0)])
        mu = w["mu_shift"][l]
        put("mu_r", mu[0:D])
        put("mu_k", mu[D:2 * D])
        put("mu_v", mu[2 * D:3 * D])
        put("mu_wa", mu[3 * D:3 * D + 128])
        put("mu_g", mu[3 * D + 128:])
        put("mu_vres", padded(w["vres_mu"][max(l - 1, 0)]))
        put("idx_w", np.concatenate([w["idx_k_norm_w"][l]] * 2))
        put("idx_b", np.concatenate([w["idx_k_norm_b"][l]] * 2))
        put("later", np.full(P, float(l > 0), np.float32))
        put("first", np.full(P, float(l == 0), np.float32))
        rt = np.concatenate([w["router_w_group"][l], w["router_w_expert"][l]], 1)
        o, n = PARAMS["router"]
        t[l, :, o:o + n] = rt.reshape(KD, P, 20).transpose(1, 0, 2).reshape(P, 160)
        o, n = PARAMS["router_b"]
        t[l, :, o:o + n] = np.concatenate([w["router_b_group"][l], w["router_b_expert"][l]])[None, :]
    return t


def weight_stream(w):
    out = np.zeros((DEPTH * LAYER_ROUNDS * RING, P, KD * P), np.float32)
    n = 0
    o_a = 3 * D
    o_s = o_a + D
    o_c = o_s + 3 * D + 256

    def columns(mat):
        nonlocal n
        v = out[n].reshape(P, KD, P)
        v[:, :, :mat.shape[1]] = mat.reshape(KD, P, -1).transpose(1, 0, 2)
        n += 1

    def blocks(*mats):
        nonlocal n
        for mat, row, col in mats:
            out[n, row:row + mat.shape[0], col:col + mat.shape[1]] = mat
        n += 1

    for l in range(DEPTH):
        wi, lv = w["w_in"][l], max(l - 1, 0)

        def start(phase):
            assert n == (l * LAYER_ROUNDS + FIRST[phase]) * RING, (phase, n)

        def merge(phase, proj, gate):
            start(phase)
            for j in range(8):
                columns(proj[:, j * P:(j + 1) * P])
                columns(wi[:, gate * D + j * P:gate * D + (j + 1) * P])

        start("lowrank")
        columns(wi[:, o_s + 3 * D:o_s + 3 * D + 128])
        columns(wi[:, o_s + 3 * D + 128:o_s + 3 * D + 256])
        columns(w["vres_w_down"][lv])
        n += 1
        start("pairs")
        for q in range(NPAIR):
            cq = slice(q * P, (q + 1) * P)
            blocks((w["rwkv_w2"][l][:, cq], 0, 0), (w["rwkv_a2"][l][:, cq], 64, P),
                   (w["rwkv_g2"][l][:, cq], 0, 2 * P), (w["vres_v2"][lv][:, cq], 0, 3 * P))
            for k in range(3):
                columns(wi[:, o_s + k * D + q * P:o_s + k * D + (q + 1) * P])
        merge("merge_b", w["w_proj_b"][l], 1)
        start("pool")
        for j in range(8):
            columns(wi[:, o_a + j * P:o_a + (j + 1) * P])
        for half in range(2):
            blocks(*((w["pool_w"][l, 2 * half + g, kb * P:(kb + 1) * P, nb * P:(nb + 1) * P], 0,
                      (g * 4 + nb * 2 + kb) * P) for g in range(2) for nb in range(2) for kb in range(2)))
        n += 2
        merge("merge_a", w["w_proj_a"][l], 0)
        start("dsa_in")
        columns(wi[:, o_c:o_c + 128])
        columns(wi[:, o_c + 128:o_c + 256])
        columns(wi[:, o_c + 256:o_c + 384])
        kidx = wi[:, o_c + 416:o_c + 480]
        columns(np.concatenate([kidx, kidx], 1))
        columns(np.concatenate([np.zeros((D, 64), np.float32), wi[:, o_c + 384:o_c + 416],
                                wi[:, o_c + 480:o_c + 488]], 1))
        iq = w["idx_w_q"][l]
        blocks(*((iq[kb * P:(kb + 1) * P, j * P:(j + 1) * P], 0, (2 * j + kb) * P)
                 for j in range(4) for kb in range(2)))
        n += 2
        start("heads")
        for b in range(4):
            uq = w["mla_w_uq"][l]
            blocks(*((uq[kb * P:(kb + 1) * P, (4 * b + k) * 96:(4 * b + k + 1) * 96], 0, (2 * k + kb) * P)
                     for k in range(4) for kb in range(2)))
            blocks(*((w["mla_w_uk"][l, 4 * b + k], 0, 64 * k) for k in range(4)),
                   *((w["mla_w_uv"][l, 4 * b + k], 0, 256 + 64 * k) for k in range(4)))
        merge("merge_c", w["w_proj_c"][l], 2)
        start("out")
        for j in range(8):
            columns(w["w_out"][l][:, j * P:(j + 1) * P])
        start("moe")
        for g in range(4):
            for e in range(4 * g, 4 * g + 4):
                for f in range(2):
                    columns(w["expert_w1"][l, e][:, f * P:(f + 1) * P])
                    columns(w["expert_w3"][l, e][:, f * P:(f + 1) * P])
            down = np.concatenate([w["expert_w2"][l, e] for e in range(4 * g, 4 * g + 4)], 0)
            for j in range(8):
                columns(down[:, j * P:(j + 1) * P])
    assert n == out.shape[0], (n, out.shape)
    return out


def kernel(**inputs):
    import concourse.bacc as bacc
    from concourse.bass_utils import run_bass_kernel_spmd

    w = {k: np.asarray(v) for k, v in inputs.items()}
    tokens = np.concatenate([w["meta_tokens"], w["x"][0]], 0)
    arrays = {
        "x_t": np.ascontiguousarray(tokens.T.reshape(KD, P, T)),
        "consts": constant_table(),
        "params": param_table(w),
        "stream": weight_stream(w),
    }
    nc = bacc.Bacc("TRN2", target_bir_lowering=False, num_devices=1)
    args = [nc.dram_tensor(k, a.shape, mybir.dt.from_np(a.dtype), kind="ExternalInput").ap()
            for k, a in arrays.items()]
    args.append(nc.dram_tensor("out_t", (KD, P, SEQ), mybir.dt.float32, kind="ExternalOutput").ap())
    trunk_program(nc, *args)
    r = run_bass_kernel_spmd(nc, [arrays], core_ids=[0])
    return r.results[0]["out_t"].reshape(D, SEQ).T.reshape(1, SEQ, D)
```

```python
import numpy as np
import concourse.bass as bass
from concourse import mybir
from contextlib import ExitStack

D, SEQ, N_META, DEPTH = 1024, 512, 16, 2
T = SEQ + N_META
P = 128
KD = D // P
HALF = T // 2
CH = 96
NCH = -(-T // CH)
TP = NCH * CH
GROUP_COLS = (144, 192)
NPAIR = 8
RING = 4
EPS = 1e-6
GN_EPS = 64e-5
TOPK = min(256, SEQ // 4)
LEVELS = [2, 4, 8, 16, 32, 64]
NEG_CAUSAL, TAKEN, NEG_BIAS = -3.0e38, -3.2e38, -1.0e30
IDX_SCALE = 8 ** -0.5 * 64 ** -0.5
ATT_SCALE = (64 + 32) ** -0.5
GRAM_BANKS = (4, 6, 2, 0)
POOL_WINDOWS = (2, 4, 8, 16)

ROUNDS = {"lowrank": 1, "pairs": 8, "merge_b": 4, "pool": 3, "dsa_in": 2, "merge_a": 4, "heads": 2,
          "merge_c": 4, "out": 2, "moe": 24}
FIRST, _n = {}, 0
for _k, _v in ROUNDS.items():
    FIRST[_k] = _n
    _n += _v
LAYER_ROUNDS = _n

CONSTS, _n = {}, 0
for _k, _v in (("ident", 128), ("ones", 128), ("headones", 128), ("perm", 128), ("cos", T), ("sin", T),
               ("reset", T), ("grams", 4 * CH), ("low1", CH), ("level", (1 + len(LEVELS)) * CH), ("causal", CH),
               ("bias", CH), ("keys", 4), ("counts", 16), ("slot", NCH), ("own", NCH)):
    CONSTS[_k] = (_n, _v)
    _n += _v
N_CONST = _n
PARAMS, _n = {}, 0
for _k, _v in (("norm_mix", 8), ("norm_ffn", 8), ("norm_final", 8), ("pool_scale", 8), ("w0", 8), ("a0", 8),
               ("k_k", 8), ("k_a", 8), ("r_k", 8), ("ln_w", 8), ("ln_b", 8), ("v0", 8), ("mu_r", 8),
               ("mu_k", 8), ("mu_v", 8), ("mu_wa", 1), ("mu_g", 1), ("mu_vres", 1), ("q_norm", 2),
               ("kv_norm", 1), ("idx_w", 1), ("idx_b", 1), ("later", 1), ("first", 1), ("router", 160),
               ("router_b", 20)):
    PARAMS[_k] = (_n, _v)
    _n += _v
N_PARAM = _n


def tile_rows(i):
    return min(CH, T - i * CH)


def tile_keys(i):
    return min((i + 1) * CH, T)


def window(i):
    return min(i * CH, T - CH)


class Steps:

    def __init__(self, sem, names):
        self.sem, self.names, self.next = sem, list(names), 0
        self.place = {n: i for i, n in enumerate(self.names)}

    def inc(self, name):
        assert self.names[self.next] == name, (self.names[self.next], name)
        self.next = (self.next + 1) % len(self.names)
        return self.sem

    def at(self, turn, name):
        return (turn + 1) * len(self.names) + self.place[name] + 1

    def before(self, turn, name):
        return turn * len(self.names) + self.place[name] + 1


def trunk_program(nc, x_t, consts, params, stream, out_t):
    f32 = mybir.dt.float32
    ALU = mybir.AluOpType
    ACT = mybir.ActivationFunctionType
    AX = mybir.AxisListType
    ds = bass.ds
    ctx = ExitStack()
    with ctx:
        def sb(name, shape):
            return ctx.enter_context(nc.sbuf_tensor(name, shape, f32))

        def sem(name):
            return ctx.enter_context(nc.semaphore(name))

        h = sb("h", [P, KD, T])
        u = sb("u", [P, KD, T])
        y = sb("y", [P, KD, T])
        m = sb("m", [P, KD, T])
        v_first = nc.dram_tensor("v_first", (NPAIR, P, T), f32, kind="Internal").ap()
        ring = sb("ring", [P, RING, KD * P])
        cst = sb("cst", [P, N_CONST])
        par = sb("par", [P, N_PARAM])
        scratch = sb("scratch", [P, 26400])
        ps = ctx.enter_context(nc.psum_tensor("ps", [P, 8, 512], f32))

        def c(name, rows=P):
            o, n = CONSTS[name]
            return cst[0:rows, o:o + n]

        ident, ones, headones, perm, cos, sin = map(c, ("ident", "ones", "headones", "perm", "cos", "sin"))

        def pc(name, j=0, rows=P):
            o, n = PARAMS[name]
            return par[0:rows, ds(o + j, 1)] if not isinstance(j, int) else par[0:rows, o + j:o + j + 1]

        def area(base=scratch[:, :]):
            at = [0]

            def take(*shape, rows=P):
                n = int(np.prod(shape))
                v = base[0:rows, at[0]:at[0] + n]
                at[0] += n
                assert at[0] <= base.shape[1], (at[0], base.shape)
                if len(shape) == 2:
                    v = v.rearrange("p (a b) -> p a b", a=shape[0])
                if len(shape) == 3:
                    v = v.rearrange("p (a b c) -> p a b c", a=shape[0], b=shape[1])
                return v
            return take

        def acc(bank, rows=slice(0, P)):
            return ps[rows, bank:bank + 2, 0:HALF]

        def two(ap):
            return ap.rearrange("p (a b) -> p a b", a=2)

        w_full = [sem(f"w_full{s}") for s in range(RING)]
        w_free = [sem(f"w_free{s}") for s in range(RING)]
        loaded, stored, par_full = sem("loaded"), sem("stored"), sem("par_full")
        zeroed = sem("zeroed")
        ends = {k: sem(f"{k}_phase_end") for k in ("pe", "dve", "act", "pool")}

        N_PHASES = 15
        passed = {k: sem(f"{k}_passed") for k in ("PE", "DVE", "Activation", "Pool")}

        def alone(eng):
            eng.sem_inc(passed[eng.engine.name], 1)

        phase_of = {"pe": 0, "dve": 0, "act": 0, "pool": 0}

        def next_phase(eng, me, layer):
            phase_of[me] += 1
            k = phase_of[me]
            alone(eng)
            eng.drain().then_inc(ends[me], 1)
            for other in ("pe", "dve", "act", "pool"):
                if other != me:
                    eng.wait_ge(ends[other], layer * N_PHASES + k)
            alone(eng)

        norm_pe = Steps(sem("norm_pe"), ["sum"])
        norm_act = Steps(sem("norm_act"), ["sq0", "sq1", "sq2", "sq3", "sq4", "sq5", "sq6", "sq7", "sqrt"])
        norm_dve = Steps(sem("norm_dve"), ["mean"])
        low_pe = Steps(sem("low_pe"), ["wa", "g", "vres"])
        low_act = Steps(sem("low_act"), ["wa", "g", "vres", "tanh"])
        low_dve = Steps(sem("low_dve"), ["shift"])
        prep_pe = Steps(sem("prep_pe"), ["z", "a", "g", "vres", "k", "kk", "r", "v"])
        prep_act = Steps(sem("prep_act"), ["z", "a", "g", "vres", "G", "k", "sq", "r", "norm", "v"])
        prep_dve = Steps(sem("prep_dve"), ["c", "kk", "kkmax", "r", "rkk", "a", "rbk", "v"])
        prep_pool = Steps(sem("prep_pool"), ["r"])
        pair_pe = Steps(sem("pair_pe"), ["tb", "tk"] + [f"gram{i}" for i in range(NCH)] + ["tv"]
                        + [n for lv in LEVELS for n in
                           [f"t{lv}_{x}" for x in range(3)] + (["bonus"] if lv == 2 else [])
                           + [f"nm{lv}_{x}" for x in range(3)]]
                        + [f"{s}{i}" for i in range(NCH) for s in "xuod" if (s, i) != ("d", NCH - 1)]
                        + ["mean", "var"])
        pair_act = Steps(sem("pair_act"), ["tb", "tk", "tv"] + [f"t{lv}_{x}" for lv in LEVELS for x in range(3)]
                         + [f"{s}{i}" for i in range(NCH) for s in ("u", "o")] + ["sq", "std"])
        pair_dve = Steps(sem("pair_dve"), ["gram0", "gram1", "one0", "gram2", "gram3", "one1", "gram4", "gram5", "one2", "bonus"]
                         + [f"nm{lv}_{x}" for lv in LEVELS for x in range(3)]
                         + [f"{s}{i}" for i in range(NCH) for s in "xs" if (s, i) != ("s", NCH - 1)]
                         + ["cen", "var", "y"])
        vf_in, vf_out = sem("vf_in"), sem("vf_out")
        pair_pool = Steps(sem("pair_pool"), ["ar"] + [f"lv{lv}_{x}" for lv in LEVELS for x in range(3)])
        merge_pe = Steps(sem("merge_pe"), ["p0", "g0", "p1", "g1"])
        merge_act = Steps(sem("merge_act"), ["g0", "g1"])
        merge_dve = Steps(sem("merge_dve"), ["m0", "m1"])
        merge_a_act = Steps(sem("merge_a_act"), ["p0", "g0", "p1", "g1"])
        merge_a_pool = Steps(sem("merge_a_pool"), ["m0", "m1"])
        pool_pe = Steps(sem("pool_pe"), [f"p{j}" for j in range(8)] + [f"y{j}" for j in range(8)])
        pool_act = Steps(sem("pool_act"), [f"p{j}" for j in range(8)] + [f"y{j}" for j in range(8)])
        pool_dve = Steps(sem("pool_dve"), [f"p{j}" for j in range(8)])
        lat_pe = Steps(sem("lat_pe"), ["cq0", "cq1", "ckv", "kidx", "kr", "qsum", "kvsum", "mean", "var", "kperm",
                                       "rperm", "q0", "q1", "q2", "q3", "qp0", "qp1", "qp2", "qp3", "w"])
        lat_act = Steps(sem("lat_act"), ["cq0", "cq1", "ckv", "kidx", "kr", "sq", "std", "var", "std2",
                                         "q0", "q1", "q2", "q3", "w"])
        lat_dve = Steps(sem("lat_dve"), ["means", "latents", "center", "var", "kidx", "ropes", "rope0", "rope1",
                                         "rope2", "rope3"])
        IDX = [(i, hd) for i in range(1, NCH) for hd in range(8)]
        idx_pe = Steps(sem("idx_pe"), [f"s{i}_{hd}" for i, hd in IDX])
        idx_act = Steps(sem("idx_act"), [f"s{i}_{hd}" for i, hd in IDX])
        idx_dve = Steps(sem("idx_dve"), [f"s{i}_{hd}" for i, hd in IDX])
        UNITS = [(hd, i) for hd in range(8) for i in range(NCH)]

        def unit_steps(now, later, last, inputs):
            names = []
            for n in range(len(UNITS) + 3):
                if n < len(UNITS):
                    hd, i = UNITS[n]
                    names += [f"{now}{i}_{hd}"] + ([f"{inputs[i]}{hd + 1}"] if hd < 7 and i in inputs else [])
                for d, kind in ((2, later), (3, last)):
                    if kind and 0 <= n - d < len(UNITS):
                        hd, i = UNITS[n - d]
                        names.append(f"{kind}{i}_{hd}")
            return names

        att_pe = Steps(sem("att_pe"), ["q0", "k0", "perm0", "v0"]
                       + unit_steps("s", "pt", "pv", {0: "q", 1: "k", 2: "perm", 3: "v"}))
        att_act = Steps(sem("att_act"), ["q0", "k0", "v0"] + unit_steps("e", "pt", "pv", {0: "q", 1: "k", 3: "v"}))
        dve_units = []
        for _n in range(len(UNITS) + 1):
            if _n < len(UNITS):
                _hd, _i = UNITS[_n]
                dve_units += [f"m{_i}_{_hd}"] + ([f"rope{_hd + 1}"] if _hd < 7 and _i == 2 else [])
            if _n >= 1:
                _hd, _i = UNITS[_n - 1]
                dve_units.append(f"n{_i}_{_hd}")
        att_dve = Steps(sem("att_dve"), ["kr", "rope0"] + dve_units)
        res_pe = Steps(sem("res_pe"), [f"o{s}" for s in range(4)])
        res_dve = Steps(sem("res_dve"), [f"h{s}" for s in range(4)])
        rt_pe = Steps(sem("rt_pe"), ["logits"] + [f"ut{i}" for i in range(NCH)] + ["oh", "start", "pos", "ct"]
                      + [f"su{j}" for j in range(KD)])
        rt_act = Steps(sem("rt_act"), ["ut0", "ut1", "ut2", "gexp", "ut3", "eexp", "ut4", "ut5", "pos", "ct"]
                       + [f"su{j}" for j in range(0, KD, 2)])
        rt_dve = Steps(sem("rt_dve"), ["gmax", "ediff", "oh", "rank", "pos", "take"] + [f"perm{i}" for i in range(NCH)]
                       + [f"su{j}" for j in range(1, KD, 2)])
        back_pe = Steps(sem("back_pe"), [f"yt{i}" for i in range(NCH)] + [f"h{j}" for j in range(KD)])
        back_act = Steps(sem("back_act"), [f"yt{i}" for i in range(NCH)])
        back_dve = Steps(sem("back_dve"), [f"h{j}" for j in range(KD)])
        grp_pe = Steps(sem("grp_pe"), [f"c{e}" for e in range(4)])
        grp_act = Steps(sem("grp_act"), [f"c{e}" for e in range(4)])
        grp_dve = Steps(sem("grp_dve"), [f"c{e}" for e in range(4)])
        exp_pe = Steps(sem("exp_pe"), ["a0", "b0", "a1", "b1"])
        exp_act = Steps(sem("exp_act"), ["t0", "t1"])
        exp_dve = Steps(sem("exp_dve"), ["h0", "h1"])
        dn_pe = Steps(sem("down_pe"), [f"o{s}" for s in range(4)])
        dn_dve = Steps(sem("down_dve"), [f"h{s}" for s in range(4)])
        out_ready = sem("out_ready")

        PE_STEPS = [norm_pe, low_pe, prep_pe, pair_pe, merge_pe, pool_pe, lat_pe, idx_pe, att_pe, res_pe, rt_pe, grp_pe,
                    exp_pe, dn_pe, back_pe]
        ACT_STEPS = [norm_act, low_act, prep_act, pair_act, merge_act, merge_a_act, pool_act, lat_act, idx_act, att_act, rt_act, grp_act,
                     exp_act, back_act]
        DVE_STEPS = [norm_dve, low_dve, prep_dve, pair_dve, merge_dve, pool_dve, lat_dve, idx_dve, att_dve, res_dve, rt_dve,
                     grp_dve, exp_dve, dn_dve, back_dve]

        t = area()
        n_sq, n_rs = t(KD, T), t(T)
        t = area()
        lr_wa, lr_g, lr_v = t(T), t(T), t(T)
        raw_r, raw_k, raw_v = t(T + 1), t(T + 1), t(T + 1)
        pr, pk, pv = t(T), t(T), t(TP)
        tz, ta, tv, pg, pg_now = t(T), t(T), t(T), t(T), t(T)
        sqk, cum, kk, kh, bonus = t(T), t(T), t(T), t(T), t(T)
        G, Gi, Gx, vfb = t(T), t(T), t(T), t(T)
        ar = t(2, TP)
        bb, kb_ = t(TP), t(TP)
        arh = t(4, TP)
        tm = t(3, NCH * P, rows=CH)
        state, xs, us = t(P), t(P), t(P)
        gend = t(NCH - 1)
        gr = t(2 * NCH, 4 * CH, rows=CH)
        half_w0, half_a0, half_v0 = t(8), t(8), t(8)
        lv_t = t(2 * NCH, CH, rows=CH)
        pairs_o, otmp = t(T), t(T)
        area_m = area(m[:, :, :].rearrange("p a b -> p (a b)"))
        inv_t = area_m(2 * NCH, CH, rows=CH)
        inv = area_m(2 * NCH, CH, rows=CH)
        lv_a = area_m(2 * NCH, CH, rows=CH)
        lv_as = [lv_a[:, 4 * x:4 * x + 4, :] for x in range(3)]
        lv_ts = [lv_t[:, 4 * x:4 * x + 4, :] for x in range(3)]
        t = area()
        g_tanh, g_tmp = t(2, T), t(2, T)
        t = area()
        p_raw, p_a, p_b, pooled = t(2, T), t(T), t(T), t(KD, T)
        t = area()
        cq, ckv, kidx, kr = t(2, T), t(T), t(T), t(T)
        kidx2 = t(2, T)
        qi = t(4, T)
        wtok = t(NCH, 8, rows=CH)
        sel = t(sum(tile_keys(i) for i in range(NCH)), rows=CH)
        lat_mark = t
        l_sq, l_tmp, l_tmp2, l_rs, l_rs2 = t(3, T), t(T), t(T), t(T), t(T)
        relu_b, top8 = t(2, T, rows=CH), t(8, rows=CH)
        qh, kh2, vh = t(2, T, rows=96), t(2, T, rows=96), t(2, NCH * 64, rows=CH)
        es, pts = t(3, T, rows=CH), t(2, T, rows=CH)
        rope_t = t(T)
        ma_p, ma_g, ma_s = t(2, T), t(2, T), t(2, T)
        mx, rs, ri = t(3, rows=CH), t(3, rows=CH), t(3, rows=CH)
        t = area()
        comb = t(NCH, 16, rows=CH)
        comb_t, comb_sel = t(T, rows=16), t(T, rows=16)
        comb_b, hid, e_tanh, e_tmp = t(4, T), t(8, T), t(2, T), t(2, T)
        lg = t(NCH, 20, rows=CH)
        r1, r2, r3, oh, oh1, oh2, ce = (t(NCH, 4, rows=CH) for _ in range(7))
        r16 = t(NCH, 16, rows=CH)
        s1, s2, s3, s4, s5 = (t(NCH, rows=CH) for _ in range(5))
        tok = t(NCH, D, rows=CH)
        take, give = t(NCH, T, rows=CH), t(NCH, T, rows=CH)
        place = t(T)
        place_tok = t(NCH, rows=CH)
        count1 = t(T)
        all1, oh_t, rank, place4 = t(T), t(T, rows=4), t(T, rows=4), t(T, rows=4)
        start4, start_row, most = t(1, rows=4), t(8, rows=1), t(1, rows=1)
        starts = ctx.enter_context(nc.sbuf_tensor("starts", [1, 8], mybir.dt.int32))
        narrow = ctx.enter_context(nc.sbuf_tensor("narrow", [1, 4], mybir.dt.int32))
        fits = ctx.enter_context(nc.sbuf_tensor("fits", [1, 1], mybir.dt.int32))

        def sel_of(i):
            o = sum(tile_keys(k) for k in range(i))
            return sel[0:tile_rows(i), o:o + tile_keys(i)]

        def n_parts(i):
            return -(-tile_keys(i) // 512)

        def scores(b, i):
            n = n_parts(i)
            return ps[0:tile_rows(i), b:b + n, 0:tile_keys(i) // n]

        def score_bank(i):
            return i % 2 if n_parts(i) == 1 else 2

        def parts(ap, i):
            return ap.rearrange("p (a b) -> p a b", a=n_parts(i))

        def by_width(eng, group):
            with eng.If(eng.value_load(fits[0:1, 0:1], min_val=0, max_val=1)):
                with eng.Fori(0, 4) as g:
                    with eng.If(eng.value_load(narrow[0:1, ds(g, 1)], min_val=0, max_val=1)):
                        group(g, GROUP_COLS[0])
                    with eng.Else():
                        group(g, GROUP_COLS[1])
            with eng.Else():
                with eng.Fori(0, 4) as g:
                    group(g, T)

        def first_col(eng, g, cols):
            if cols == T:
                return 0
            o = 4 * GROUP_COLS.index(cols)
            return eng.value_load(starts[0:1, ds(g + o, 1)], min_val=0, max_val=T - cols)

        def bank_cols(b, cols):
            return acc(b) if cols == T else ps[:, b, 0:cols]

        def first_cols(x, cols):
            return two(x) if cols == T else x[:, 0:cols]

        block = ctx.enter_context(nc.Block())

        @block.sync
        def _(sp):
            for j in range(KD):
                sp.dma_start(h[:, j, :], x_t[j]).then_inc(loaded, 16)
            sp.wait_ge(loaded, 16 * (KD + 1))
            for s in range(RING):
                sp.dma_start(ring[:, s, :], stream[s]).then_inc(w_full[s], 16)
            with sp.Fori(1, DEPTH * LAYER_ROUNDS) as n:
                for s in range(RING):
                    sp.wait_ge(w_free[s], n)
                    sp.dma_start(ring[:, s, :], stream[n * RING + s]).then_inc(w_full[s], 16)
            sp.wait_ge(out_ready, 1)
            for j in range(KD):
                sp.dma_start(out_t[j], u[:, j, N_META:]).then_inc(stored, 16)
            sp.wait_ge(stored, 16 * KD)

        @block.tensor
        def _(pe):
            mm = nc.tensor.matmul
            for S in PE_STEPS:
                pe.sem_inc(S.sem, len(S.names))

            def tile(s, rnd):
                pe.wait_ge(w_full[s], (rnd + 1) * 16)
                return ring[:, s, :]

            def project(s, rnd, src, bank, done):
                w = tile(s, rnd)
                for kb in range(KD):
                    for hf in range(2):
                        last = mm(ps[:, bank + hf, 0:HALF], w[:, kb * P:(kb + 1) * P],
                                  src[:, kb, hf * HALF:(hf + 1) * HALF], start=kb == 0, stop=kb == KD - 1)
                    if kb == 0 and used:
                        last.then_inc(w_free[used.pop()], 1)
                last.then_inc(done, 1)
                used.append(s)

            def let_go():
                pe.drain().then_inc(w_free[used.pop()], 1)

            def release(s, rnd=None):
                if used:
                    let_go()
                if rnd is not None:
                    pe.wait_ge(w_full[s], (rnd + 1) * 16)
                    alone(pe)
                pe.drain().then_inc(w_free[s], 1)

            used = []

            def halves(lhsT, rhs, bank, rows=slice(0, P), start=True, stop=True):
                for hf in range(2):
                    last = mm(ps[rows, bank + hf, 0:HALF], lhsT, rhs[:, hf * HALF:(hf + 1) * HALF],
                              start=start, stop=stop)
                return last

            def norm(turn, n=KD):
                for j in range(n):
                    pe.wait_ge(norm_act.sem, norm_act.at(turn, f"sq{j}"))
                    last = halves(ones, n_sq[:, j, :], 0, start=j == 0, stop=j == n - 1)
                last.then_inc(norm_pe.inc("sum"), 1)

            pe.wait_ge(loaded, 16 * (KD + 1))
            with pe.Fori(0, DEPTH) as l:
                rnd0 = l * LAYER_ROUNDS
                norm(l * 2)
                next_phase(pe, "pe", l)

                rnd = rnd0 + FIRST["lowrank"]
                project(0, rnd, u, 0, low_pe.inc("wa"))
                project(1, rnd, u, 2, low_pe.inc("g"))
                project(2, rnd, u, 4, low_pe.inc("vres"))
                release(3, rnd)
                next_phase(pe, "pe", l)

                def prepare(turn, rnd, first, last):
                    A = prep_act
                    for n in range(first, last):
                        if n < 4:
                            name, rw, src, b, free = (("z", slice(0, 64), lr_wa, 6, None), ("a", slice(64, 128), lr_wa, 6, "z"),
                                                      ("g", slice(0, P), lr_g, 6, "a"), ("vres", slice(0, 32), lr_v, 6, "g"))[n]
                            if n == 0:
                                tile(0, rnd)
                            if free:
                                pe.wait_ge(A.sem, A.at(turn, free))
                            halves(ring[rw, 0, n * P:(n + 1) * P], src[rw, :], b).then_inc(prep_pe.inc(name), 1)
                            if n == 3:
                                used.append(0)
                            continue
                        k, kb = (n - 4) // 8, (n - 4) % 8
                        name, free = (("k", "vres"), ("r", "k"), ("v", "r"))[k]
                        if kb == 0:
                            pe.wait_ge(A.sem, A.at(turn, free))
                            tile(1 + k, rnd)
                        for hf in range(2):
                            mm_ = mm(ps[:, 6 + hf, 0:HALF], ring[:, 1 + k, kb * P:(kb + 1) * P],
                                     u[:, kb, hf * HALF:(hf + 1) * HALF], start=kb == 0, stop=kb == 7)
                            if kb == 0 and used:
                                mm_.then_inc(w_free[used.pop()], 1)
                        if kb == 7:
                            mm_.then_inc(prep_pe.inc(name), 1)
                            used.append(1 + k)

                def key_norm(turn):
                    pe.wait_ge(prep_act.sem, prep_act.at(turn, "sq"))
                    halves(headones, sqk, 4).then_inc(prep_pe.inc("kk"), 1)

                def pair(q, more):
                    it, rnd = l * NPAIR + q, rnd0 + FIRST["pairs"] + q
                    S, A, V = pair_pe, pair_act, pair_dve

                    def act_did(name):
                        pe.wait_ge(A.sem, A.at(it, name))

                    def dve_did(name):
                        pe.wait_ge(V.sem, V.at(it, name))

                    pe.wait_ge(prep_dve.sem, prep_dve.at(it, "rbk"))
                    def token_major(name, src, bank):
                        for i in range(NCH):
                            last = nc.tensor.transpose(ps[0:CH, bank + i // 4, (i % 4) * P:(i % 4 + 1) * P],
                                                       src[:, i * CH:(i + 1) * CH], ident)
                        last.then_inc(S.inc(name), 1)

                    token_major("tb", bb, 4)
                    pe.wait_ge(prep_act.sem, prep_act.at(it, "v"))
                    token_major("tk", kb_, 6)
                    pe.wait_ge(prep_pool.sem, prep_pool.at(it, "r"))
                    pe.wait_ge(prep_dve.sem, prep_dve.at(it, "a"))
                    for i in range(NCH):
                        if i == 2:
                            pe.wait_ge(V.sem, V.before(it, "var"))
                        elif i < 2:
                            act_did(("tb", "tk")[i])
                        elif i >= 4:
                            dve_did(f"gram{i - 4}")
                        b = GRAM_BANKS[i % 4]
                        cc = slice(i * CH, (i + 1) * CH)
                        for hd in range(2):
                            a_r = arh[:, 2 * hd:2 * hd + 2, cc]
                            mm(ps[0:CH, b + hd, 0:2 * CH], bb[:, cc], a_r, start=True, stop=True)
                            mm(ps[0:CH, b + hd, 2 * CH:4 * CH], kb_[:, cc], a_r, start=True, stop=True)
                            last = mm(ps[0:CH, b + hd, 4 * CH:5 * CH], arh[:, 2 * hd, cc], bb[:, cc], start=True, stop=True)
                        last.then_inc(S.inc(f"gram{i}"), 1)
                    pe.wait_ge(prep_dve.sem, prep_dve.at(it, "v"))
                    dve_did("gram2")
                    token_major("tv", pv, 2)
                    gap_units = [0, 0, 1, 2, 3, 4, 8, 12, 12, 14, 16, 16, 16]

                    def fill(upto, first):
                        if more:
                            prepare(it + 1, rnd + 1, first, upto)

                    def between(gap):
                        if gap == 0 and more:
                            key_norm(it + 1)
                        elif gap > 0:
                            fill(min(16 + gap, 28), min(15 + gap, 28))

                    for n, lv in enumerate(LEVELS):
                        for x in range(3):
                            pe.wait_ge(pair_pool.sem, pair_pool.at(it, f"lv{lv}_{x}"))
                            if n == 0:
                                dve_did(("gram3", "one1", "one2")[x])
                            else:
                                dve_did(f"nm{LEVELS[n - 1]}_{x}")
                            if x == 2:
                                act_did(f"t{lv}_0")
                            for k in range(4):
                                last = mm(ps[0:CH, x % 2, k * CH:(k + 1) * CH], lv_as[x][:, k, :],
                                          inv[:, 4 * x + k, :], start=True, stop=True)
                            last.then_inc(S.inc(f"t{lv}_{x}"), 1)
                        if n == 0:
                            halves(headones, tz, 6).then_inc(S.inc("bonus"), 1)
                        fill(gap_units[2 * n + 1], gap_units[2 * n])
                        for x in range(3):
                            act_did(f"t{lv}_{x}")
                            if x != 1:
                                if x == 2:
                                    dve_did(f"nm{lv}_0")
                                elif n > 0:
                                    dve_did(f"nm{LEVELS[n - 1]}_2")
                            for k in range(4):
                                last = mm(ps[0:CH, 2 + x % 2, k * CH:(k + 1) * CH], lv_ts[x][:, k, :],
                                          inv_t[:, 4 * x + k, :], start=True, stop=True)
                            if lv != LEVELS[-1]:
                                for k in range(4):
                                    last = mm(ps[0:CH, 4 + x % 2, k * CH:(k + 1) * CH], inv_t[:, 4 * x + k, :],
                                              lv_ts[x][:, k, :], start=True, stop=True)
                            last.then_inc(S.inc(f"nm{lv}_{x}"), 1)
                        if n == 0:
                            dve_did("bonus")
                        fill(gap_units[2 * n + 2], gap_units[2 * n + 1])
                    for i in range(NCH):
                        cc = slice(i * CH, (i + 1) * CH)
                        tmv = tm[:, 2, i * P:(i + 1) * P]
                        dve_did(f"nm{LEVELS[-1]}_2" if i == 0 else f"s{i - 1}")
                        mm(ps[0:CH, 0, 0:P], ar[:, 0, cc], state, start=True, stop=False, skip_group_check=True)
                        for hd in range(2):
                            last = mm(ps[0:CH, 0, 64 * hd:64 * hd + 64], gr[:, 2 * i + hd, 2 * CH:3 * CH],
                                      tmv[:, 64 * hd:64 * hd + 64], start=False, stop=hd == 1, skip_group_check=True)
                        last.then_inc(S.inc(f"x{i}"), 1)
                        between(3 * i)
                        dve_did(f"x{i}")
                        for hd in range(2):
                            last = mm(ps[0:CH, 1, 64 * hd:64 * hd + 64], inv_t[:, 2 * i + hd, :],
                                      xs[0:CH, 64 * hd:64 * hd + 64], start=True, stop=True)
                        last.then_inc(S.inc(f"u{i}"), 1)
                        between(3 * i + 1)
                        act_did(f"u{i}")
                        if i >= 1:
                            act_did(f"o{i - 1}")
                        tr = tile_rows(i)
                        c2 = slice(i * CH, i * CH + tr)
                        mm(ps[:, 2, 0:tr], state, ar[:, 1, c2], start=True, stop=False, skip_group_check=True)
                        for hd in range(2):
                            rw = slice(64 * hd, 64 * hd + 64)
                            mm(ps[rw, 2, 0:tr], us[0:CH, rw], gr[:, 2 * i + hd, CH:CH + tr],
                               start=False, stop=False, skip_group_check=True)
                            last = mm(ps[rw, 2, 0:tr], tmv[:, rw], gr[:, 2 * i + hd, 3 * CH:3 * CH + tr],
                                      start=False, stop=True, skip_group_check=True)
                        last.then_inc(S.inc(f"o{i}"), 1)
                        if i < NCH - 1:
                            mm(ps[:, 3, 0:P], tm[:, 0, i * P:(i + 1) * P], us[0:CH, :], start=True, stop=False)
                            mm(ps[:, 3, 0:P], tm[:, 1, i * P:(i + 1) * P], tmv, start=False, stop=True
                               ).then_inc(S.inc(f"d{i}"), 1)
                        between(3 * i + 2)
                    act_did(f"o{NCH - 1}")
                    halves(headones, pairs_o, 0).then_inc(S.inc("mean"), 1)
                    if more:
                        let_go()
                    act_did("sq")
                    halves(headones, otmp, 2).then_inc(S.inc("var"), 1)

                rnd = rnd0 + FIRST["pairs"]
                prepare(l * NPAIR, rnd, 0, 12)
                key_norm(l * NPAIR)
                prepare(l * NPAIR, rnd, 12, 28)
                let_go()
                with pe.Fori(0, NPAIR - 1) as q:
                    pair(q, True)
                pair(NPAIR - 1, False)
                next_phase(pe, "pe", l)

                def merge(phase, k):
                    with pe.Fori(0, 4) as q:
                        it, rnd = l * 12 + 4 * k + q, rnd0 + FIRST[phase] + q
                        for n in range(2):
                            if k == 1:
                                pe.wait_ge(merge_a_act.sem, merge_a_act.before(l * 4 + q, f"g{n}"))
                            else:
                                pe.wait_ge(merge_dve.sem, merge_dve.before(l * 8 + 2 * k + q, f"m{n}"))
                            project(2 * n, rnd, y, 4 * n, merge_pe.inc(f"p{n}"))
                            project(2 * n + 1, rnd, u, 4 * n + 2, merge_pe.inc(f"g{n}"))
                        let_go()
                    next_phase(pe, "pe", l)

                merge("merge_b", 0)

                for j in range(8):
                    if j >= 4:
                        pe.wait_ge(pool_act.sem, pool_act.at(l, f"p{j - 4}"))
                    project(j % 4, rnd0 + FIRST["pool"] + j // 4, u, 2 * (j % 4), pool_pe.inc(f"p{j}"))
                let_go()
                rnd = rnd0 + FIRST["pool"] + 2
                for j in range(8):
                    g, nb = j // 2, j % 2
                    w = tile(g // 2, rnd)
                    pe.wait_ge(pool_act.sem, pool_act.at(l, f"p{j + 4}" if j < 4 else f"y{j - 4}"))
                    for kb in range(2):
                        pe.wait_ge(pool_dve.sem, pool_dve.at(l, f"p{2 * g + kb}"))
                        blk = (g % 2) * 4 + nb * 2 + kb
                        last = halves(w[:, blk * P:(blk + 1) * P], pooled[:, 2 * g + kb, :], 2 * (j % 4),
                                      start=kb == 0, stop=kb == 1)
                    last.then_inc(pool_pe.inc(f"y{j}"), 1)
                    if j in (3, 7):
                        release(j // 4)
                release(2, rnd)
                release(3, rnd)
                next_phase(pe, "pe", l)

                S, A, V = lat_pe, lat_act, lat_dve

                def act_did(name):
                    pe.wait_ge(A.sem, A.at(l, name))

                def dve_did(name):
                    pe.wait_ge(V.sem, V.at(l, name))

                rnd = rnd0 + FIRST["dsa_in"]
                for s, name in enumerate(("cq0", "cq1", "ckv", "kidx")):
                    project(s, rnd, u, 2 * s, S.inc(name))
                act_did("cq0")
                project(0, rnd + 1, u, 0, S.inc("kr"))
                let_go()
                act_did("sq")
                act_did("cq1")
                halves(ones, l_sq[:, 0, :], 2, start=True, stop=False)
                halves(ones, l_sq[:, 1, :], 2, start=False, stop=True).then_inc(S.inc("qsum"), 1)
                act_did("ckv")
                halves(ones, l_sq[:, 2, :], 4).then_inc(S.inc("kvsum"), 1)
                act_did("kidx")
                halves(headones, kidx, 6).then_inc(S.inc("mean"), 1)
                act_did("var")
                halves(headones, l_sq[:, 0, :], 6).then_inc(S.inc("var"), 1)
                dve_did("kidx")
                halves(perm, kidx, 2).then_inc(S.inc("kperm"), 1)
                act_did("kr")
                halves(perm, kr, 4).then_inc(S.inc("rperm"), 1)
                w = tile(1, rnd + 1)
                for j in range(4):
                    dve_did("ropes")
                    b = 2 * j
                    for kb in range(2):
                        blk = 2 * j + kb
                        last = halves(w[:, blk * P:(blk + 1) * P], cq[:, kb, :], b, start=kb == 0, stop=kb == 1)
                    last.then_inc(S.inc(f"q{j}"), 1)
                release(1)
                release(2, rnd + 1)
                release(3, rnd + 1)
                for j in range(4):
                    act_did(f"q{j}")
                    halves(perm, qi[:, j, :], 2 * j).then_inc(S.inc(f"qp{j}"), 1)
                dve_did("rope0")
                alone(pe)
                for i in range(NCH):
                    last = nc.tensor.transpose(ps[0:tile_rows(i), 0, i * 8:(i + 1) * 8],
                                               kr[96:104, i * CH:tile_keys(i)], ident[96:104, 96:104])
                last.then_inc(S.inc("w"), 1)
                next_phase(pe, "pe", l)

                for n, (i, hd) in enumerate(IDX):
                    if n >= 4:
                        j, g = IDX[n - 4]
                        pe.wait_ge(idx_act.sem, idx_act.at(l, f"s{j}_{g}"))
                        if tile_rows(i) < CH:
                            alone(pe)
                    b = 2 * (n % 4)
                    wd = tile_keys(i) // n_parts(i)
                    for k in range(n_parts(i)):
                        last = mm(ps[0:tile_rows(i), b + k, 0:wd], qi[:, hd // 2, i * CH:tile_keys(i)],
                                  kidx2[:, hd % 2, k * wd:(k + 1) * wd], start=True, stop=True)
                    last.then_inc(idx_pe.inc(f"s{i}_{hd}"), 1)
                next_phase(pe, "pe", l)

                merge("merge_a", 1)

                with pe.Fori(0, 2) as q:
                    it, rnd = l * 2 + q, rnd0 + FIRST["heads"] + q
                    S, A, V = att_pe, att_act, att_dve

                    def act_did(name):
                        pe.wait_ge(A.sem, A.at(it, name))

                    def dve_did(name):
                        pe.wait_ge(V.sem, V.at(it, name))

                    def inputs(hd, part):
                        b4, hh, z = hd // 4, hd % 4, hd % 2
                        wq, wkv = ring[:, 2 * b4, :], ring[:, 2 * b4 + 1, :]
                        if part == 0:
                            if hh == 0:
                                tile(2 * b4, rnd)
                                tile(2 * b4 + 1, rnd)
                            if hd == 0:
                                pe.wait_ge(A.sem, A.before(it, "v7"))
                                pe.wait_ge(V.sem, V.before(it, "m5_7"))
                            elif hd >= 2:
                                dve_did(f"m5_{hd - 2}")
                            for kb in range(2):
                                blk = 2 * hh + kb
                                last = halves(wq[:, blk * P:blk * P + 96], cq[:, kb, :], 2, rows=slice(0, 96),
                                              start=kb == 0, stop=kb == 1)
                            last.then_inc(S.inc(f"q{hd}"), 1)
                        if part == 1:
                            act_did(f"q{hd}")
                            halves(wkv[:, hh * 64:hh * 64 + 64], ckv, 2, rows=slice(0, 64)).then_inc(S.inc(f"k{hd}"), 1)
                        if part == 2:
                            act_did(f"k{hd}")
                            alone(pe)
                            halves(perm[64:96, 64:96], qh[64:96, z, :], 2, rows=slice(64, 96)
                                   ).then_inc(S.inc(f"perm{hd}"), 1)
                        if part == 3:
                            dve_did(f"rope{hd}")
                            for i in range(NCH):
                                last = mm(ps[0:tile_rows(i), 2, i * 64:i * 64 + 64], ckv[:, i * CH:tile_keys(i)],
                                          wkv[:, 256 + hh * 64:256 + hh * 64 + 64], start=True, stop=True)
                            last.then_inc(S.inc(f"v{hd}"), 1)
                            if hh == 3:
                                release(2 * b4)
                                release(2 * b4 + 1)

                    for part in range(4):
                        inputs(0, part)
                    for n in range(len(UNITS) + 3):
                        if n < len(UNITS):
                            hd, i = UNITS[n]
                            if i == 0:
                                dve_did(f"rope{hd}")
                                act_did(f"v{hd}")
                            if i < NCH - 1 and n >= 2:
                                g, j = UNITS[n - 2]
                                dve_did(f"m{j}_{g}")
                            if i == NCH - 1 and hd < 7:
                                act_did(f"v{hd + 1}")
                            if tile_rows(i) < CH:
                                alone(pe)
                            wd, z = tile_keys(i) // n_parts(i), hd % 2
                            for k in range(n_parts(i)):
                                last = mm(ps[0:tile_rows(i), score_bank(i) + k, 0:wd], qh[:, z, i * CH:tile_keys(i)],
                                          kh2[:, z, k * wd:(k + 1) * wd], start=True, stop=True)
                            last.then_inc(S.inc(f"s{i}_{hd}"), 1)
                            if hd < 7 and i < 4:
                                inputs(hd + 1, i)
                        if 0 <= n - 2 < len(UNITS):
                            hd, i = UNITS[n - 2]
                            dve_did(f"n{i}_{hd}")
                            b, tr = 4 + 2 * (i % 2), tile_rows(i)
                            if tr < CH:
                                alone(pe)
                            for k in range(i + 1):
                                last = nc.tensor.transpose(ps[0:tile_rows(k), b, k * tr:(k + 1) * tr],
                                                           es[0:tr, (n - 2) % 3, k * CH:tile_keys(k)],
                                                           ident[0:tr, 0:tr])
                            last.then_inc(S.inc(f"pt{i}_{hd}"), 1)
                        if n >= 3:
                            hd, i = UNITS[n - 3]
                            z = hd % 2
                            act_did(f"pt{i}_{hd}")
                            if n >= 5:
                                g, j = UNITS[n - 5]
                                act_did(f"pv{j}_{g}")
                            rw = slice(64 * z, 64 * z + 64)
                            b, tr = 5 + 2 * (i % 2), tile_rows(i)
                            for k in range(i + 1):
                                last = mm(ps[rw, b, 0:tr], vh[0:tile_rows(k), z, k * 64:k * 64 + 64],
                                          pts[0:tile_rows(k), i % 2, k * tr:(k + 1) * tr], start=k == 0, stop=k == i)
                            last.then_inc(S.inc(f"pv{i}_{hd}"), 1)
                next_phase(pe, "pe", l)
                merge("merge_c", 2)

                with pe.Fori(0, 2) as q:
                    it, rnd = l * 2 + q, rnd0 + FIRST["out"] + q
                    for s in range(4):
                        pe.wait_ge(res_dve.sem, res_dve.before(it, f"h{s}"))
                        project(s, rnd, m, 2 * s, res_pe.inc(f"o{s}"))
                    let_go()
                next_phase(pe, "pe", l)
                norm(l * 2 + 1)
                next_phase(pe, "pe", l)

                S, A, V = rt_pe, rt_act, rt_dve

                def act_did(name):
                    pe.wait_ge(A.sem, A.at(l, name))

                def dve_did(name):
                    pe.wait_ge(V.sem, V.at(l, name))

                o = PARAMS["router"][0]
                for i in range(NCH):
                    for kb in range(KD):
                        last = mm(ps[0:CH, 0, i * 20:i * 20 + 20], u[:, kb, window(i):window(i) + CH],
                                  par[:, o + kb * 20:o + kb * 20 + 20], start=kb == 0, stop=kb == KD - 1)
                last.then_inc(S.inc("logits"), 1)
                for i in range(NCH):
                    if i >= 3:
                        act_did(f"ut{i - 3}")
                    for j in range(KD):
                        last = nc.tensor.transpose(ps[0:CH, 2 + 2 * (i % 3) + j // 4, (j % 4) * P:(j % 4 + 1) * P],
                                                   u[:, j, window(i):window(i) + CH], ident)
                    last.then_inc(S.inc(f"ut{i}"), 1)
                dve_did("oh")
                for i in range(NCH):
                    last = nc.tensor.transpose(ps[0:4, i // 5, (i % 5) * CH:(i % 5 + 1) * CH], oh[:, i, :],
                                               ident[0:CH, 0:CH])
                last.then_inc(S.inc("oh"), 1)
                dve_did("rank")
                alone(pe)
                below = c("grams", 4)[:, 0:4]
                mm(ps[0:4, 0, 0:1], below, rank[:, T - 1:T], start=True, stop=True)
                mm(ps[0:1, 0, 4:8], rank[:, T - 1:T], below, start=True, stop=True)
                mm(ps[0:1, 0, 8:12], rank[:, T - 1:T], ident[0:4, 0:4], start=True, stop=True
                   ).then_inc(S.inc("start"), 1)
                dve_did("pos")
                act_did("ut3")
                alone(pe)
                halves(ones[0:4, :], place4, 2)
                for i in range(NCH):
                    last = mm(ps[0:CH, 1, i:i + 1], place4[:, window(i):window(i) + CH], ones[0:4, 0:1],
                              start=True, stop=True)
                last.then_inc(S.inc("pos"), 1)
                act_did("ut4")
                for i in range(NCH):
                    dve_did(f"perm{i}")
                    last = halves(comb[:, i, :], take[:, i, :], 4, rows=slice(0, 16), start=i == 0, stop=i == NCH - 1)
                last.then_inc(S.inc("ct"), 1)
                for j in range(KD):
                    if j < 4:
                        act_did(("ut5", "ut5", "pos", "ct")[j])
                    elif j % 2 == 0:
                        act_did(f"su{j - 4}")
                    else:
                        dve_did(f"su{j - 4}")
                    for i in range(NCH):
                        last = halves(tok[:, i, j * P:(j + 1) * P], take[:, i, :], (6, 0, 2, 4)[j % 4],
                                      start=i == 0, stop=i == NCH - 1)
                    last.then_inc(S.inc(f"su{j}"), 1)
                next_phase(pe, "pe", l)

                def group(g, cols):
                    gi = l * 4 + g
                    off = first_col(pe, g, cols)

                    def product(s, rnd, src, at, bank, done):
                        if cols == T:
                            project(s, rnd, src, bank, done)
                            return
                        w = tile(s, rnd)
                        alone(pe)
                        for kb in range(KD):
                            last = mm(ps[:, bank, 0:cols], w[:, kb * P:(kb + 1) * P],
                                      src[:, kb, ds(at, cols)] if at is not None else src[:, kb, 0:cols],
                                      start=kb == 0, stop=kb == KD - 1)
                            if kb == 0 and used:
                                last.then_inc(w_free[used.pop()], 1)
                        last.then_inc(done, 1)
                        used.append(s)

                    for e in range(4):
                        pe.wait_ge(grp_dve.sem, grp_dve.at(gi, f"c{e}"))
                        if e == 0:
                            pe.wait_ge(dn_dve.sem, dn_dve.before(gi * 2, "h3"))
                        if cols == T:
                            last = halves(ones[0:16, :], comb_sel, 2 * e)
                        else:
                            last = mm(ps[:, 2 * e, 0:cols], ones[0:16, :], comb_sel[:, 0:cols],
                                      start=True, stop=True)
                        last.then_inc(grp_pe.inc(f"c{e}"), 1)
                        pe.wait_ge(grp_act.sem, grp_act.at(gi, f"c{e}"))
                    alone(pe)
                    with pe.Fori(0, 4) as e:
                        it, rnd = gi * 4 + e, rnd0 + FIRST["moe"] + g * 6 + e
                        for n in range(2):
                            pe.wait_ge(exp_dve.sem, exp_dve.before(it, f"h{n}"))
                            product(2 * n, rnd, u, off, 4 * n, exp_pe.inc(f"a{n}"))
                            product(2 * n + 1, rnd, u, off, 4 * n + 2, exp_pe.inc(f"b{n}"))
                        let_go()
                    pe.wait_ge(exp_dve.sem, exp_dve.at(gi * 4 + 3, "h1"))
                    alone(pe)
                    with pe.Fori(0, 2) as q:
                        it, rnd = gi * 2 + q, rnd0 + FIRST["moe"] + g * 6 + 4 + q
                        for s in range(4):
                            pe.wait_ge(dn_dve.sem, dn_dve.before(it, f"h{s}"))
                            product(s, rnd, hid, None, 2 * s, dn_pe.inc(f"o{s}"))
                        let_go()

                by_width(pe, group)
                next_phase(pe, "pe", l)

                for i in range(NCH):
                    if i >= 4:
                        pe.wait_ge(back_act.sem, back_act.at(l, f"yt{i - 4}"))
                        alone(pe)
                    tr = tile_rows(i)
                    for j in range(KD):
                        last = nc.tensor.transpose(ps[0:tr, 2 * (i % 4) + j // 4, (j % 4) * P:(j % 4 + 1) * P],
                                                   y[:, j, i * CH:i * CH + tr], ident)
                    last.then_inc(back_pe.inc(f"yt{i}"), 1)
                for j in range(KD):
                    if j < 4:
                        pe.wait_ge(back_act.sem, back_act.at(l, f"yt{NCH - 1}"))
                    else:
                        pe.wait_ge(back_dve.sem, back_dve.at(l, f"h{j - 4}"))
                    for i in range(NCH):
                        tr = tile_rows(i)
                        last = halves(tok[0:tr, i, j * P:(j + 1) * P], give[0:tr, i, :], 2 * (j % 4),
                                      start=i == 0, stop=i == NCH - 1)
                    last.then_inc(back_pe.inc(f"h{j}"), 1)
                next_phase(pe, "pe", l)
            norm(DEPTH * 2)

        @block.scalar
        def _(act):
            A_ = nc.scalar.activation
            act.dma_start(cst[:, :], consts).then_inc(loaded, 16)
            for S in ACT_STEPS:
                act.sem_inc(S.sem, len(S.names))
            act.wait_ge(loaded, 16 * (KD + 1))

            def norm(turn):
                for j in range(KD):
                    A_(n_sq[:, j, :], h[:, j, :], ACT.Square).then_inc(norm_act.inc(f"sq{j}"), 1)
                act.wait_ge(norm_dve.sem, norm_dve.at(turn, "mean"))
                A_(n_rs, n_rs, ACT.Sqrt).then_inc(norm_act.inc("sqrt"), 1)

            with act.Fori(0, DEPTH) as l:
                act.dma_start(par[:, :], params[l]).then_inc(par_full, 16)
                norm(l * 2)
                next_phase(act, "act", l)

                for name, dst, b in (("wa", raw_r, 0), ("g", raw_k, 2), ("vres", raw_v, 4)):
                    act.wait_ge(low_pe.sem, low_pe.at(l, name))
                    A_(two(dst[:, 1:]), acc(b), ACT.Copy).then_inc(low_act.inc(name), 1)
                act.wait_ge(low_dve.sem, low_dve.at(l, "shift"))
                A_(lr_wa[0:64, :], lr_wa[0:64, :], ACT.Tanh)
                A_(lr_g, lr_g, ACT.Tanh, scale=0.5).then_inc(low_act.inc("tanh"), 1)
                next_phase(act, "act", l)

                def evacuate(turn, q, *names):
                    for name in names:
                        act.wait_ge(prep_pe.sem, prep_pe.at(turn, name))
                        if name == "z":
                            last = A_(two(tz), acc(6), ACT.Tanh, bias=col(half_w0, q), scale=0.5)
                        elif name == "a":
                            last = A_(two(ta), acc(6), ACT.Tanh, bias=col(half_a0, q), scale=0.5)
                        elif name == "vres":
                            last = A_(two(tv), acc(6), ACT.Tanh, bias=col(half_v0, q), scale=0.5)
                        else:
                            dst = {"g": pg, "r": raw_r[:, 1:], "k": raw_k[:, 1:], "v": raw_v[:, 1:]}[name]
                            last = A_(two(dst), acc(6), ACT.Copy)
                        last.then_inc(prep_act.inc(name), 1)

                def decays(turn):
                    act.wait_ge(prep_dve.sem, prep_dve.at(turn, "c"))
                    A_(G, cum, ACT.Exp)
                    A_(Gi, cum, ACT.Exp, scale=-1.0)
                    A_(Gx, Gx, ACT.Exp).then_inc(prep_act.inc("G"), 1)

                def key_squares(turn):
                    act.wait_ge(prep_dve.sem, prep_dve.at(turn, "kk"))
                    A_(sqk, kk, ACT.Square).then_inc(prep_act.inc("sq"), 1)

                def key_norm(turn):
                    act.wait_ge(prep_dve.sem, prep_dve.at(turn, "kkmax"))
                    A_(sqk, sqk, ACT.Sqrt).then_inc(prep_act.inc("norm"), 1)

                def pair(q, more):
                    it = l * NPAIR + q
                    S, E, V = pair_act, pair_pe, pair_dve

                    def pe_did(name):
                        act.wait_ge(E.sem, E.at(it, name))

                    for k, (name, b) in enumerate((("tb", 4), ("tk", 6), ("tv", 2))):
                        pe_did(name)
                        A_(tm[:, k, 0:4 * P], ps[0:CH, b, 0:4 * P], ACT.Copy)
                        A_(tm[:, k, 4 * P:6 * P], ps[0:CH, b + 1, 0:2 * P], ACT.Copy).then_inc(S.inc(name), 1)
                    for lv in LEVELS:
                        if more:
                            evacuate(it + 1, q + 1, *{4: ("z",), 8: ("g",)}.get(lv, ()))
                        for x in range(3):
                            pe_did(f"t{lv}_{x}")
                            A_(lv_ts[x], ps[0:CH, x % 2, 0:4 * CH].rearrange("p (a b) -> p a b", a=4), ACT.Copy
                               ).then_inc(S.inc(f"t{lv}_{x}"), 1)
                        if more:
                            if lv == 16:
                                decays(it + 1)
                            evacuate(it + 1, q + 1, *{4: ("a",), 8: ("vres",), 32: ("k",)}.get(lv, ()))
                            if lv == 32:
                                key_squares(it + 1)
                    for i in range(NCH):
                        pe_did(f"u{i}")
                        if i >= 1:
                            pe_did(f"d{i - 1}")
                        A_(us[0:CH, :], ps[0:CH, 1, 0:P], ACT.Copy).then_inc(S.inc(f"u{i}"), 1)
                        pe_did(f"o{i}")
                        tr = tile_rows(i)
                        A_(pairs_o[:, i * CH:i * CH + tr], ps[:, 2, 0:tr], ACT.Copy).then_inc(S.inc(f"o{i}"), 1)
                        if more and i == 1:
                            evacuate(it + 1, q + 1, "r")
                            key_norm(it + 1)
                        if more and i == 4:
                            evacuate(it + 1, q + 1, "v")
                    act.wait_ge(V.sem, V.at(it, "cen"))
                    A_(otmp, pairs_o, ACT.Square).then_inc(S.inc("sq"), 1)
                    act.wait_ge(V.sem, V.at(it, "var"))
                    A_(otmp, otmp, ACT.Sqrt).then_inc(S.inc("std"), 1)

                def col(ap, q):
                    return ap[:, q:q + 1] if isinstance(q, int) else ap[:, ds(q, 1)]

                evacuate(l * NPAIR, 0, "z", "a", "g", "vres")
                decays(l * NPAIR)
                evacuate(l * NPAIR, 0, "k")
                key_squares(l * NPAIR)
                evacuate(l * NPAIR, 0, "r")
                key_norm(l * NPAIR)
                evacuate(l * NPAIR, 0, "v")
                with act.Fori(0, NPAIR - 1) as q:
                    pair(q, True)
                pair(NPAIR - 1, False)
                next_phase(act, "act", l)

                def merge(k):
                    with act.Fori(0, 4) as q:
                        it = l * 12 + 4 * k + q
                        for n in range(2):
                            if k == 1:
                                act.wait_ge(merge_a_pool.sem, merge_a_pool.before(l * 4 + q, f"m{n}"))
                                act.wait_ge(merge_pe.sem, merge_pe.at(it, f"p{n}"))
                                A_(two(ma_p[:, n, :]), acc(4 * n), ACT.Copy, scale=0.5
                                   ).then_inc(merge_a_act.inc(f"p{n}"), 1)
                                act.wait_ge(merge_pe.sem, merge_pe.at(it, f"g{n}"))
                                A_(two(ma_g[:, n, :]), acc(4 * n + 2), ACT.Tanh, scale=0.5
                                   ).then_inc(merge_a_act.inc(f"g{n}"), 1)
                                continue
                            act.wait_ge(merge_dve.sem, merge_dve.before(l * 8 + 2 * k + q, f"m{n}"))
                            act.wait_ge(merge_pe.sem, merge_pe.at(it, f"g{n}"))
                            A_(two(g_tanh[:, n, :]), acc(4 * n + 2), ACT.Tanh, scale=0.5
                               ).then_inc(merge_act.inc(f"g{n}"), 1)
                    next_phase(act, "act", l)

                merge(0)
                for j in range(8):
                    act.wait_ge(pool_pe.sem, pool_pe.at(l, f"p{j}"))
                    if j >= 2:
                        act.wait_ge(pool_dve.sem, pool_dve.at(l, f"p{j - 2}"))
                    A_(two(p_raw[:, j % 2, :]), acc(2 * (j % 4)), ACT.Copy).then_inc(pool_act.inc(f"p{j}"), 1)
                for j in range(8):
                    act.wait_ge(pool_pe.sem, pool_pe.at(l, f"y{j}"))
                    A_(two(y[:, j, :]), acc(2 * (j % 4)), ACT.Copy, scale=pc("pool_scale", j)
                       ).then_inc(pool_act.inc(f"y{j}"), 1)
                next_phase(act, "act", l)

                def pe_did(name):
                    act.wait_ge(lat_pe.sem, lat_pe.at(l, name))

                def dve_did(name):
                    act.wait_ge(lat_dve.sem, lat_dve.at(l, name))
                S = lat_act
                for name, dst, b in (("cq0", cq[:, 0, :], 0), ("cq1", cq[:, 1, :], 2), ("ckv", ckv, 4),
                                     ("kidx", kidx, 6), ("kr", kr, 0)):
                    pe_did(name)
                    A_(two(dst), acc(b), ACT.Copy).then_inc(S.inc(name), 1)
                act.drain()
                A_(l_sq[:, 0:2, :], cq, ACT.Square)
                A_(l_sq[:, 2, :], ckv, ACT.Square).then_inc(S.inc("sq"), 1)
                dve_did("means")
                A_(l_rs, l_rs, ACT.Sqrt)
                A_(l_rs2, l_rs2, ACT.Sqrt).then_inc(S.inc("std"), 1)
                dve_did("center")
                pe_did("qsum")
                A_(l_sq[:, 0, :], kidx, ACT.Square).then_inc(S.inc("var"), 1)
                dve_did("var")
                A_(l_tmp, l_tmp, ACT.Sqrt).then_inc(S.inc("std2"), 1)
                for j in range(4):
                    pe_did(f"q{j}")
                    A_(two(qi[:, j, :]), acc(2 * j), ACT.Copy).then_inc(S.inc(f"q{j}"), 1)
                pe_did("w")
                A_(wtok[:, 0:NCH - 1, :], ps[0:CH, 0, 0:8 * (NCH - 1)].rearrange("p (a b) -> p a b", a=NCH - 1),
                   ACT.Copy, scale=IDX_SCALE)
                tr = tile_rows(NCH - 1)
                A_(wtok[0:tr, NCH - 1, :], ps[0:tr, 0, 8 * (NCH - 1):8 * NCH], ACT.Copy, scale=IDX_SCALE
                   ).then_inc(S.inc("w"), 1)
                next_phase(act, "act", l)

                for n, (i, hd) in enumerate(IDX):
                    act.wait_ge(idx_pe.sem, idx_pe.at(l, f"s{i}_{hd}"))
                    if n >= 2:
                        j, g = IDX[n - 2]
                        act.wait_ge(idx_dve.sem, idx_dve.at(l, f"s{j}_{g}"))
                    b, z, wd = 2 * (n % 4), n % 2, tile_keys(i)
                    A_(parts(relu_b[0:tile_rows(i), z, 0:wd], i), scores(b, i), ACT.Relu).then_inc(idx_act.inc(f"s{i}_{hd}"), 1)
                next_phase(act, "act", l)

                merge(1)

                with act.Fori(0, 2) as q:
                    it = l * 2 + q
                    S = att_act

                    def pe_did(name):
                        act.wait_ge(att_pe.sem, att_pe.at(it, name))

                    def dve_did(name):
                        act.wait_ge(att_dve.sem, att_dve.at(it, name))

                    def inputs(hd, part):
                        z = hd % 2
                        if part == 0:
                            pe_did(f"q{hd}")
                            A_(two(qh[:, z, :]), acc(2, slice(0, 96)), ACT.Copy).then_inc(S.inc(f"q{hd}"), 1)
                        if part == 1:
                            pe_did(f"k{hd}")
                            A_(two(kh2[0:64, z, :]), acc(2, slice(0, 64)), ACT.Copy).then_inc(S.inc(f"k{hd}"), 1)
                        if part == 3:
                            pe_did(f"v{hd}")
                            A_(vh[:, z, 0:(NCH - 1) * 64], ps[0:CH, 2, 0:(NCH - 1) * 64], ACT.Copy)
                            tr = tile_rows(NCH - 1)
                            A_(vh[0:tr, z, (NCH - 1) * 64:NCH * 64], ps[0:tr, 2, (NCH - 1) * 64:NCH * 64], ACT.Copy
                               ).then_inc(S.inc(f"v{hd}"), 1)

                    for part in range(4):
                        inputs(0, part)
                    for n in range(len(UNITS) + 3):
                        if n < len(UNITS):
                            hd, i = UNITS[n]
                            wd, tr, k = tile_keys(i), tile_rows(i), n % 3
                            dve_did(f"m{i}_{hd}")
                            A_(es[0:tr, k, 0:wd], es[0:tr, k, 0:wd], ACT.Exp, bias=mx[0:tr, k:k + 1],
                               scale=ATT_SCALE, accum_out=rs[0:tr, k:k + 1]).then_inc(S.inc(f"e{i}_{hd}"), 1)
                            if hd < 7 and i < 4:
                                inputs(hd + 1, i)
                        if 0 <= n - 2 < len(UNITS):
                            hd, i = UNITS[n - 2]
                            b, tr = 4 + 2 * (i % 2), tile_rows(i)
                            wd = min(i + 1, NCH - 1) * tr
                            pe_did(f"pt{i}_{hd}")
                            last = A_(pts[:, i % 2, 0:wd], ps[0:CH, b, 0:wd], ACT.Copy)
                            if i == NCH - 1:
                                last = A_(pts[0:tr, i % 2, wd:wd + tr], ps[0:tr, b, wd:wd + tr], ACT.Copy)
                            last.then_inc(S.inc(f"pt{i}_{hd}"), 1)
                        if n >= 3:
                            hd, i = UNITS[n - 3]
                            z = hd % 2
                            b, tr = 5 + 2 * (i % 2), tile_rows(i)
                            rw = slice(64 * z, 64 * z + 64)
                            pe_did(f"pv{i}_{hd}")
                            A_(y[rw, ds(q * 4 + hd // 2, 1), i * CH:tile_keys(i)],
                               ps[rw, b:b + 1, 0:tr], ACT.Copy).then_inc(S.inc(f"pv{i}_{hd}"), 1)
                next_phase(act, "act", l)
                merge(2)
                next_phase(act, "act", l)
                norm(l * 2 + 1)
                next_phase(act, "act", l)

                S = rt_act

                def rows_out(i, tr, pe_steps, steps):
                    b = (2 + 2 * (i % 3)) if steps is rt_act else 2 * (i % 4)
                    name = ("ut" if steps is rt_act else "yt") + str(i)
                    act.wait_ge(pe_steps.sem, pe_steps.at(l, name))
                    A_(tok[0:tr, i, :].rearrange("p (a b) -> p a b", a=2), ps[0:tr, b:b + 2, :], ACT.Copy
                       ).then_inc(steps.inc(name), 1)

                for i in range(3):
                    rows_out(i, CH, rt_pe, rt_act)
                act.wait_ge(rt_dve.sem, rt_dve.at(l, "gmax"))
                A_(r1, r1, ACT.Exp).then_inc(S.inc("gexp"), 1)
                rows_out(3, CH, rt_pe, rt_act)
                act.wait_ge(rt_dve.sem, rt_dve.at(l, "ediff"))
                A_(s4, s4, ACT.Exp).then_inc(S.inc("eexp"), 1)
                rows_out(4, CH, rt_pe, rt_act)
                rows_out(5, CH, rt_pe, rt_act)
                act.wait_ge(rt_pe.sem, rt_pe.at(l, "pos"))
                A_(two(place), acc(2), ACT.Copy).then_inc(S.inc("pos"), 1)
                act.wait_ge(rt_pe.sem, rt_pe.at(l, "ct"))
                A_(two(comb_t), acc(4, slice(0, 16)), ACT.Copy).then_inc(S.inc("ct"), 1)
                for j in range(0, KD, 2):
                    act.wait_ge(rt_pe.sem, rt_pe.at(l, f"su{j}"))
                    A_(two(u[:, j, :]), acc((6, 0, 2, 4)[j % 4]), ACT.Copy).then_inc(S.inc(f"su{j}"), 1)
                next_phase(act, "act", l)

                def group(g, cols):
                    gi = l * 4 + g
                    for e in range(4):
                        act.wait_ge(grp_pe.sem, grp_pe.at(gi, f"c{e}"))
                        A_(first_cols(comb_b[:, e, :], cols), bank_cols(2 * e, cols), ACT.Copy).then_inc(grp_act.inc(f"c{e}"), 1)
                    with act.Fori(0, 4) as e:
                        it = gi * 4 + e
                        for n in range(2):
                            act.wait_ge(exp_pe.sem, exp_pe.at(it, f"a{n}"))
                            act.wait_ge(exp_dve.sem, exp_dve.before(it, f"h{n}"))
                            A_(first_cols(e_tanh[:, n, :], cols), bank_cols(4 * n, cols), ACT.Tanh, scale=0.5
                               ).then_inc(exp_act.inc(f"t{n}"), 1)

                by_width(act, group)
                next_phase(act, "act", l)
                for i in range(NCH):
                    rows_out(i, tile_rows(i), back_pe, back_act)
                next_phase(act, "act", l)
            norm(DEPTH * 2)

        @block.gpsimd
        def _(pool):
            for S in (prep_pool, pair_pool, merge_a_pool):
                pool.sem_inc(S.sem, len(S.names))
            pool.memset(vfb, 0.0)
            pool.drain().then_inc(zeroed, 1)
            pool.wait_ge(zeroed, 1)
            for q in range(NPAIR):
                pool.dma_start(v_first[q], vfb).then_inc(vf_out, 16)
            pool.wait_ge(loaded, 16 * (KD + 1))
            pool.wait_ge(vf_out, 16 * NPAIR)
            with pool.Fori(0, DEPTH) as l:
                for _ in range(2):
                    next_phase(pool, "pool", l)

                def receptance(turn):
                    pool.drain()
                    pool.wait_ge(prep_act.sem, prep_act.at(turn, "G"))
                    pool.wait_ge(prep_dve.sem, prep_dve.at(turn, "r"))
                    nc.gpsimd.tensor_tensor(arh[0:64, 1, 0:T], pr[0:64, :], G[0:64, :], ALU.mult)
                    nc.gpsimd.tensor_tensor(arh[64:128, 3, 0:T], pr[64:128, :], G[64:128, :], ALU.mult)
                    pool.drain().then_inc(prep_pool.inc("r"), 1)

                def pair(q, more):
                    it = l * NPAIR + q
                    pool.drain()
                    pool.wait_ge(pair_pe.sem, pair_pe.before(it, f"o{NCH - 1}"))
                    pool.wait_ge(prep_dve.sem, prep_dve.at(it, "a"))
                    alone(pool)
                    nc.gpsimd.tensor_copy(ar[0:64, :, :], arh[0:64, 0:2, :])
                    nc.gpsimd.tensor_copy(ar[64:128, :, :], arh[64:128, 2:4, :])
                    pool.drain().then_inc(pair_pool.inc("ar"), 1)
                    pool.wait_ge(prep_dve.sem, prep_dve.at(it, "v"))
                    alone(pool)
                    pool.dma_start(v_first[ds(q, 1)].rearrange("a p b -> p (a b)") if more else v_first[q], vfb
                                   ).then_inc(vf_out, 16)
                    if more:
                        pool.wait_ge(vf_out, 16 * (NPAIR + 1) + 16 * it)
                        alone(pool)
                        pool.dma_start(vfb, v_first[ds(q + 1, 1)].rearrange("a p b -> p (a b)")).then_inc(vf_in, 16)
                    for n, lv in enumerate(LEVELS):
                        o = CONSTS["level"][0] + (n + 1) * CH
                        mask = cst[0:CH, o:o + CH].rearrange("p (a b) -> p a b", a=1).to_broadcast([CH, 4, CH])
                        for x in range(3):
                            if n == 0:
                                pool.wait_ge(pair_dve.sem, pair_dve.at(it, f"gram{2 * x + 1}"))
                            else:
                                pool.wait_ge(pair_pe.sem, pair_pe.at(it, f"t{LEVELS[n - 1]}_{x}"))
                            nc.gpsimd.tensor_tensor(lv_as[x], gr[:, 4 * x:4 * x + 4, 0:CH], mask, ALU.mult
                                                    ).then_inc(pair_pool.inc(f"lv{lv}_{x}"), 1)
                    if more:
                        receptance(it + 1)

                pool.wait_ge(vf_out, 16 * NPAIR + 16 * NPAIR * l)
                alone(pool)
                pool.dma_start(vfb, v_first[0]).then_inc(vf_in, 16)
                receptance(l * NPAIR)
                with pool.Fori(0, NPAIR - 1) as q:
                    pair(q, True)
                pair(NPAIR - 1, False)
                for _ in range(5):
                    next_phase(pool, "pool", l)
                with pool.Fori(0, 4) as q:
                    it = l * 4 + q
                    for n in range(2):
                        pool.wait_ge(merge_a_act.sem, merge_a_act.at(it, f"g{n}"))
                        nc.gpsimd.tensor_tensor(ma_s[:, n, :], ma_g[:, n, :], ma_p[:, n, :], ALU.mult)
                        pool.drain()
                        nc.gpsimd.tensor_tensor(ma_s[:, n, :], ma_s[:, n, :], ma_p[:, n, :], ALU.add)
                        pool.drain()
                        dst = m[:, ds(2 * q + n, 1), :].rearrange("p a b -> p (a b)")
                        nc.gpsimd.tensor_tensor(dst, dst, ma_s[:, n, :], ALU.add)
                        pool.drain().then_inc(merge_a_pool.inc(f"m{n}"), 1)
                for _ in range(N_PHASES - 7):
                    next_phase(pool, "pool", l)

        @block.vector
        def _(dve):
            V = nc.vector
            for S in DVE_STEPS:
                dve.sem_inc(S.sem, len(S.names))
            dve.wait_ge(loaded, 16 * (KD + 1))
            dve.wait_ge(zeroed, 1)

            def norm(turn, gains):
                dve.wait_ge(norm_pe.sem, norm_pe.at(turn, "sum"))
                V.tensor_scalar(two(n_rs), acc(0), 1.0 / D, EPS, ALU.mult, ALU.add).then_inc(norm_dve.inc("mean"), 1)
                dve.wait_ge(norm_act.sem, norm_act.at(turn, "sqrt"))
                V.reciprocal(n_rs, n_rs)
                dve.drain()
                for j in range(KD):
                    V.scalar_tensor_tensor(u[:, j, :], h[:, j, :], pc(gains, j), n_rs, ALU.mult, ALU.mult)
                dve.drain()

            def rope(dst, src, rotated, tmp, rows=slice(0, P)):
                V.tensor_tensor(tmp, rotated, two(sin[rows, :]), ALU.mult)
                V.tensor_tensor(src, src, cos[rows, :], ALU.mult)
                dve.drain()
                return V.tensor_tensor(dst, src, tmp.rearrange("p a b -> p (a b)"), ALU.add)

            def shift(dst, raw, mu, tmp):
                V.tensor_tensor(tmp, raw[:, 0:T], raw[:, 1:T + 1], ALU.subtract)
                dve.drain()
                return V.scalar_tensor_tensor(dst, tmp, mu, raw[:, 1:T + 1], ALU.mult, ALU.add)

            with dve.Fori(0, DEPTH) as l:
                dve.wait_ge(par_full, (l + 1) * 16)
                norm(l * 2, "norm_mix")
                next_phase(dve, "dve", l)

                V.memset(raw_r[:, 0:1], 0.0)
                V.memset(raw_k[:, 0:1], 0.0)
                V.memset(raw_v[:, 0:1], 0.0)
                V.tensor_scalar(half_w0, par[:, PARAMS["w0"][0]:PARAMS["w0"][0] + 8], 0.5, None, ALU.mult)
                V.tensor_scalar(half_a0, par[:, PARAMS["a0"][0]:PARAMS["a0"][0] + 8], 0.5, None, ALU.mult)
                V.tensor_scalar(half_v0, par[:, PARAMS["v0"][0]:PARAMS["v0"][0] + 8], 0.5, None, ALU.mult)
                dve.drain()
                dve.wait_ge(low_act.sem, low_act.at(l, "wa"))
                shift(lr_wa, raw_r, pc("mu_wa"), tz)
                dve.wait_ge(low_act.sem, low_act.at(l, "g"))
                shift(lr_g, raw_k, pc("mu_g"), ta)
                dve.wait_ge(low_act.sem, low_act.at(l, "vres"))
                shift(lr_v, raw_v, pc("mu_vres"), tv).then_inc(low_dve.inc("shift"), 1)
                dve.wait_ge(low_act.sem, low_act.at(l, "tanh"))
                V.tensor_scalar(lr_g, lr_g, 0.5, 0.5, ALU.mult, ALU.add)
                next_phase(dve, "dve", l)

                P_ = prep_dve

                def decay(turn):
                    dve.wait_ge(prep_act.sem, prep_act.at(turn, "z"))
                    rate = -0.5 * float(np.exp(-0.5))
                    V.tensor_scalar(tz, tz, rate, rate, ALU.mult, ALU.add)
                    dve.drain()
                    V.tensor_tensor_scan(cum, c("reset"), tz, 0.0, ALU.mult, ALU.add)
                    dve.drain()
                    V.tensor_tensor(Gx, cum, tz, ALU.subtract).then_inc(P_.inc("c"), 1)

                def sigmoids(turn):
                    dve.wait_ge(prep_act.sem, prep_act.at(turn, "vres"))
                    V.tensor_scalar(ta, ta, 0.5, 0.5, ALU.mult, ALU.add)
                    V.tensor_scalar(tv, tv, 0.5, 0.5, ALU.mult, ALU.add)

                def receptance(turn, q):
                    dve.wait_ge(prep_act.sem, prep_act.at(turn, "r"))
                    shift(pr, raw_r, pc("mu_r", q), tz).then_inc(P_.inc("r"), 1)

                def keys_of(turn, q):
                    dve.drain()
                    dve.wait_ge(prep_act.sem, prep_act.at(turn, "k"))
                    shift(pk, raw_k, pc("mu_k", q), kh)
                    dve.drain()
                    V.tensor_scalar(kk, pk, pc("k_k", q), None, ALU.mult).then_inc(P_.inc("kk"), 1)

                def decayed_keys(turn, q):
                    dve.drain()
                    V.tensor_scalar(kh, ta, -1.0, pc("k_a", q), ALU.add, ALU.mult)
                    dve.drain()
                    V.scalar_tensor_tensor(kh, kh, 1.0, pk, ALU.add, ALU.mult)
                    dve.drain()

                def key_squares(turn, q):
                    dve.wait_ge(prep_pe.sem, prep_pe.at(turn, "kk"))
                    V.tensor_scalar(two(sqk), acc(4), 1e-24, None, ALU.max).then_inc(P_.inc("kkmax"), 1)

                def bonus_terms(turn, q):
                    dve.drain()
                    V.scalar_tensor_tensor(tz, pr, pc("r_k", q), kh, ALU.mult, ALU.mult).then_inc(P_.inc("rkk"), 1)

                def unit_keys(turn, q):
                    dve.wait_ge(prep_act.sem, prep_act.at(turn, "norm"))
                    V.reciprocal(sqk, sqk)
                    dve.drain()
                    V.tensor_tensor(kk, kk, sqk, ALU.mult)
                    dve.drain()

                def abar(turn, q):
                    V.scalar_tensor_tensor(arh[0:64, 0, 0:T], kk[0:64, :], -1.0, Gx[0:64, :], ALU.mult, ALU.mult)
                    V.scalar_tensor_tensor(arh[64:128, 2, 0:T], kk[64:128, :], -1.0, Gx[64:128, :], ALU.mult,
                                           ALU.mult)
                    dve.drain().then_inc(P_.inc("a"), 1)

                def bbar_kbar(turn, q):
                    V.tensor_tensor(kk, kk, ta, ALU.mult)
                    V.tensor_tensor(kb_[:, 0:T], kh, Gi, ALU.mult)
                    dve.drain()
                    V.tensor_tensor(bb[:, 0:T], kk, Gi, ALU.mult)
                    dve.drain().then_inc(P_.inc("rbk"), 1)

                def shifted_values(turn, q):
                    dve.wait_ge(prep_act.sem, prep_act.at(turn, "v"))
                    shift(pv[:, 0:T], raw_v, pc("mu_v", q), pk)

                def values(turn, q):
                    v, tmp = pv[:, 0:T], raw_v[:, 1:T + 1]
                    dve.drain()
                    dve.wait_ge(vf_in, 16 * (turn + 1))
                    V.tensor_tensor(tmp, vfb, v, ALU.subtract)
                    dve.drain()
                    V.scalar_tensor_tensor(tmp, tmp, pc("later"), tv, ALU.mult, ALU.mult)
                    dve.drain()
                    V.tensor_tensor(v, v, tmp, ALU.add)
                    dve.drain()
                    V.tensor_tensor(tv, v, vfb, ALU.subtract)
                    dve.drain()
                    V.scalar_tensor_tensor(vfb, tv, pc("first"), vfb, ALU.mult, ALU.add)
                    dve.drain().then_inc(P_.inc("v"), 1)

                CHUNK_PARTS = ((decayed_keys,), (key_squares, receptance), (unit_keys,), (bonus_terms, abar),
                               (bbar_kbar,), (shifted_values, values))

                def pair(q, more):
                    it = l * NPAIR + q
                    S = pair_dve

                    def pe_did(name):
                        dve.wait_ge(pair_pe.sem, pair_pe.at(it, name))

                    def act_did(name):
                        dve.wait_ge(pair_act.sem, pair_act.at(it, name))

                    dve.drain()
                    V.memset(state, 0.0)
                    V.tensor_copy(gend.rearrange("p (a b) -> p a b", b=1),
                                  G[:, 0:(NCH - 1) * CH].rearrange("p (a b) -> p a b", b=CH)[:, :, CH - 1:CH])
                    V.tensor_copy(pg_now, pg)
                    gmask = c("grams", CH).rearrange("p (a b) -> p a b", a=1).to_broadcast([CH, 2, 4 * CH])
                    low1 = c("low1", CH).rearrange("p (a b) -> p a b", a=1).to_broadcast([CH, 2, CH])
                    o = CONSTS["level"][0]
                    lv1 = cst[0:CH, o:o + CH].rearrange("p (a b) -> p a b", a=1).to_broadcast([CH, 4, CH])
                    i96 = ident[0:CH, 0:CH].rearrange("p (a b) -> p a b", a=1).to_broadcast([CH, 4, CH])
                    for i in range(NCH):
                        pe_did(f"gram{i}")
                        b = GRAM_BANKS[i % 4]
                        V.tensor_tensor(gr[:, 2 * i:2 * i + 2, :], ps[0:CH, b:b + 2, 0:4 * CH], gmask, ALU.mult)
                        V.tensor_tensor(inv[:, 2 * i:2 * i + 2, :], ps[0:CH, b:b + 2, 4 * CH:5 * CH], low1, ALU.mult)
                        dve.drain().then_inc(S.inc(f"gram{i}"), 1)
                        if i % 2 == 1:
                            x = i // 2
                            it4, iv4 = inv_t[:, 4 * x:4 * x + 4, :], inv[:, 4 * x:4 * x + 4, :]
                            V.tensor_tensor(it4, gr[:, 4 * x:4 * x + 4, 0:CH], lv1, ALU.mult)
                            V.tensor_tensor(iv4, iv4, i96, ALU.add)
                            dve.drain()
                            V.tensor_tensor(it4, it4, i96, ALU.add)
                            dve.drain().then_inc(S.inc(f"one{x}"), 1)
                    pe_did("bonus")
                    V.tensor_tensor(two(bonus), acc(6), two(pv[:, 0:T]), ALU.mult).then_inc(S.inc("bonus"), 1)
                    for lv in LEVELS:
                        for x in range(3):
                            pe_did(f"nm{lv}_{x}")
                            for dst, b in ((inv_t, 2 + x % 2), (inv, 4 + x % 2))[0:1 if lv == LEVELS[-1] else 2]:
                                V.tensor_tensor(dst[:, 4 * x:4 * x + 4, :], dst[:, 4 * x:4 * x + 4, :],
                                                ps[0:CH, b, 0:4 * CH].rearrange("p (a b) -> p a b", a=4), ALU.add)
                            dve.drain().then_inc(S.inc(f"nm{lv}_{x}"), 1)
                        if more and lv == 4:
                            decay(it + 1)
                        if more and lv == 8:
                            sigmoids(it + 1)
                        if more and lv == 32:
                            keys_of(it + 1, q + 1)
                    for i in range(NCH):
                        pe_did(f"x{i}")
                        V.tensor_copy(xs[0:CH, :], ps[0:CH, 0, 0:P]).then_inc(S.inc(f"x{i}"), 1)
                        if more:
                            for part in CHUNK_PARTS[i]:
                                part(it + 1, q + 1)
                        if i < NCH - 1:
                            pe_did(f"d{i}")
                            V.tensor_tensor(state, state, ps[:, 3, 0:P], ALU.add)
                            dve.drain()
                            V.scalar_tensor_tensor(state, state, gend[:, i:i + 1], headones, ALU.mult,
                                                   ALU.mult).then_inc(S.inc(f"s{i}"), 1)
                    pe_did("mean")
                    V.scalar_tensor_tensor(two(pairs_o), acc(0), -1.0 / 64, two(pairs_o), ALU.mult, ALU.add
                                           ).then_inc(S.inc("cen"), 1)
                    pe_did("var")
                    V.tensor_scalar(two(otmp), acc(2), 1.0 / 64, GN_EPS, ALU.mult, ALU.add).then_inc(S.inc("var"), 1)
                    act_did("std")
                    V.reciprocal(otmp, otmp)
                    dve.drain()
                    V.tensor_tensor(pairs_o, pairs_o, otmp, ALU.mult)
                    dve.drain()
                    V.tensor_scalar(pairs_o, pairs_o, pc("ln_w", q), pc("ln_b", q), ALU.mult, ALU.add)
                    dve.drain()
                    V.tensor_tensor(pairs_o, pairs_o, bonus, ALU.add)
                    dve.drain()
                    y_q = y[:, q, :] if isinstance(q, int) else y[:, ds(q, 1), :].rearrange("p a b -> p (a b)")
                    V.tensor_tensor(y_q, pairs_o, pg_now, ALU.mult).then_inc(S.inc("y"), 1)

                V.memset(bb[:, T:TP], 0.0)
                V.memset(kb_[:, T:TP], 0.0)
                V.memset(pv[:, T:TP], 0.0)
                V.memset(arh, 0.0)
                dve.drain()
                first = l * NPAIR
                decay(first)
                sigmoids(first)
                keys_of(first, 0)
                for parts_ in CHUNK_PARTS:
                    for part in parts_:
                        part(first, 0)
                with dve.Fori(0, NPAIR - 1) as q:
                    pair(q, True)
                pair(NPAIR - 1, False)
                next_phase(dve, "dve", l)

                def merge(k):
                    with dve.Fori(0, 4) as q:
                        it = l * 12 + 4 * k + q
                        for n in range(2):
                            dve.wait_ge(merge_act.sem, merge_act.at(l * 8 + 2 * k + q, f"g{n}"))
                            dve.wait_ge(merge_pe.sem, merge_pe.at(it, f"p{n}"))
                            V.scalar_tensor_tensor(two(g_tmp[:, n, :]), two(g_tanh[:, n, :]), 1.0, acc(4 * n),
                                                   ALU.add, ALU.mult)
                            dve.drain()
                            dst = m[:, ds(2 * q + n, 1), :].rearrange("p a b -> p (a b)")
                            if k == 0:
                                last = V.tensor_scalar(dst, g_tmp[:, n, :], 0.5, None, ALU.mult)
                            else:
                                last = V.scalar_tensor_tensor(dst, g_tmp[:, n, :], 0.5, dst, ALU.mult, ALU.add)
                            last.then_inc(merge_dve.inc(f"m{n}"), 1)
                    next_phase(dve, "dve", l)

                merge(0)
                o = CONSTS["counts"][0]
                for j in range(8):
                    w = POOL_WINDOWS[j // 2]
                    dve.wait_ge(pool_act.sem, pool_act.at(l, f"p{j}"))
                    src, k = p_raw[:, j % 2, :], 1
                    bufs = [p_a, p_b]
                    while k < w:
                        dst = bufs[0]
                        V.tensor_tensor(dst[:, k:T], src[:, k:T], src[:, 0:T - k], ALU.add)
                        V.tensor_copy(dst[:, 0:k], src[:, 0:k])
                        dve.drain()
                        src, k = dst, 2 * k
                        bufs.reverse()
                    dst = bufs[0]
                    V.scalar_tensor_tensor(pooled[:, j, w:T], src[:, w:T], 1.0 / w, p_raw[:, j % 2, w:T], ALU.mult,
                                           ALU.subtract)
                    V.tensor_tensor(dst[:, 0:w], src[:, 0:w], cst[:, o:o + w], ALU.mult)
                    dve.drain()
                    V.tensor_tensor(pooled[:, j, 0:w], dst[:, 0:w], p_raw[:, j % 2, 0:w], ALU.subtract)
                    dve.drain().then_inc(pool_dve.inc(f"p{j}"), 1)
                next_phase(dve, "dve", l)

                def pe_did(name):
                    dve.wait_ge(lat_pe.sem, lat_pe.at(l, name))

                def act_did(name):
                    dve.wait_ge(lat_act.sem, lat_act.at(l, name))
                S = lat_dve
                V.memset(kidx2, 0.0)
                pe_did("qsum")
                V.tensor_scalar(two(l_rs), acc(2), 1.0 / 256, EPS, ALU.mult, ALU.add)
                pe_did("kvsum")
                V.tensor_scalar(two(l_rs2), acc(4), 1.0 / 128, EPS, ALU.mult, ALU.add)
                dve.drain().then_inc(S.inc("means"), 1)
                act_did("std")
                V.reciprocal(l_rs, l_rs)
                V.reciprocal(l_rs2, l_rs2)
                dve.drain()
                for j in range(2):
                    V.scalar_tensor_tensor(cq[:, j, :], cq[:, j, :], pc("q_norm", j), l_rs, ALU.mult, ALU.mult)
                V.scalar_tensor_tensor(ckv, ckv, pc("kv_norm"), l_rs2, ALU.mult, ALU.mult)
                dve.drain().then_inc(S.inc("latents"), 1)
                pe_did("mean")
                V.scalar_tensor_tensor(two(kidx), acc(6), -1.0 / 64, two(kidx), ALU.mult, ALU.add
                                       ).then_inc(S.inc("center"), 1)
                pe_did("var")
                V.tensor_scalar(two(l_tmp), acc(6), 1.0 / 64, EPS, ALU.mult, ALU.add).then_inc(S.inc("var"), 1)
                act_did("std2")
                V.reciprocal(l_tmp, l_tmp)
                dve.drain()
                V.tensor_tensor(kidx, kidx, l_tmp, ALU.mult)
                dve.drain()
                V.tensor_scalar(kidx, kidx, pc("idx_w"), pc("idx_b"), ALU.mult, ALU.add).then_inc(S.inc("kidx"), 1)
                pe_did("kperm")
                rope(kidx, kidx, acc(2), two(l_tmp))
                dve.drain()
                for z in range(2):
                    rw = slice(64 * z, 64 * z + 64)
                    V.tensor_copy(kidx2[rw, z, :], kidx[rw, :])
                pe_did("rperm")
                rope(kr, kr, acc(4), two(l_tmp2))
                dve.drain().then_inc(S.inc("ropes"), 1)
                for j in range(4):
                    pe_did(f"qp{j}")
                    rope(qi[:, j, :], qi[:, j, :], acc(2 * j), two((l_tmp, l_tmp2)[j % 2])
                         ).then_inc(S.inc(f"rope{j}"), 1)
                next_phase(dve, "dve", l)

                tri, tri_b = c("causal", CH), c("bias", CH)
                V.tensor_copy(sel_of(0), tri_b)
                for n, (i, hd) in enumerate(IDX):
                    z, wd, tr = n % 2, tile_keys(i), tile_rows(i)
                    dve.wait_ge(idx_act.sem, idx_act.at(l, f"s{i}_{hd}"))
                    sc = sel_of(i)
                    if hd == 0:
                        last = V.tensor_scalar(sc, relu_b[0:tr, z, 0:wd], wtok[0:tr, i, 0:1], None, ALU.mult)
                    else:
                        last = V.scalar_tensor_tensor(sc, relu_b[0:tr, z, 0:wd], wtok[0:tr, i, hd:hd + 1], sc,
                                                      ALU.mult, ALU.add)
                    last.then_inc(idx_dve.inc(f"s{i}_{hd}"), 1)
                    dve.drain()
                next_phase(dve, "dve", l)
                for i in range(1, NCH):
                    sc, wd, tr = sel_of(i), tile_keys(i), tile_rows(i)
                    V.tensor_tensor(sc[:, i * CH:wd], sc[:, i * CH:wd], tri[0:tr, 0:tr], ALU.add)
                    dve.drain()
                    for _ in range(TOPK // 8):
                        V.max(top8[0:tr, :], sc)
                        dve.drain()
                        V.match_replace(sc, top8[0:tr, :], sc, TAKEN)
                        dve.drain()
                    V.tensor_scalar(sc, sc, TAKEN, NEG_BIAS, ALU.is_gt, ALU.mult)
                    dve.drain()
                    V.tensor_tensor(sc[:, i * CH:wd], sc[:, i * CH:wd], tri_b[0:tr, 0:tr], ALU.add)
                next_phase(dve, "dve", l)

                with dve.Fori(0, 2) as q:
                    it = l * 2 + q
                    S = att_dve

                    def pe_did(name):
                        dve.wait_ge(att_pe.sem, att_pe.at(it, name))

                    def act_did(name):
                        dve.wait_ge(att_act.sem, att_act.at(it, name))

                    V.tensor_copy(kh2[64:96, 0, :], kr[64:96, :])
                    V.tensor_copy(kh2[64:96, 1, :], kr[64:96, :])
                    dve.drain().then_inc(S.inc("kr"), 1)
                    def rotate(hd):
                        z = hd % 2
                        pe_did(f"perm{hd}")
                        rope(qh[64:96, z, :], qh[64:96, z, :], acc(2, slice(64, 96)), two(rope_t[64:96, :]),
                             slice(64, 96)).then_inc(S.inc(f"rope{hd}"), 1)

                    rotate(0)
                    for n in range(len(UNITS) + 1):
                        if n < len(UNITS):
                            hd, i = UNITS[n]
                            wd, k, tr = tile_keys(i), n % 3, tile_rows(i)
                            pe_did(f"s{i}_{hd}")
                            if n >= 3:
                                g, j = UNITS[n - 3]
                                pe_did(f"pt{j}_{g}")
                            else:
                                dve.wait_ge(att_pe.sem, att_pe.before(it, f"pt{NCH - 3 + n}_7"))
                            alone(dve)
                            V.tensor_tensor_reduce(
                                out=parts(es[0:tr, k, 0:wd], i), in0=scores(score_bank(i), i), in1=parts(sel_of(i), i),
                                scale=1.0, scalar=NEG_CAUSAL, op0=ALU.add, op1=ALU.max,
                                accum_out=mx[0:tr, k:k + 1])
                            dve.drain()
                            V.tensor_scalar(mx[0:tr, k:k + 1], mx[0:tr, k:k + 1], -ATT_SCALE, None, ALU.mult
                                            ).then_inc(S.inc(f"m{i}_{hd}"), 1)
                            if hd < 7 and i == 2:
                                rotate(hd + 1)
                        if n >= 1:
                            hd, i = UNITS[n - 1]
                            wd, k, tr = tile_keys(i), (n - 1) % 3, tile_rows(i)
                            act_did(f"e{i}_{hd}")
                            V.reciprocal(ri[0:tr, k:k + 1], rs[0:tr, k:k + 1])
                            dve.drain()
                            V.tensor_scalar(es[0:tr, k, 0:wd], es[0:tr, k, 0:wd], ri[0:tr, k:k + 1], None, ALU.mult
                                            ).then_inc(S.inc(f"n{i}_{hd}"), 1)
                next_phase(dve, "dve", l)
                merge(2)

                with dve.Fori(0, 2) as q:
                    it = l * 2 + q
                    for s in range(4):
                        dve.wait_ge(res_pe.sem, res_pe.at(it, f"o{s}"))
                        dst = h[:, ds(4 * q + s, 1), :].rearrange("p a b -> p (a b)")
                        V.tensor_tensor(two(dst), two(dst), acc(2 * s), ALU.add).then_inc(res_dve.inc(f"h{s}"), 1)
                next_phase(dve, "dve", l)
                norm(l * 2 + 1, "norm_ffn")
                next_phase(dve, "dve", l)

                S = rt_dve
                V.memset(y[:, :, :], 0.0)
                V.memset(all1, 1.0)
                dve.drain()
                V.tensor_tensor_scan(count1, all1, all1, 0.0, ALU.mult, ALU.add)
                dve.wait_ge(rt_pe.sem, rt_pe.at(l, "logits"))
                ob = PARAMS["router_b"][0]
                V.tensor_tensor(lg, ps[0:CH, 0, 0:20 * NCH].rearrange("p (a b) -> p a b", a=NCH),
                                par[0:CH, ob:ob + 20].rearrange("p (a b) -> p a b", a=1).to_broadcast([CH, NCH, 20]),
                                ALU.add)
                dve.drain()
                keys = c("keys", CH).rearrange("p (a b) -> p a b", a=1).to_broadcast([CH, NCH, 4])

                def over(v):
                    return v.rearrange("p (a b) -> p a b", b=1).to_broadcast([CH, NCH, 4])

                def first_max(dst, src, top):
                    V.tensor_reduce(top, src, AX.X, ALU.max)
                    dve.drain()
                    V.tensor_tensor(r2, src, over(top), ALU.is_ge)
                    dve.drain()
                    V.tensor_tensor(r2, r2, keys, ALU.mult)
                    dve.drain()
                    V.tensor_reduce(s5, r2, AX.X, ALU.max)
                    dve.drain()
                    V.tensor_tensor(dst, r2, over(s5), ALU.is_equal)
                    dve.drain()

                first_max(oh, lg[:, :, 0:4], s1)
                V.tensor_tensor(r1, lg[:, :, 0:4], over(s1), ALU.subtract)
                dve.drain().then_inc(S.inc("gmax"), 1)
                e16 = lg[:, :, 4:20].rearrange("p a (g e) -> p a g e", g=4)
                r16v = r16.rearrange("p a (g e) -> p a g e", g=4)
                for g in range(4):
                    V.tensor_tensor(r16v[:, :, g, :], e16[:, :, g, :], oh[:, :, g:g + 1].to_broadcast([CH, NCH, 4]),
                                    ALU.mult)
                dve.drain()
                V.tensor_reduce(r3, r16.rearrange("p a (g e) -> p a e g", g=4), AX.X, ALU.add)
                dve.drain()
                first_max(oh1, r3, s2)
                V.scalar_tensor_tensor(r3, oh1, NEG_CAUSAL, r3, ALU.mult, ALU.add)
                dve.drain()
                first_max(oh2, r3, s3)
                V.tensor_tensor(s4, s3, s2, ALU.subtract).then_inc(S.inc("ediff"), 1)
                dve.wait_ge(rt_act.sem, rt_act.at(l, "gexp"))
                V.tensor_reduce(s1, r1, AX.X, ALU.add)
                dve.wait_ge(rt_act.sem, rt_act.at(l, "eexp"))
                V.tensor_scalar(s2, s4, 1.0, None, ALU.add)
                dve.drain()
                V.tensor_tensor(s2, s2, s1, ALU.mult)
                dve.drain()
                V.reciprocal(s2, s2)
                dve.drain()
                V.tensor_tensor(s3, s2, s4, ALU.mult)
                V.tensor_tensor(oh1, oh1, over(s2), ALU.mult)
                dve.drain()
                V.tensor_tensor(oh2, oh2, over(s3), ALU.mult)
                dve.drain()
                V.tensor_tensor(ce, oh1, oh2, ALU.add)
                dve.drain()
                for g in range(4):
                    V.tensor_tensor(comb[:, :, 4 * g:4 * g + 4], ce, oh[:, :, g:g + 1].to_broadcast([CH, NCH, 4]),
                                    ALU.mult)
                dve.drain().then_inc(S.inc("oh"), 1)
                dve.wait_ge(rt_pe.sem, rt_pe.at(l, "oh"))
                V.tensor_copy(oh_t[:, 0:5 * CH], ps[0:4, 0, 0:5 * CH])
                V.tensor_copy(oh_t[:, 5 * CH:T], ps[0:4, 1, 5 * CH - window(5):CH])
                dve.drain()
                V.tensor_tensor_scan(rank, all1[0:4, :], oh_t, 0.0, ALU.mult, ALU.add)
                dve.drain().then_inc(S.inc("rank"), 1)
                dve.wait_ge(rt_pe.sem, rt_pe.at(l, "start"))
                V.tensor_copy(start4, ps[0:4, 0, 0:1])
                V.tensor_copy(start_row, ps[0:1, 0, 4:12])
                dve.drain()
                V.scalar_tensor_tensor(place4, rank, start4, oh_t, ALU.add, ALU.mult)
                dve.drain().then_inc(S.inc("pos"), 1)
                for k, cols in enumerate(GROUP_COLS):
                    V.tensor_scalar(starts[0:1, 4 * k:4 * k + 4], start_row[:, 0:4], float(T - cols), None, ALU.min)
                V.tensor_scalar(narrow[0:1, :], start_row[:, 4:8], GROUP_COLS[0] + 0.5, None, ALU.is_lt)
                V.tensor_reduce(most, start_row[:, 4:8], AX.X, ALU.max)
                dve.drain()
                V.tensor_scalar(fits[0:1, :], most, GROUP_COLS[1] + 0.5, None, ALU.is_lt)
                dve.wait_ge(rt_pe.sem, rt_pe.at(l, "pos"))
                V.tensor_tensor(place_tok, ps[0:CH, 1, 0:NCH], c("own", CH), ALU.mult)
                dve.drain().then_inc(S.inc("take"), 1)
                for i in range(NCH):
                    V.tensor_scalar(take[:, i, :], count1[0:CH, :], place_tok[:, i:i + 1], None, ALU.is_equal
                                    ).then_inc(S.inc(f"perm{i}"), 1)
                dve.wait_ge(rt_act.sem, rt_act.at(l, "pos"))
                slot = c("slot", CH)
                for i in range(NCH):
                    V.tensor_scalar(give[:, i, :], place[0:CH, :], slot[:, i:i + 1], None, ALU.is_equal)
                for j in range(1, KD, 2):
                    dve.wait_ge(rt_pe.sem, rt_pe.at(l, f"su{j}"))
                    V.tensor_copy(two(u[:, j, :]), acc((6, 0, 2, 4)[j % 4])).then_inc(S.inc(f"su{j}"), 1)
                next_phase(dve, "dve", l)

                def group(g, cols):
                    gi = l * 4 + g
                    off = first_col(dve, g, cols)
                    y_flat = y[:, :, :].rearrange("p a b -> p (a b)")
                    for e in range(4):
                        if e == 0:
                            dve.wait_ge(grp_pe.sem, grp_pe.before(gi, "c3"))
                        else:
                            dve.wait_ge(grp_pe.sem, grp_pe.at(gi, f"c{e - 1}"))
                        if e == 0:
                            alone(dve)
                        src = comb_t if cols == T else comb_t[:, ds(off, cols)]
                        V.tensor_scalar(comb_sel[:, 0:cols], src, ident[0:16, ds(4 * g + e, 1)], None, ALU.mult
                                        ).then_inc(grp_dve.inc(f"c{e}"), 1)
                    dve.wait_ge(grp_act.sem, grp_act.at(gi, "c3"))
                    alone(dve)
                    with dve.Fori(0, 4) as e:
                        it = gi * 4 + e
                        for n in range(2):
                            dve.wait_ge(exp_act.sem, exp_act.at(it, f"t{n}"))
                            dve.wait_ge(exp_pe.sem, exp_pe.at(it, f"b{n}"))
                            tmp = first_cols(e_tmp[:, n, :], cols)
                            V.scalar_tensor_tensor(tmp, first_cols(e_tanh[:, n, :], cols), 1.0, bank_cols(4 * n, cols), ALU.add, ALU.mult)
                            dve.drain()
                            V.tensor_tensor(tmp, tmp, bank_cols(4 * n + 2, cols), ALU.mult)
                            dve.drain()
                            V.scalar_tensor_tensor(
                                hid[:, ds(2 * e + n, 1), 0:cols].rearrange("p a b -> p (a b)"),
                                e_tmp[:, n, 0:cols], 0.5,
                                comb_b[:, ds(e, 1), 0:cols].rearrange("p a b -> p (a b)"), ALU.mult, ALU.mult)
                            dve.drain().then_inc(exp_dve.inc(f"h{n}"), 1)
                    with dve.Fori(0, 2) as q:
                        it = gi * 2 + q
                        for s in range(4):
                            dve.wait_ge(dn_pe.sem, dn_pe.at(it, f"o{s}"))
                            dst = y_flat[:, ds((4 * q + s) * T + off, cols)]
                            if cols == T:
                                dst = two(dst)
                            V.tensor_tensor(dst, dst, bank_cols(2 * s, cols), ALU.add).then_inc(dn_dve.inc(f"h{s}"), 1)

                by_width(dve, group)
                next_phase(dve, "dve", l)
                for j in range(KD):
                    dve.wait_ge(back_pe.sem, back_pe.at(l, f"h{j}"))
                    V.tensor_tensor(two(h[:, j, :]), two(h[:, j, :]), acc(2 * (j % 4)), ALU.add
                                    ).then_inc(back_dve.inc(f"h{j}"), 1)
                next_phase(dve, "dve", l)
            norm(DEPTH * 2, "norm_final")
            dve.drain().then_inc(out_ready, 1)


def constant_table():
    t = np.zeros((P, N_CONST), np.float32)

    def put(name, a, rows=P):
        o, n = CONSTS[name]
        t[:rows, o:o + n] = a

    p = np.arange(P)
    put("ident", np.eye(P))
    put("ones", 1.0)
    put("headones", (p[:, None] // 64 == p[None, :] // 64))
    rot = p % 64 < 32
    partner = np.where(rot, np.where(p % 32 < 16, p + 16, p - 16), p)
    put("perm", partner[:, None] == p[None, :])
    inv = np.float32(10000.0) ** (-np.arange(0, 32, 2, dtype=np.float32) / np.float32(32))
    ang = np.arange(T, dtype=np.float32)[None, :] * inv.astype(np.float32)[p % 16][:, None]
    put("cos", np.where(rot[:, None], np.cos(ang), 1.0))
    put("sin", np.where(rot[:, None], np.where((p % 32 < 16)[:, None], -1.0, 1.0) * np.sin(ang), 0.0))
    put("reset", (np.arange(T) % CH != 0)[None, :])
    a, b = np.arange(CH)[:, None], np.arange(CH)[None, :]
    put("grams", np.concatenate([a < b, a <= b, a < b, a <= b], 1), CH)
    put("low1", (a > b) & (a // 2 == b // 2), CH)
    put("level", np.concatenate([(a // (2 * n) == b // (2 * n)) & (a // n != b // n) for n in [1] + LEVELS], 1), CH)
    put("causal", np.where(b > a, NEG_CAUSAL, 0.0), CH)
    put("bias", np.where(b > a, NEG_BIAS, 0.0), CH)
    put("keys", np.array([[4.0, 3.0, 2.0, 1.0]]))
    put("counts", 1.0 / np.arange(1, 17)[None, :])
    put("slot", p[:, None] + CH * np.arange(NCH)[None, :] + 1.0)
    put("own", (p[:, None] + np.array([window(i) for i in range(NCH)])[None, :]) >= CH * np.arange(NCH)[None, :])
    return t


def param_table(w):
    t = np.zeros((DEPTH, P, N_PARAM), np.float32)
    for l in range(DEPTH):
        def put(name, v):
            o, n = PARAMS[name]
            t[l, :, o:o + n] = np.asarray(v).reshape(n, P).T

        def padded(v):
            out = np.zeros(P, np.float32)
            out[:len(v)] = v
            return out

        for name, key in (("norm_mix", "norm_mix"), ("norm_ffn", "norm_ffn"), ("pool_scale", "pool_scale"),
                          ("w0", "rwkv_w0"), ("a0", "rwkv_a0"), ("k_k", "rwkv_k_k"), ("k_a", "rwkv_k_a"),
                          ("r_k", "rwkv_r_k"), ("ln_w", "rwkv_ln_w"), ("ln_b", "rwkv_ln_b"),
                          ("q_norm", "mla_q_norm"), ("kv_norm", "mla_kv_norm")):
            put(name, w[key][l])
        put("norm_final", w["norm_final"])
        put("v0", w["vres_v0"][max(l - 1, 0)])
        mu = w["mu_shift"][l]
        put("mu_r", mu[0:D])
        put("mu_k", mu[D:2 * D])
        put("mu_v", mu[2 * D:3 * D])
        put("mu_wa", mu[3 * D:3 * D + 128])
        put("mu_g", mu[3 * D + 128:])
        put("mu_vres", padded(w["vres_mu"][max(l - 1, 0)]))
        put("idx_w", np.concatenate([w["idx_k_norm_w"][l]] * 2))
        put("idx_b", np.concatenate([w["idx_k_norm_b"][l]] * 2))
        put("later", np.full(P, float(l > 0), np.float32))
        put("first", np.full(P, float(l == 0), np.float32))
        rt = np.concatenate([w["router_w_group"][l], w["router_w_expert"][l]], 1)
        o, n = PARAMS["router"]
        t[l, :, o:o + n] = rt.reshape(KD, P, 20).transpose(1, 0, 2).reshape(P, 160)
        o, n = PARAMS["router_b"]
        t[l, :, o:o + n] = np.concatenate([w["router_b_group"][l], w["router_b_expert"][l]])[None, :]
    return t


def weight_stream(w):
    out = np.zeros((DEPTH * LAYER_ROUNDS * RING, P, KD * P), np.float32)
    n = 0
    o_a = 3 * D
    o_s = o_a + D
    o_c = o_s + 3 * D + 256

    def columns(mat):
        nonlocal n
        v = out[n].reshape(P, KD, P)
        v[:, :, :mat.shape[1]] = mat.reshape(KD, P, -1).transpose(1, 0, 2)
        n += 1

    def blocks(*mats):
        nonlocal n
        for mat, row, col in mats:
            out[n, row:row + mat.shape[0], col:col + mat.shape[1]] = mat
        n += 1

    for l in range(DEPTH):
        wi, lv = w["w_in"][l], max(l - 1, 0)

        def start(phase):
            assert n == (l * LAYER_ROUNDS + FIRST[phase]) * RING, (phase, n)

        def merge(phase, proj, gate):
            start(phase)
            for j in range(8):
                columns(proj[:, j * P:(j + 1) * P])
                columns(wi[:, gate * D + j * P:gate * D + (j + 1) * P])

        start("lowrank")
        columns(wi[:, o_s + 3 * D:o_s + 3 * D + 128])
        columns(wi[:, o_s + 3 * D + 128:o_s + 3 * D + 256])
        columns(w["vres_w_down"][lv])
        n += 1
        start("pairs")
        for q in range(NPAIR):
            cq = slice(q * P, (q + 1) * P)
            blocks((w["rwkv_w2"][l][:, cq], 0, 0), (w["rwkv_a2"][l][:, cq], 64, P),
                   (w["rwkv_g2"][l][:, cq], 0, 2 * P), (w["vres_v2"][lv][:, cq], 0, 3 * P))
            for k in (1, 0, 2):
                columns(wi[:, o_s + k * D + q * P:o_s + k * D + (q + 1) * P])
        merge("merge_b", w["w_proj_b"][l], 1)
        start("pool")
        for j in range(8):
            columns(wi[:, o_a + j * P:o_a + (j + 1) * P])
        for half in range(2):
            blocks(*((w["pool_w"][l, 2 * half + g, kb * P:(kb + 1) * P, nb * P:(nb + 1) * P], 0,
                      (g * 4 + nb * 2 + kb) * P) for g in range(2) for nb in range(2) for kb in range(2)))
        n += 2
        start("dsa_in")
        columns(wi[:, o_c:o_c + 128])
        columns(wi[:, o_c + 128:o_c + 256])
        columns(wi[:, o_c + 256:o_c + 384])
        kidx = wi[:, o_c + 416:o_c + 480]
        columns(np.concatenate([kidx, kidx], 1))
        columns(np.concatenate([np.zeros((D, 64), np.float32), wi[:, o_c + 384:o_c + 416],
                                wi[:, o_c + 480:o_c + 488]], 1))
        iq = w["idx_w_q"][l]
        blocks(*((iq[kb * P:(kb + 1) * P, j * P:(j + 1) * P], 0, (2 * j + kb) * P)
                 for j in range(4) for kb in range(2)))
        n += 2
        merge("merge_a", w["w_proj_a"][l], 0)
        start("heads")
        for b in range(4):
            uq = w["mla_w_uq"][l]
            blocks(*((uq[kb * P:(kb + 1) * P, (4 * b + k) * 96:(4 * b + k + 1) * 96], 0, (2 * k + kb) * P)
                     for k in range(4) for kb in range(2)))
            blocks(*((w["mla_w_uk"][l, 4 * b + k], 0, 64 * k) for k in range(4)),
                   *((w["mla_w_uv"][l, 4 * b + k], 0, 256 + 64 * k) for k in range(4)))
        merge("merge_c", w["w_proj_c"][l], 2)
        start("out")
        for j in range(8):
            columns(w["w_out"][l][:, j * P:(j + 1) * P])
        start("moe")
        for g in range(4):
            for e in range(4 * g, 4 * g + 4):
                for f in range(2):
                    columns(w["expert_w1"][l, e][:, f * P:(f + 1) * P])
                    columns(w["expert_w3"][l, e][:, f * P:(f + 1) * P])
            down = np.concatenate([w["expert_w2"][l, e] for e in range(4 * g, 4 * g + 4)], 0)
            for j in range(8):
                columns(down[:, j * P:(j + 1) * P])
    assert n == out.shape[0], (n, out.shape)
    return out


def kernel(**inputs):
    import concourse.bacc as bacc
    from concourse.bass_utils import run_bass_kernel_spmd

    w = {k: np.asarray(v) for k, v in inputs.items()}
    tokens = np.concatenate([w["meta_tokens"], w["x"][0]], 0)
    arrays = {
        "x_t": np.ascontiguousarray(tokens.T.reshape(KD, P, T)),
        "consts": constant_table(),
        "params": param_table(w),
        "stream": weight_stream(w),
    }
    nc = bacc.Bacc("TRN2", target_bir_lowering=False, num_devices=1)
    args = [nc.dram_tensor(k, a.shape, mybir.dt.from_np(a.dtype), kind="ExternalInput").ap()
            for k, a in arrays.items()]
    args.append(nc.dram_tensor("out_t", (KD, P, SEQ), mybir.dt.float32, kind="ExternalOutput").ap())
    trunk_program(nc, *args)
    r = run_bass_kernel_spmd(nc, [arrays], core_ids=[0])
    return r.results[0]["out_t"].reshape(D, SEQ).T.reshape(1, SEQ, D)
```
